# Optimizing a Trainium2 kernel written in Bass

```python
import math
import jax, jax.numpy as jnp
from jax import lax
import numpy as np

D_MODEL = 1024
BATCH = 1
SEQ = 512
DEPTH = 2
DEC_BATCH = 8
DEC_SEQ = 4
PAST_LEN = 2048
PAGE_SIZE = 128

N_MIXERS = 2
N_NSA = (DEPTH + 1) // 2
N_GDN = DEPTH // 2
MEM_LEN = 256
HEAD_DIM = 64
NSA_HEADS = 12
NSA_KV_HEADS = 2
NSA_GROUP = NSA_HEADS // NSA_KV_HEADS
NSA_WIDTH = NSA_HEADS * HEAD_DIM
NSA_KV_COLS = NSA_KV_HEADS * HEAD_DIM
CMP_STRIDE = 16
CMP_BLOCK = 2 * CMP_STRIDE
CMP_HIDDEN = 128
SLC_BLOCK = 64
SLC_TOPN = 16
WINDOW = 512
SLC_QBLOCK = 64
WIN_QBLOCK = 128
GDN_HEADS = 6
GDN_DK = 128
GDN_DV = 128
GDN_WIDTH = GDN_HEADS * GDN_DV
GDN_CONV = 4
GDN_CONV_CH = 2 * GDN_HEADS * GDN_DK + GDN_HEADS * GDN_DV
GDN_CHUNK = 64
XA_HEADS = 4
XA_DIM = 64
XA_WIDTH = XA_HEADS * XA_DIM
MIX_WIDTH = NSA_WIDTH + XA_WIDTH
NSA_MIX_IN = NSA_WIDTH + 6 * NSA_KV_COLS + 3 * NSA_HEADS
NSA_IN = NSA_MIX_IN + XA_WIDTH
GDN_MIX_IN = GDN_CONV_CH + GDN_WIDTH + 2 * GDN_HEADS
GDN_IN = GDN_MIX_IN + XA_WIDTH
D_FF = 4 * D_MODEL
NORM_EPS = 1e-6
L2_EPS = 1e-6
NEG_INF = -1e30
FORCED = 1e9

kernel_name = 'nsa_gdn_hybrid_decode_step'

def rms_norm(x, g):
    xf = x.astype(jnp.float32)
    y = xf * lax.rsqrt(jnp.mean(xf * xf, axis=-1, keepdims=True) + NORM_EPS)
    return (y * g.astype(jnp.float32)).astype(x.dtype)

def alibi_slopes():
    h = jnp.arange(1, NSA_HEADS + 1, dtype=jnp.float32)
    return jnp.exp2(-8.0 * h / NSA_HEADS).reshape(NSA_KV_HEADS, NSA_GROUP)

def masked_softmax(s, mask):
    return jax.nn.softmax(jnp.where(mask, s.astype(jnp.float32), NEG_INF), axis=-1)

def map_query_blocks(fn, T, qb, items):
    nb = -(-T // qb)
    pad = nb * qb - T
    split = []
    for a, ax in items:
        if pad:
            widths = [(0, 0)] * a.ndim
            widths[ax] = (0, pad)
            a = jnp.pad(a, widths, mode='edge')
        shp = a.shape
        a = a.reshape(shp[:ax] + (nb, qb) + shp[ax + 1:])
        split.append(jnp.moveaxis(a, ax, 0))
    out = jnp.moveaxis(lax.map(fn, tuple(split)), 0, 1)
    out = out.reshape((out.shape[0], nb * qb) + out.shape[3:])
    return out[:, :T]

def compress_blocks(kv, pe, w1, w2):
    B, L, KH, D = kv.shape
    c = kv.reshape(B, L // CMP_STRIDE, CMP_STRIDE, KH, D)
    blocks = jnp.concatenate([c[:, :-1], c[:, 1:]], axis=2) + pe[None, None, :, None, :]
    hid = jax.nn.silu(jnp.einsum('bnlkd,ldf->bnkf', blocks, w1))
    return jnp.einsum('bnkf,fd->bnkd', hid, w2)

def cmp_to_slc(nc, ns):
    start = jnp.arange(nc)[:, None] * CMP_STRIDE
    j = jnp.arange(ns)[None, :]
    return ((start < (j + 1) * SLC_BLOCK) & (start + CMP_BLOCK > j * SLC_BLOCK)).astype(jnp.float32)

def nsa_mix(q, pos, gates, kv_full, win_kv, win_pos0, pe_k, w1_k, w2_k, pe_v, w1_v, w2_v):
    B, T, H, D = q.shape
    L = kv_full.shape[1]
    dt = q.dtype
    f32 = jnp.float32
    slopes = alibi_slopes()
    qg = (q * D ** -0.5).reshape(B, T, NSA_KV_HEADS, NSA_GROUP, D)

    kc = compress_blocks(kv_full[:, :, 0], pe_k, w1_k, w2_k)
    vc = compress_blocks(kv_full[:, :, 1], pe_v, w1_v, w2_v)
    nc = kc.shape[1]
    cdist = pos[:, None] - (jnp.arange(nc) * CMP_STRIDE + CMP_BLOCK - 1)[None, :]
    cvis = cdist >= 0
    s = jnp.einsum('btkgd,bnkd->bkgtn', qg, kc).astype(f32) - slopes[:, :, None, None] * cdist.astype(f32)
    p_cmp = masked_softmax(s, cvis) * jnp.any(cvis, axis=-1, keepdims=True)
    o_cmp = jnp.einsum('bkgtn,bnkd->btkgd', p_cmp.astype(dt), vc)

    ns = L // SLC_BLOCK
    imp = jnp.einsum('bkgtn,nj->bktj', p_cmp, cmp_to_slc(nc, ns))
    blk = jnp.arange(ns)[None, :]
    cur = (pos // SLC_BLOCK)[:, None]
    forced = (blk == 0) | (blk == cur) | (blk == cur - 1)
    imp = jnp.where(forced, FORCED, jnp.where(blk <= cur, imp, NEG_INF))
    top_s, top_i = lax.top_k(imp, min(SLC_TOPN, ns))
    top_ok = top_s > 0.5 * NEG_INF

    kb = kv_full[:, :, 2].reshape(B, ns, SLC_BLOCK, NSA_KV_HEADS, D).transpose(0, 3, 1, 2, 4)
    vb = kv_full[:, :, 3].reshape(B, ns, SLC_BLOCK, NSA_KV_HEADS, D).transpose(0, 3, 1, 2, 4)
    gather = jax.vmap(jax.vmap(lambda blocks, idx: blocks[idx]))

    def slc_block(args):
        qb, pb, ib, okb = args
        ks = gather(kb, ib)
        vs = gather(vb, ib)
        kpos = ib[..., None] * SLC_BLOCK + jnp.arange(SLC_BLOCK)
        dist = pb[:, None, None] - kpos
        mask = ((dist >= 0) & okb[..., None])[:, :, None]
        sc = jnp.einsum('btkgd,bktnsd->bkgtns', qb, ks).astype(f32) - slopes[:, :, None, None, None] * dist[:, :, None].astype(f32)
        sh = sc.shape
        pr = masked_softmax(sc.reshape(sh[:4] + (-1,)), mask.reshape(mask.shape[:4] + (-1,)))
        return jnp.einsum('bkgtns,bktnsd->btkgd', pr.reshape(sh).astype(dt), vs)

    o_slc = map_query_blocks(slc_block, T, min(SLC_QBLOCK, T), [(qg, 1), (pos, 0), (top_i, 2), (top_ok, 2)])

    qw = min(WIN_QBLOCK, T)
    kvw = jnp.pad(win_kv, ((0, 0), (WINDOW, qw), (0, 0), (0, 0), (0, 0)))

    def win_block(args):
        qb, pb = args
        kv = lax.dynamic_slice_in_dim(kvw, pb[0] - win_pos0, WINDOW + qw, axis=1)
        kpos = pb[0] - WINDOW + jnp.arange(WINDOW + qw)
        dist = pb[:, None] - kpos[None, :]
        mask = (dist >= 0) & (dist < WINDOW) & (kpos >= win_pos0)[None, :]
        sc = jnp.einsum('btkgd,bskd->bkgts', qb, kv[:, :, 0]).astype(f32) - slopes[:, :, None, None] * dist.astype(f32)
        pr = masked_softmax(sc, mask)
        return jnp.einsum('bkgts,bskd->btkgd', pr.astype(dt), kv[:, :, 1])

    o_win = map_query_blocks(win_block, T, qw, [(qg, 1), (pos, 0)])

    g = gates.reshape(B, T, NSA_KV_HEADS, NSA_GROUP, 3)
    o = g[..., 0:1] * o_cmp + g[..., 1:2] * o_slc + g[..., 2:3] * o_win
    return o.reshape(B, T, H * D)

def nsa_layer_mix(proj, pos0, past, pe_k, w1_k, w2_k, pe_v, w1_v, w2_v):
    B, T, _ = proj.shape
    q = proj[..., :NSA_WIDTH].reshape(B, T, NSA_HEADS, HEAD_DIM)
    kv = proj[..., NSA_WIDTH:NSA_WIDTH + 6 * NSA_KV_COLS].reshape(B, T, 6, NSA_KV_HEADS, HEAD_DIM)
    gates = jax.nn.sigmoid(proj[..., NSA_WIDTH + 6 * NSA_KV_COLS:NSA_MIX_IN]).reshape(B, T, NSA_HEADS, 3)
    rows, win_new = kv[:, :, :4], kv[:, :, 4:]
    if past is None:
        full, win, win_pos0 = rows, win_new, pos0
    else:
        full = jnp.concatenate([past[0], rows], axis=1)
        win = jnp.concatenate([past[1], win_new], axis=1)
        win_pos0 = pos0 - past[1].shape[1]
    L = full.shape[1]
    Lp = -(-L // SLC_BLOCK) * SLC_BLOCK
    full = jnp.pad(full, ((0, 0), (0, Lp - L), (0, 0), (0, 0), (0, 0)))
    pos = pos0 + jnp.arange(T, dtype=jnp.int32)
    o = nsa_mix(q, pos, gates, full, win, win_pos0, pe_k, w1_k, w2_k, pe_v, w1_v, w2_v)
    return o, rows, win[:, -min(WINDOW, win.shape[1]):]

def chunked_gated_delta(q, k, v, g, beta, S0):
    B, T, H, DK = q.shape
    DV = v.shape[-1]
    f32 = jnp.float32
    C = min(GDN_CHUNK, T)
    nc = -(-T // C)
    pad = nc * C - T
    q = q.astype(f32)
    k = k.astype(f32)
    q = q * lax.rsqrt(jnp.sum(q * q, -1, keepdims=True) + L2_EPS) * DK ** -0.5
    k = k * lax.rsqrt(jnp.sum(k * k, -1, keepdims=True) + L2_EPS)

    def prep(a):
        a = a.astype(f32)
        a = jnp.pad(a, [(0, 0), (0, pad)] + [(0, 0)] * (a.ndim - 2))
        a = a.reshape((B, nc, C) + a.shape[2:])
        return jnp.moveaxis(jnp.moveaxis(a, 3, 2), 1, 0)

    q, k, v, g, beta = prep(q), prep(k), prep(v), prep(g), prep(beta)
    gc = jnp.cumsum(g, axis=-1)
    incl = jnp.tril(jnp.ones((C, C), bool))
    strict = jnp.tril(jnp.ones((C, C), bool), -1)
    decay = jnp.exp(jnp.where(incl, gc[..., :, None] - gc[..., None, :], NEG_INF))
    kb = k * beta[..., None]
    A = jnp.where(strict, jnp.einsum('nbhid,nbhjd->nbhij', kb, k) * decay, 0.0)
    rhs = jnp.concatenate([v * beta[..., None], kb * jnp.exp(gc)[..., None]], axis=-1)
    sol = lax.linalg.triangular_solve(A, rhs, left_side=True, lower=True, unit_diagonal=True)
    u, w = sol[..., :DV], sol[..., DV:]
    qk = jnp.where(incl, jnp.einsum('nbhid,nbhjd->nbhij', q, k) * decay, 0.0)

    def step(S, xs):
        qc, kc, uc, wc, gcc, qkc = xs
        v_new = uc - jnp.einsum('bhck,bhkv->bhcv', wc, S)
        o = jnp.einsum('bhck,bhkv->bhcv', qc * jnp.exp(gcc)[..., None], S) + jnp.einsum('bhij,bhjv->bhiv', qkc, v_new)
        gl = gcc[..., -1:]
        S = S * jnp.exp(gl)[..., None] + jnp.einsum('bhck,bhcv->bhkv', kc * jnp.exp(gl - gcc)[..., None], v_new)
        return S, o

    S, o = lax.scan(step, S0.astype(f32), (q, k, u, w, gc, qk))
    o = jnp.swapaxes(jnp.moveaxis(o, 0, 1), 2, 3).reshape(B, nc * C, H, DV)[:, :T]
    return o, S

def gdn_mix(proj, conv_buf, S0, conv_w, a_log, dt_bias, norm_g):
    B, T, _ = proj.shape
    f32 = jnp.float32
    qkv = proj[..., :GDN_CONV_CH]
    z = proj[..., GDN_CONV_CH:GDN_CONV_CH + GDN_WIDTH].reshape(B, T, GDN_HEADS, GDN_DV)
    b_raw = proj[..., GDN_CONV_CH + GDN_WIDTH:GDN_CONV_CH + GDN_WIDTH + GDN_HEADS]
    a_raw = proj[..., GDN_CONV_CH + GDN_WIDTH + GDN_HEADS:GDN_MIX_IN]
    xc = jnp.concatenate([conv_buf.astype(qkv.dtype), qkv], axis=1)
    conv = xc[:, 0:T] * conv_w[0]
    for i in range(1, GDN_CONV):
        conv = conv + xc[:, i:i + T] * conv_w[i]
    act = jax.nn.silu(conv)
    new_buf = xc[:, -(GDN_CONV - 1):]
    hk = GDN_HEADS * GDN_DK
    q = act[..., :hk].reshape(B, T, GDN_HEADS, GDN_DK)
    k = act[..., hk:2 * hk].reshape(B, T, GDN_HEADS, GDN_DK)
    v = act[..., 2 * hk:].reshape(B, T, GDN_HEADS, GDN_DV)
    beta = jax.nn.sigmoid(b_raw.astype(f32))
    g = -jnp.exp(a_log.astype(f32)) * jax.nn.softplus(a_raw.astype(f32) + dt_bias.astype(f32))
    o, S = chunked_gated_delta(q, k, v, g, beta, S0)
    o = rms_norm(o.astype(proj.dtype), norm_g) * jax.nn.silu(z)
    return o.reshape(B, T, GDN_WIDTH), S.astype(S0.dtype), new_buf

def cross_attend(xq, mkv):
    B, T, _ = xq.shape
    q = xq.reshape(B, T, XA_HEADS, XA_DIM) * XA_DIM ** -0.5
    s = jnp.einsum('bthd,bmhd->bhtm', q, mkv[:, :, 0]).astype(jnp.float32)
    p = jax.nn.softmax(s, axis=-1).astype(xq.dtype)
    return jnp.einsum('bhtm,bmhd->bthd', p, mkv[:, :, 1]).reshape(B, T, XA_WIDTH)

def run_trunk(x, pos0, mem_kv, nsa_past, gdn_state, p):
    nsa_rows, nsa_win, gdn_s, gdn_conv = [], [], [], []
    for i in range(DEPTH):
        li = i // N_MIXERS
        h = rms_norm(x, p['norm_mix_g'][i])
        if i % N_MIXERS == 0:
            proj = h @ p['nsa_w_in'][li]
            o_mix, rows, win = nsa_layer_mix(proj[..., :NSA_MIX_IN], pos0, nsa_past[li],
                                             p['cmp_pe_k'][li], p['cmp_w1_k'][li], p['cmp_w2_k'][li],
                                             p['cmp_pe_v'][li], p['cmp_w1_v'][li], p['cmp_w2_v'][li])
            nsa_rows.append(rows)
            nsa_win.append(win)
        else:
            proj = h @ p['gdn_w_in'][li]
            S0, buf0 = gdn_state[li]
            o_mix, S, buf = gdn_mix(proj[..., :GDN_MIX_IN], buf0, S0, p['gdn_conv_w'][li], p['gdn_a_log'][li],
                                    p['gdn_dt_bias'][li], p['gdn_norm_g'][li])
            gdn_s.append(S)
            gdn_conv.append(buf)
        o_mem = cross_attend(proj[..., -XA_WIDTH:], mem_kv[i])
        x = x + jnp.concatenate([o_mix, o_mem], axis=-1) @ p['w_out'][i]
        h = rms_norm(x, p['norm_ffn_g'][i])
        x = x + jnp.square(jax.nn.relu(h @ p['w_up'][i])) @ p['w_down'][i]
    y = rms_norm(x, p['final_norm_g'])
    return y, jnp.stack(nsa_rows, 2), jnp.stack(nsa_win, 1), jnp.stack(gdn_s, 1), jnp.stack(gdn_conv, 1)

def setup_inputs(seed: int = 0) -> dict:
    key = jax.random.key(seed)
    ks = iter(jax.random.split(key, 40))
    nrm = lambda shape, scale=1.0: jax.random.normal(next(ks), shape, jnp.float32) * scale
    gain = lambda shape: 1.0 + nrm(shape, 0.05)
    n_pages = PAST_LEN // PAGE_SIZE
    n_phys = (DEC_BATCH * n_pages * 5 + 3) // 4
    win_buf = min(WINDOW, PAST_LEN)
    page_table = jax.random.permutation(next(ks), n_phys)[:DEC_BATCH * n_pages].reshape(DEC_BATCH, n_pages).astype(jnp.int32)
    dt = jnp.exp(jax.random.uniform(next(ks), (N_GDN, GDN_HEADS), jnp.float32, math.log(1e-3), math.log(1e-1)))
    dt_bias = dt + jnp.log(-jnp.expm1(-dt))
    a_log = jnp.log(jax.random.uniform(next(ks), (N_GDN, GDN_HEADS), jnp.float32, 1.0, 16.0))
    return {
        'x_prompt': nrm((BATCH, SEQ, D_MODEL)),
        'x_sample': nrm((DEC_BATCH, DEC_SEQ, D_MODEL)),
        'mem_prompt': nrm((BATCH, MEM_LEN, D_MODEL)),
        'cache_nsa_kv': nrm((n_phys, PAGE_SIZE, N_NSA, 4, NSA_KV_HEADS, HEAD_DIM)),
        'cache_nsa_win': nrm((DEC_BATCH, N_NSA, win_buf, 2, NSA_KV_HEADS, HEAD_DIM)),
        'state_gdn_s': nrm((DEC_BATCH, N_GDN, GDN_HEADS, GDN_DK, GDN_DV), 0.1),
        'state_gdn_conv': nrm((DEC_BATCH, N_GDN, GDN_CONV - 1, GDN_CONV_CH)),
        'cache_mem_kv': nrm((DEC_BATCH, DEPTH, MEM_LEN, 2, XA_HEADS, XA_DIM)),
        'page_table': page_table,
        'norm_mix_g': gain((DEPTH, D_MODEL)),
        'norm_mem_g': gain((DEPTH, D_MODEL)),
        'w_mem_kv': nrm((DEPTH, D_MODEL, 2 * XA_WIDTH), D_MODEL ** -0.5),
        'nsa_w_in': nrm((N_NSA, D_MODEL, NSA_IN), D_MODEL ** -0.5),
        'cmp_pe_k': nrm((N_NSA, CMP_BLOCK, HEAD_DIM), 0.5),
        'cmp_w1_k': nrm((N_NSA, CMP_BLOCK, HEAD_DIM, CMP_HIDDEN), (CMP_BLOCK * HEAD_DIM) ** -0.5),
        'cmp_w2_k': nrm((N_NSA, CMP_HIDDEN, HEAD_DIM), CMP_HIDDEN ** -0.5),
        'cmp_pe_v': nrm((N_NSA, CMP_BLOCK, HEAD_DIM), 0.5),
        'cmp_w1_v': nrm((N_NSA, CMP_BLOCK, HEAD_DIM, CMP_HIDDEN), (CMP_BLOCK * HEAD_DIM) ** -0.5),
        'cmp_w2_v': nrm((N_NSA, CMP_HIDDEN, HEAD_DIM), CMP_HIDDEN ** -0.5),
        'gdn_w_in': nrm((N_GDN, D_MODEL, GDN_IN), D_MODEL ** -0.5),
        'gdn_conv_w': nrm((N_GDN, GDN_CONV, GDN_CONV_CH), GDN_CONV ** -0.5),
        'gdn_a_log': a_log,
        'gdn_dt_bias': dt_bias,
        'gdn_norm_g': gain((N_GDN, GDN_DV)),
        'w_out': nrm((DEPTH, MIX_WIDTH, D_MODEL), MIX_WIDTH ** -0.5),
        'norm_ffn_g': gain((DEPTH, D_MODEL)),
        'w_up': nrm((DEPTH, D_MODEL, D_FF), D_MODEL ** -0.5),
        'w_down': nrm((DEPTH, D_FF, D_MODEL), D_FF ** -0.5),
        'final_norm_g': gain((D_MODEL,)),
    }

def reference(x_prompt, x_sample, mem_prompt, cache_nsa_kv, cache_nsa_win, state_gdn_s, state_gdn_conv,
              cache_mem_kv, page_table, norm_mix_g, norm_mem_g, w_mem_kv, nsa_w_in, cmp_pe_k, cmp_w1_k,
              cmp_w2_k, cmp_pe_v, cmp_w1_v, cmp_w2_v, gdn_w_in, gdn_conv_w, gdn_a_log, gdn_dt_bias,
              gdn_norm_g, w_out, norm_ffn_g, w_up, w_down, final_norm_g):
    p = dict(norm_mix_g=norm_mix_g, nsa_w_in=nsa_w_in, cmp_pe_k=cmp_pe_k, cmp_w1_k=cmp_w1_k,
             cmp_w2_k=cmp_w2_k, cmp_pe_v=cmp_pe_v, cmp_w1_v=cmp_w1_v, cmp_w2_v=cmp_w2_v,
             gdn_w_in=gdn_w_in, gdn_conv_w=gdn_conv_w, gdn_a_log=gdn_a_log, gdn_dt_bias=gdn_dt_bias,
             gdn_norm_g=gdn_norm_g, w_out=w_out, norm_ffn_g=norm_ffn_g, w_up=w_up, w_down=w_down,
             final_norm_g=final_norm_g)

    B, M = mem_prompt.shape[0], mem_prompt.shape[1]
    mem_kv_p = [(rms_norm(mem_prompt, norm_mem_g[i]) @ w_mem_kv[i]).reshape(B, M, 2, XA_HEADS, XA_DIM)
                for i in range(DEPTH)]
    gdn0 = [(jnp.zeros((B, GDN_HEADS, GDN_DK, GDN_DV), x_prompt.dtype),
             jnp.zeros((B, GDN_CONV - 1, GDN_CONV_CH), x_prompt.dtype))] * N_GDN
    y_prompt, nsa_kv_prompt, nsa_win_prompt, gdn_s_prompt, gdn_conv_prompt = run_trunk(
        x_prompt, 0, mem_kv_p, [None] * N_NSA, gdn0, p)
    mem_kv_prompt = jnp.stack(mem_kv_p, axis=1)

    DB = x_sample.shape[0]
    past_len = page_table.shape[1] * PAGE_SIZE
    past = cache_nsa_kv[page_table].reshape((DB, past_len) + cache_nsa_kv.shape[2:])
    nsa_past = [(past[:, :, li], cache_nsa_win[:, li]) for li in range(N_NSA)]
    gdn_past = [(state_gdn_s[:, li], state_gdn_conv[:, li]) for li in range(N_GDN)]
    mem_kv_s = [cache_mem_kv[:, i] for i in range(DEPTH)]
    y_sample, nsa_kv_sample, nsa_win_sample, gdn_s_sample, gdn_conv_sample = run_trunk(
        x_sample, past_len, mem_kv_s, nsa_past, gdn_past, p)

    return (y_prompt, y_sample, nsa_kv_prompt, nsa_kv_sample, nsa_win_prompt, nsa_win_sample,
            gdn_s_prompt, gdn_s_sample, gdn_conv_prompt, gdn_conv_sample, mem_kv_prompt)


_drawn_inputs = setup_inputs


def setup_inputs(seed=0):
    import zlib

    import numpy as np

    out = dict(_drawn_inputs(seed))
    spreads = {}
    factors = {'cmp_pe_k': 3.056, 'gdn_norm_g': 3.391}
    for name, (base, spread) in spreads.items():
        noise = np.random.default_rng([zlib.crc32(name.encode()), seed]).standard_normal(out[name].shape)
        drawn = base * np.exp(spread * noise) if base else spread * noise
        out[name] = __import__('jax').numpy.asarray(drawn.astype(out[name].dtype))
    for name, factor in factors.items():
        out[name] = (out[name] * factor).astype(out[name].dtype)
    return out
```

```python
from contextlib import ExitStack

import numpy as np

import concourse.bass as bass
from concourse import mybir

F32 = mybir.dt.float32
I32 = mybir.dt.int32
ALU = mybir.AluOpType
ACT = mybir.ActivationFunctionType
AX = mybir.AxisListType

P = 128
D = 1024
KT = D // P
TP, NS, DT = 512, 8, 4
TS = NS * DT
TT_ = TP + TS
MEM = 256
NKV, NG, HD = 2, 6, 64
NPAGE, PAGE = 16, 128
PAST = NPAGE * PAGE
NPHYS = (NS * NPAGE * 5 + 3) // 4
NCB = PAST // 16 - 1
NCP = TP // 16 - 1
NSLC = PAST // 64
TOPN = 16
WIN = 512
XH = 4
GH = 6
EPS = 1e-6
NEG = -1e30
FFT = 4 * D // P
NSA_T, GDN_T = 15, 27
ROWS = 64

Q0, CK, CV, SK, SV, WK, WV, XQ0, GT = 0, 6, 7, 8, 9, 10, 11, 12, 14
GQ, GK, GV, GZ, XQ1, BA = 0, 6, 12, 18, 24, 26


class Table:

    def __init__(self, *parts):
        self.at, self.size = {}, 0
        for name, *shape in parts:
            n = int(np.prod(shape))
            self.at[name] = (self.size, tuple(shape))
            self.size += n


COMMON = Table(("ident", P), ("ones", P), ("g_mix", 2, KT), ("g_mem", 2, KT), ("g_ffn", 2, KT), ("g_fin", KT),
               ("pe", 2, 16), ("w2", 2, HD), ("conv_w", 18, 4), ("g_o", 1), ("a_log", GH), ("dt_bias", GH),
               ("eps", 1), ("one", 1))
PROMPT_T = Table(("dist", TP), ("cdist", 4, NCP), ("cvis", 4), ("nslope", 12))
SAMPLE_T = Table(("b_slc", PAST), ("b_win", WIN), ("b_cmp", NCB), ("b_new", DT), ("same", ROWS), ("pick", NS, ROWS),
                 ("head", 36), ("lower", 30, 30))
GDN_TB = Table(("cum", P), ("cum_s", TS), ("all_s", TS), ("mask", P), ("mask_s", TS), ("strict", P), ("strict_s", TS),
               ("diag", P), ("off", 3, P), ("seq", NS))


def view(ap, *shape):
    if len(shape) < 2:
        return ap
    names = "abcd"[:len(shape)]
    return ap.rearrange(f"p ({' '.join(names)}) -> p {' '.join(names)}", **dict(zip(names[1:], shape[1:])))


class Arena:

    def __init__(self, t, lo, hi):
        self.t, self.lo, self.hi = t, lo, hi

    def take(self, *shape, rows=P):
        n = int(np.prod(shape))
        assert self.lo + n <= self.hi, (self.lo, n, self.hi)
        ap = self.t[0:rows, self.lo:self.lo + n]
        self.lo += n
        return view(ap, *shape)

    def table(self, tb):
        ap = self.take(tb.size)
        return ap, {k: view(ap[:, o:o + int(np.prod(s))], *s) for k, (o, s) in tb.at.items()}


class Chain:

    def __init__(self, eng, sem):
        self.eng, self.sem, self.n = eng, sem, 0

    def __call__(self, ins):
        ins.then_inc(self.sem, 1)
        self.n += 1
        self.eng.wait_ge(self.sem, self.n)


def bcast(ap, *shape):
    while len(ap.shape) < len(shape):
        ap = ap.unsqueeze(len(ap.shape))
    return ap.to_broadcast(list(shape))


def build(nc, x_in, mem_in, w_in, common_in, prompt_in, sample_in, gdn_in, pages_in, win_in, mcache_in, conv_in,
          state_in, table_in, y_out, kv_out, win_out, conv_out_p, conv_out_s, state_out_p, state_out_s, mem_out):
    with ExitStack() as ctx:
        sem = lambda name: ctx.enter_context(nc.semaphore(name))
        TOTAL = 53060
        sbuf = ctx.enter_context(nc.sbuf_tensor("sbuf", [P, TOTAL], F32))
        pages_sb = ctx.enter_context(nc.sbuf_tensor("page_table", [1, NS * NPAGE], I32))
        psum = ctx.enter_context(nc.psum_tensor("psum", [P, 8, 512], F32))
        bank = lambda b: psum[:, b, :]
        banks = lambda b, n: psum[:, b:b + n, :].rearrange("p a n -> p (a n)")

        top = Arena(sbuf, 0, TOTAL)
        _, C = top.table(COMMON)
        common_ap = sbuf[:, 0:COMMON.size]
        xT = top.take(KT, TT_)
        hT = top.take(KT, TT_)
        ring = [top.take(2048) for _ in range(4)]
        big0 = top.lo
        top.lo += 16384
        pj0 = top.lo
        top.lo += 8192
        work0 = top.lo
        big = lambda: Arena(sbuf, big0, big0 + 16384)
        pj = lambda: Arena(sbuf, pj0, pj0 + NSA_T * TT_)
        rest = lambda: Arena(sbuf, work0, TOTAL)
        mixT = hT

        a = rest()
        sq = a.take(2, TT_)
        rstd = a.take(TT_)
        norm_end = a.lo
        after_norm = lambda: Arena(sbuf, norm_end, TOTAL)

        persist = after_norm()
        gsamp = persist.take(36, rows=TS)
        pebias = persist.take(2)
        free0 = persist.lo
        free = lambda: Arena(sbuf, free0, TOTAL)

        a = free()
        mkv0 = a.take(1024)
        mkv0_end = a.lo
        memT = a.take(KT, MEM)
        a = big()
        sqm = a.take(KT, MEM)
        memn = a.take(2, KT, MEM)
        rstdm = a.take(MEM)
        mkv1_tmp = a.take(1024)

        proj = pj().take(NSA_T, TT_)
        page = [view(sbuf[:, big0 + 8192 * s:big0 + 8192 * (s + 1)], NPAGE, 512) for s in range(2)]
        mcache = [view(sbuf[:, big0 + 8192:big0 + 16384], NS, 1024), None]

        def memory_buffers(a):
            return dict(sm=[a.take(4, MEM) for _ in range(2)], pt=[a.take(2, 4, P) for _ in range(2)],
                        stat=a.take(2, 16), qm=a.take(NS * (2 * P + 16)))

        mb = [memory_buffers(Arena(sbuf, mkv0_end, TOTAL)), None]
        mkv = [mkv0, None]

        a = Arena(sbuf, big0 + 8192, big0 + 16384)
        prompt_ap, PT = a.table(PROMPT_T)
        s_sb = [a.take(4, TP) for _ in range(2)]
        qs = a.take(2, TP)
        vn = a.take(2, 4, P)
        a = free()
        scp = [a.take(2, 32) for _ in range(2)]
        ptp = [a.take(4, P) for _ in range(2)]
        ptc = a.take(2, P, rows=NCP)
        stp = a.take(2, 24)
        gnat = a.take(4, 36)
        xtp = a.take(2, 8, 2, 32)
        pab = a.take(2, 2, 64)
        phid = a.take(2, 2, 32)
        kcp = a.take(NCP)
        vcp = a.take(P, rows=NCP)

        a = free()
        sample_ap, ST = a.table(SAMPLE_T)
        S_NEW, S_WIN, S_WNEW, S_CMP = PAST, PAST + DT, PAST + DT + WIN, PAST + 2 * DT + WIN
        ssc = a.take(S_CMP + NCB + 1, rows=ROWS)
        pts = a.take(20, ROWS)
        ptcs = a.take(ROWS, rows=NCB)
        cab = a.take(2, 2, 2 * P)
        a.lo = work0
        chid = a.take(2, 2, P)
        kc = a.take(2, P)
        vc = a.take(2, P, rows=NCB)
        vnew = a.take(2, P, rows=DT)
        ptn = a.take(2, ROWS, rows=DT)
        imp = a.take(NSLC, rows=ROWS)
        sel = a.take(NSLC, rows=ROWS)
        impc = ssc[:, 1800:1800 + P]
        qb = a.take(ROWS)
        vst = a.take(2, DT)
        gr = a.take(3, rows=ROWS)
        grt = a.take(36, rows=ROWS)
        sst = a.take(16, rows=ROWS)
        assert a.lo <= norm_end
        wcache = [ring[2][:, 1024 * s:1024 * (s + 1)] for s in range(2)]
        u = view(sbuf[:, pj0 + 8192 - FFT * TT_:pj0 + 8192], FFT, TT_)

        a = big()
        gproj = a.take(GDN_T, TT_)
        gdn_b = a
        mcache[1] = view(sbuf[:, pj0:pj0 + 8192], NS, 1024)
        a = free()
        gdn_ap, GC = a.table(GDN_TB)
        sst1 = a.take(1)
        ban = a.take(5, 12)
        beta = a.take(5, GH)
        gat = a.take(5, GH)
        spl = a.take(5, GH)
        nea = a.take(GH)
        small_end = a.lo
        mkv[1] = a.take(1024)
        mb[1] = memory_buffers(a)
        a = Arena(sbuf, small_end + 1024, TOTAL)
        cacc = a.take(2, TP)
        cbuf = a.take(18, NS, 3)
        xs = a.take(18, NS, 7)
        sacc = a.take(18, NS, DT)
        stmp = a.take(18, NS, DT)
        cout_p = a.take(18, 3)
        cout_s = a.take(18, NS, 3)
        a = Arena(sbuf, small_end, TOTAL)
        cw = lambda a: a.take(GH, P)
        grs, dec, egr, bm, bmt, qt_, kbg, kdec, vb, pw = [cw(a) for _ in range(10)]
        gcn = a.take(2, 8)
        egc, bex, kde = a.take(GH), a.take(GH), a.take(GH)
        a = pj()
        a.hi = pj0 + 8192
        pwt, tt_, nwt, qg, st_p = [cw(a) for _ in range(5)]
        wm = a.take(GH, NS * (TS + DT))
        vx = a.take(NS, P, rows=TS)
        sg = [gdn_b.take(NS, P), a.take(NS, P)]
        qd, ug, tn, vnw, zz = pw, nwt, nwt, dec, pwt

        in_common, in_x, in_mem, in_table = sem("in_common"), sem("in_x"), sem("in_mem"), sem("in_table")
        in_prompt_t, in_sample_t, in_gdn_t = sem("in_prompt_t"), sem("in_sample_t"), sem("in_gdn_t")
        in_panel = [sem(f"in_panel{s}") for s in range(4)]
        in_pages = [sem(f"in_pages{s}") for s in range(2)]
        in_mcache, in_mkv1, in_conv = sem("in_mcache"), sem("in_mkv1"), sem("in_conv")
        in_state = [sem("in_state0"), sem("in_state1")]
        stored, mem_stored = sem("stored"), sem("mem_stored")
        state_stored = [sem("state_stored0"), sem("state_stored1")]
        chain_act, chain_dve = sem("chain_act"), sem("chain_dve")
        mem_sq, mem_ss, mem_std, memn_ready, memkv_ready = map(sem, ("mem_sq", "mem_ss", "mem_std", "memn_ready",
                                                                     "memkv_ready"))
        pe_out = sem("pe_out")
        act_out = sem("act_out")
        dve_out = sem("dve_out")
        u_ready = sem("u_ready")
        sq_ready, sq_used, ss_done, std_ready, h_ready = map(sem, ("sq_ready", "sq_used", "ss_done", "std_ready",
                                                                   "h_ready"))
        xs_ready, xm_ready, xp_ready, xt_done, xpt_ready, xo_done, mix_mem = map(
            sem, ("xs_ready", "xm_ready", "xp_ready", "xt_done", "xpt_ready", "xo_done", "mix_mem"))
        qm_ready, xmax_ready = sem("qm_ready"), sem("xmax_ready")
        vg_done, vg_ready, w1_used, pab_ready, phid_ready, pkv_done, pkv_ready = map(
            sem, ("vg_done", "vg_ready", "w1_used", "pab_ready", "phid_ready", "pkv_done", "pkv_ready"))
        xtp_ready, psum_ready = sem("xtp_ready"), sem("psum_ready")
        qs_ready, ps_done, ps_read, pmax_ready, pexp_ready, pp_ready = map(
            sem, ("qs_ready", "ps_done", "ps_read", "pmax_ready", "pexp_ready", "pp_ready"))
        pt_done, pt_ready, po_done, prompt_done = map(sem, ("pt_done", "pt_ready", "po_done", "prompt_done"))
        cab_ready, hsum_ready, hid_ready, kvc_done, kvc_ready = map(
            sem, ("cab_ready", "hsum_ready", "hid_ready", "kvc_done", "kvc_ready"))
        qb_ready, vnew_done, vnew_ready, sc_done, cmax_ready, cexp_ready, cp_ready, imp_done = map(
            sem, ("qb_ready", "vnew_done", "vnew_ready", "sc_done", "cmax_ready", "cexp_ready", "cp_ready",
                  "imp_done"))
        smax_ready, sexp_ready, sp_ready, spt_done, spt_ready, so_done, seq_done = map(
            sem, ("smax_ready", "sexp_ready", "sp_ready", "spt_done", "spt_ready", "so_done", "seq_done"))
        win_stored = [sem("win_stored0"), sem("win_stored1")]
        conv_acc, conv_done, couts_ready, conv_stored = map(sem, ("conv_acc", "conv_done", "couts_ready", "conv_stored"))
        ba_done, ban_ready, gate_pre, gat_ready = map(sem, ("ba_done", "ban_ready", "gate_pre", "gat_ready"))
        cn_sq, cn_ss, cn_std, cn_ready = map(sem, ("cn_sq", "cn_ss", "cn_std", "cn_ready"))
        ug_ready, gc_done, gc_ready, dexp_pre, dexp_ready, kq_done, bm_ready, tr_done, tr_ready, trd_ready = map(
            sem, ("ug_ready", "gc_done", "gc_ready", "dexp_pre", "dexp_ready", "kq_done", "bm_ready", "tr_done",
                  "tr_ready", "trd_ready"))
        inv_pe, inv_act, inv_dve = sem("inv_pe"), sem("inv_act"), sem("inv_dve")
        wt_done, nwt_ready, vn_done, vn_ready, oc_done, oc_ready, sup_mm, sup_done = map(
            sem, ("wt_done", "nwt_ready", "vn_done", "vn_ready", "oc_done", "oc_ready", "sup_mm", "sup_done"))
        wm_ready, vx_ready, snew_mm, snew_ready, vns_done, vns_ready = map(
            sem, ("wm_ready", "vx_ready", "snew_mm", "snew_ready", "vns_done", "vns_ready"))

        GEMMS = [("mem", 4), ("nsa_in", 8), ("w1", 2), ("window", 1), ("out0", 4), ("up0", 16), ("down0", 16),
                 ("gdn_in", 14), ("out1", 4), ("up1", 16), ("down1", 16)]
        TILES = dict(mem=4, nsa_in=NSA_T, out0=8, up0=32, down0=8, gdn_in=GDN_T, out1=8, up1=32, down1=8)
        wbase, obase, src, free_at = {}, {}, [], []
        w = o = n_src = 0
        for name, n in GEMMS:
            wbase[name], obase[name] = w, o
            for j in range(n):
                src.append(None if name == "window" else n_src)
                n_src += name != "window"
                if name in ("w1", "window"):
                    free_at.append(name)
                elif name == "mem":
                    free_at.append(o + j + 1)
                elif name.startswith("down"):
                    free_at.append(o + j // 2 + 1)
                else:
                    free_at.append(o + min(2 * j + 2, TILES[name]))
            w += n
            o += TILES.get(name, 0)
        n_panels = w
        evac_base = dict(nsa_in=0, up0=NSA_T, gdn_in=NSA_T + 32, up1=NSA_T + 32 + GDN_T,
                         out0=0, down0=8, out1=16, down1=24)

        def panel_uses(slot, i):
            return i // 4 + 1 - (1 if slot == 2 and i > wbase["window"] else 0)

        ident, ones = C["ident"], C["ones"]
        block = ctx.enter_context(nc.Block())

        @block.sync
        def _(sp):
            sp.dma_start(common_ap, common_in).then_inc(in_common, 16)
            sp.dma_start(memT, mem_in).then_inc(in_mem, 16)

            def panel(i):
                slot = i % 4
                if i >= 4:
                    f = free_at[i - 4]
                    if f == "w1":
                        sp.wait_ge(w1_used, NS + 1)
                    elif f == "window":
                        sp.wait_ge(seq_done, NS)
                        for b in range(2):
                            sp.wait_ge(win_stored[b], 16 * (NS // 2))
                    else:
                        sp.wait_ge(pe_out, f)
                sp.dma_start(ring[slot], w_in[src[i]]).then_inc(in_panel[slot], 16)

            for i in range(4):
                panel(i)
            sp.dma_start(xT, x_in).then_inc(in_x, 16)
            sp.dma_start(pages_sb[:, :], table_in).then_inc(in_table, 16)
            sp.wait_ge(memn_ready, 2 * KT)
            sp.wait_ge(pe_out, 4)
            sp.wait_ge(mem_stored, 32)
            sp.dma_start(mcache[0], mcache_in[0].rearrange("s p n -> p s n")).then_inc(in_mcache, 16)
            for i in range(4, 14):
                panel(i)
            sp.wait_ge(in_table, 16)

            def sequence(s):
                if s >= 2:
                    sp.wait_ge(seq_done, s - 1)
                for p in range(NPAGE):
                    v = sp.value_load(pages_sb[0:1, s * NPAGE + p:s * NPAGE + p + 1], min_val=0, max_val=NPHYS - 1)
                    sp.dma_start(page[s % 2][:, p, :], pages_in[bass.ds(v, 1), :, :].rearrange("a p n -> (a p) n"))\
                        .then_inc(in_pages[s % 2], 16)
                if s == 0:
                    sp.wait_ge(pe_out, 4 + NSA_T)
                if s >= 2:
                    sp.wait_ge(win_stored[s % 2], 16 * (s // 2))
                sp.dma_start(wcache[s % 2], win_in[s]).then_inc(in_pages[s % 2], 16)

            sp.wait_ge(mix_mem, 5)
            sp.dma_start(prompt_ap, prompt_in).then_inc(in_prompt_t, 16)
            sequence(0)
            sp.wait_ge(prompt_done, 24)
            sp.dma_start(sample_ap, sample_in).then_inc(in_sample_t, 16)
            for s in range(1, NS):
                sequence(s)
            for i in range(15, wbase["gdn_in"] + 14):
                panel(i)
                if i == wbase["gdn_in"] + 3:
                    sp.wait_ge(pe_out, obase["gdn_in"])
                    sp.wait_ge(dve_out, 16)
                    sp.dma_start(mcache[1], mcache_in[1].rearrange("s p n -> p s n")).then_inc(in_mcache, 16)
                    sp.dma_start(gdn_ap, gdn_in).then_inc(in_gdn_t, 16)
                    sp.dma_start(mkv[1], mem_out[1]).then_inc(in_mkv1, 16)
            sp.wait_ge(mix_mem, 10)
            sp.dma_start(cbuf, conv_in).then_inc(in_conv, 16)
            for i in range(wbase["out1"], wbase["out1"] + 4):
                panel(i)
            for h in range(GH):
                if h == 0:
                    sp.wait_ge(conv_done, 19)
                if h >= 2:
                    sp.wait_ge(state_stored[h % 2], 16 * (h // 2))
                sp.dma_start(sg[h % 2], state_in[h]).then_inc(in_state[h % 2], 16)
            for i in range(wbase["up1"], n_panels):
                panel(i)

        @block.gpsimd
        def _(pool):
            for l in range(2):
                pool.wait_ge(memkv_ready, 2 * l + 2)
                pool.dma_start(mem_out[l], (mkv0, mkv1_tmp)[l]).then_inc(mem_stored, 16)
            pool.wait_ge(act_out, 12)
            pool.dma_start(kv_out, proj[:, CK:WV + 1, :]).then_inc(stored, 16)
            for s in range(NS):
                pool.wait_ge(in_pages[s % 2], 16 * (NPAGE + 1) * (s // 2 + 1))
                pool.dma_start(win_out[s], wcache[s % 2]).then_inc(win_stored[s % 2], 16)
            pool.wait_ge(conv_done, 19)
            pool.wait_ge(couts_ready, 2)
            pool.dma_start(conv_out_p, cout_p).then_inc(conv_stored, 16)
            pool.dma_start(conv_out_s, cout_s).then_inc(conv_stored, 16)
            pool.wait_ge(sup_done, 4)
            pool.dma_start(state_out_p, st_p).then_inc(stored, 16)
            for h in range(GH):
                pool.wait_ge(snew_ready, h + 1)
                pool.dma_start(state_out_s[h], sg[h % 2]).then_inc(state_stored[h % 2], 16)
            for k in range(KT):
                pool.wait_ge(h_ready, 4 * KT + k + 1)
                pool.dma_start(y_out[:, k, :], hT[:, k, :]).then_inc(stored, 16)
            pool.wait_ge(stored, 16 * (2 + KT))
            pool.wait_ge(mem_stored, 32)
            pool.wait_ge(conv_stored, 32)
            for b in range(2):
                pool.wait_ge(win_stored[b], 16 * (NS // 2))
                pool.wait_ge(state_stored[b], 16 * (GH // 2))

        ident, ones = C["ident"], C["ones"]


        groups = lambda n: sum(m % 4 + 2 for m in range(n))

        def pe_nsa_prompt(pe):
            mm = pe.matmul
            w1 = [view(ring[kind], 16, P) for kind in range(2)]
            pe.wait_ge(mix_mem, 5)
            for j in range(4):
                pe.transpose(bank(0)[:, 48 * j:48 * j + 36], proj[0:36, GT, P * j:P * (j + 1)], ident[0:36, 0:36])
            pe.transpose(bank(0)[0:TS, 192:228], proj[0:36, GT, TP:TT_], ident[0:36, 0:36])
            for br, tile in enumerate((SV, WV)):
                for j in range(4):
                    last = pe.transpose(bank(1 + br)[:, P * j:P * (j + 1)], proj[:, tile, P * j:P * (j + 1)], ident)
            last.then_inc(vg_done, 1)
            pe.wait_ge(in_panel[0], 16 * panel_uses(0, wbase["w1"]))
            pe.wait_ge(in_panel[1], 16 * panel_uses(1, wbase["w1"] + 1))
            for kind in range(2):
                for lp in range(16):
                    mm(bank(3)[:, kind:kind + 1], w1[kind][:, lp, :], C["pe"][:, kind, lp:lp + 1],
                       start=lp == 0, stop=lp == 15)
            pe.wait_ge(xtp_ready, 1)
            for kind in range(2):
                for half in range(2):
                    for lp in range(8):
                        last = mm(bank(4 + kind)[:, 64 * half:64 * half + 64], w1[kind][:, 8 * half + lp, :],
                                  xtp[:, kind, lp, :, :].rearrange("p k c -> p (k c)"), start=lp == 0, stop=lp == 7)
            last.then_inc(w1_used, 1)
            pe.wait_ge(phid_ready, 2)
            for kv in range(NKV):
                mm(bank(6)[64 * kv:64 * kv + 64, 0:NCP], C["w2"][:, 0, :], phid[:, 0, kv, 0:NCP], start=True, stop=True)
            for kv in range(NKV):
                last = mm(bank(7)[0:NCP, 64 * kv:64 * kv + 64], phid[:, 1, kv, 0:NCP], C["w2"][:, 1, :],
                          start=True, stop=True)
            last.then_inc(pkv_done, 1)
            pe.wait_ge(pkv_ready, 1)
            pe.wait_ge(vg_ready, 1)

            def scores(n):
                g, qt = n // 4, n % 4
                pe.wait_ge(qs_ready, g + 1)
                if n:
                    pe.wait_ge(ps_read, n)
                nk = P * (qt + 1)
                for kv in range(NKV):
                    r = slice(64 * kv, 64 * kv + 64)
                    q = qs[r, g % 2, P * qt:P * (qt + 1)]
                    mm(bank(kv)[:, 0:nk], q, proj[r, SK, 0:nk], start=True, stop=True)
                    mm(bank(2 + kv)[:, 0:nk], q, proj[r, WK, 0:nk], start=True, stop=True)
                    last = mm(bank(4 + kv)[:, 0:NCP], q, kcp[r, :], start=True, stop=True)
                last.then_inc(ps_done, 1)

            def values(n):
                g, qt = n // 4, n % 4
                pe.wait_ge(pp_ready, n + 1)

                def turn(q):
                    if groups(n) + q:
                        pe.wait_ge(pt_ready, groups(n) + q)
                    if q <= qt:
                        for r in range(4):
                            last = pe.transpose(bank(6)[:, P * r:P * (r + 1)], s_sb[n % 2][:, r, P * q:P * (q + 1)],
                                                ident)
                    else:
                        for kv in range(NKV):
                            last = pe.transpose(bank(6)[0:NCP, P * kv:P * (kv + 1)], scp[n % 2][:, kv, 0:NCP], ident)
                    last.then_inc(pt_done, 1)

                turn(0)
                if n:
                    pe.wait_ge(prompt_done, n)
                for q in range(qt + 2):
                    if q <= qt:
                        turn(q + 1)
                    else:
                        pe.wait_ge(pt_ready, groups(n) + q + 1)
                    for kv in range(NKV):
                        o = bank(7)[64 * kv:64 * kv + 64, 0:P]
                        if q <= qt:
                            for br in range(2):
                                mm(o, vn[:, br, q, 64 * kv:64 * kv + 64], ptp[q % 2][:, 2 * br + kv, :],
                                   start=q == br == 0, stop=False)
                        else:
                            last = mm(o, vcp[:, 64 * kv:64 * kv + 64], ptc[:, kv, :], start=False, stop=True)
                last.then_inc(po_done, 1)

            scores(0)
            for n in range(24):
                if n < 23:
                    scores(n + 1)
                values(n)

        def act_nsa_prompt(act, own):
            f = act.activation
            act.wait_ge(vg_done, 1)
            f(gnat, view(bank(0)[:, 0:192], 4, 48)[:, :, 0:36], ACT.Sigmoid)
            f(gsamp, bank(0)[0:TS, 192:228], ACT.Sigmoid)
            for br in range(2):
                last = f(vn[:, br, :, :].rearrange("p j c -> p (j c)"), bank(1 + br), ACT.Copy)
            last.then_inc(vg_ready, 1)
            act.wait_ge(w1_used, 1)
            own(f(pebias, bank(3)[:, 0:2], ACT.Copy))
            for kind in range(2):
                last = f(pab[:, kind, :, :].rearrange("p h c -> p (h c)"), bank(4 + kind)[:, 0:P], ACT.Copy)
            last.then_inc(pab_ready, 1)
            for kind in range(2):
                act.wait_ge(psum_ready, kind + 1)
                f(phid[:, kind, :, 0:NCP], phid[:, kind, :, 0:NCP], ACT.Silu, bias=pebias[:, kind:kind + 1])\
                    .then_inc(phid_ready, 1)
            act.wait_ge(pkv_done, 1)
            f(kcp, bank(6)[:, 0:NCP], ACT.Copy)
            f(vcp, bank(7)[0:NCP, 0:P], ACT.Copy).then_inc(pkv_ready, 1)

            def queries(g):
                if g >= 2:
                    act.wait_ge(ps_done, 4 * (g - 1))
                f(qs[:, g % 2, :], proj[:, Q0 + g, 0:TP], ACT.Copy, scale=HD ** -0.5).then_inc(qs_ready, 1)

            def exps(n):
                nk, st = P * (n % 4 + 1), stp[:, n % 2, :]
                act.wait_ge(pmax_ready, n + 1)
                for r in range(4):
                    f(s_sb[n % 2][:, r, 0:nk], s_sb[n % 2][:, r, 0:nk], ACT.Exp, bias=st[:, r:r + 1],
                      accum_out=st[:, 8 + r:9 + r])
                for kv in range(NKV):
                    last = f(scp[n % 2][:, kv, 0:NCP], scp[n % 2][:, kv, 0:NCP], ACT.Exp, bias=st[:, 4 + kv:5 + kv],
                             accum_out=st[:, 12 + kv:13 + kv])
                last.then_inc(pexp_ready, 1)

            def turned(n):
                for q in range(n % 4 + 2):
                    act.wait_ge(pt_done, groups(n) + q + 1)
                    if q <= n % 4:
                        f(ptp[q % 2].rearrange("p r q -> p (r q)"), bank(6), ACT.Copy).then_inc(pt_ready, 1)
                    else:
                        f(ptc.rearrange("p r q -> p (r q)"), bank(6)[0:NCP, 0:2 * P], ACT.Copy).then_inc(pt_ready, 1)

            queries(0)
            queries(1)
            exps(0)
            for n in range(24):
                if n < 23:
                    exps(n + 1)
                if n % 4 == 3 and n // 4 + 2 < NG:
                    queries(n // 4 + 2)
                turned(n)

        def dve_nsa_prompt(dve, own):
            tt, ts, stt = dve.tensor_tensor, dve.tensor_scalar, dve.scalar_tensor_tensor
            for kind in range(2):
                for kv in range(NKV):
                    src_ = proj[64 * kv:64 * kv + 64, CK + kind, 0:TP].rearrange("p (c l two) -> p two l c", two=2, l=8)
                    for two in range(2):
                        last = dve.tensor_copy(xtp[64 * two:64 * two + 64, kind, :, kv, :], src_[:, two, :, :])
            last.then_inc(xtp_ready, 1)
            dve.wait_ge(pab_ready, 1)
            for kind in range(2):
                part = pab[:, kind, :, :].rearrange("p h (k c) -> p h k c", k=2)
                tt(phid[:, kind, :, 0:NCP], part[:, 0, :, 0:NCP], part[:, 1, :, 1:NCP + 1], ALU.add)\
                    .then_inc(psum_ready, 1)
            dve.wait_ge(in_prompt_t, 16)
            dve.wait_ge(vg_ready, 1)

            def biased(n):
                g, qt = n // 4, n % 4
                nk, st, s = P * (qt + 1), stp[:, n % 2, :], s_sb[n % 2]
                dve.wait_ge(ps_done, n + 1)
                if n >= 2:
                    dve.wait_ge(pt_done, groups(n - 1))
                slope = lambda kv: PT["nslope"][:, 6 * kv + g:6 * kv + g + 1]
                for r in range(4):
                    stt(out=s[:, r, 0:nk], in0=PT["dist"][:, TP - nk:TP], scalar=slope(r % 2), in1=bank(r)[:, 0:nk],
                        op0=ALU.mult, op1=ALU.add)
                for kv in range(NKV):
                    last = stt(out=scp[n % 2][:, kv, 0:NCP], in0=PT["cdist"][:, qt, :], scalar=slope(kv),
                               in1=bank(4 + kv)[:, 0:NCP], op0=ALU.mult, op1=ALU.add)
                last.then_inc(ps_read, 1)
                dve.wait_ge(ps_read, n + 1)
                dve.tensor_reduce(st[:, 0:4], s[:, :, 0:nk], AX.X, ALU.max, negate=True)
                dve.tensor_reduce(st[:, 4:6], scp[n % 2][:, :, 0:NCP], AX.X, ALU.max, negate=True)\
                    .then_inc(pmax_ready, 1)

            def scaled(n):
                g, qt = n // 4, n % 4
                nk, st, s = P * (qt + 1), stp[:, n % 2, :], s_sb[n % 2]
                dve.wait_ge(pexp_ready, n + 1)
                own(dve.reciprocal(st[:, 16:22], st[:, 8:14]))
                own(tt(st[:, 16:22], st[:, 16:22], gnat[:, qt, 6 * g:6 * g + 6], ALU.mult))
                own(ts(st[:, 20:22], st[:, 20:22], PT["cvis"][:, qt:qt + 1], None, ALU.mult))
                tt(s[:, :, 0:nk], s[:, :, 0:nk], bcast(st[:, 16:20], P, 4, nk), ALU.mult)
                tt(scp[n % 2][:, :, 0:NCP], scp[n % 2][:, :, 0:NCP], bcast(st[:, 20:22], P, 2, NCP), ALU.mult)\
                    .then_inc(pp_ready, 1)

            def output(n):
                dve.wait_ge(po_done, n + 1)
                dve.tensor_copy(mixT[:, n // 4, P * (n % 4):P * (n % 4 + 1)], bank(7)[:, 0:P]).then_inc(prompt_done, 1)

            biased(0)
            for n in range(24):
                if n < 23:
                    biased(n + 1)
                scaled(n)
                if n:
                    output(n - 1)
            output(23)

        def pe_nsa_sample(pe):
            mm = pe.matmul
            w1 = [view(ring[kind], 16, P) for kind in range(2)]

            def compress(s):
                pe.wait_ge(in_pages[s % 2], 16 * (NPAGE + 1) * (s // 2 + 1))
                if s:
                    pe.wait_ge(vnew_ready, s)
                    pe.wait_ge(kvc_ready, s)
                else:
                    pe.wait_ge(prompt_done, 24)
                for kind in range(2):
                    for half in range(2):
                        for lp in range(8):
                            last = mm(bank(6 + kind)[:, 2 * P * half:2 * P * (half + 1)], w1[kind][:, 8 * half + lp, :],
                                      page[s % 2][:, :, P * kind + 16 * lp:P * kind + 16 * lp + 16],
                                      start=lp == 0, stop=lp == 7)
                last.then_inc(w1_used, 1)

            def compressed(s):
                pe.wait_ge(hid_ready, s + 1)
                for kv in range(NKV):
                    mm(bank(6)[64 * kv:64 * kv + 64, 0:NCB], C["w2"][:, 0, :], chid[:, 0, kv, 0:NCB],
                       start=True, stop=True)
                for kv in range(NKV):
                    last = mm(bank(6)[0:NCB, P + 64 * kv:P + 64 * kv + 64], chid[:, 1, kv, 0:NCB], C["w2"][:, 1, :],
                              start=True, stop=True)
                last.then_inc(kvc_done, 1)

            def new_rows(s):
                pe.wait_ge(qb_ready, s + 1)
                pe.wait_ge(cab_ready, s + 1)
                for br in range(2):
                    pe.transpose(bank(7)[0:DT, P * br:P * (br + 1)], vst[:, br, :], ident)
                mm(bank(7)[0:ROWS, 256:292], ST["pick"][0:TS, s, :], gsamp, start=True, stop=True)\
                    .then_inc(vnew_done, 1)

            def scores(s):
                pe.wait_ge(kvc_ready, s + 1)
                if s:
                    pe.wait_ge(seq_done, s)
                pg, kn = page[s % 2], slice(TP + DT * s, TP + DT * (s + 1))
                for j in range(4):
                    mm(bank(j)[0:ROWS, :], qb, pg[:, 4 * j:4 * j + 4, 256:384], start=True, stop=True)
                mm(bank(4)[0:ROWS, :], qb, wcache[s % 2][:, 0:WIN], start=True, stop=True)
                mm(bank(5)[0:ROWS, 0:DT], qb, proj[:, SK, kn], start=True, stop=True)
                mm(bank(5)[0:ROWS, DT:2 * DT], qb, proj[:, WK, kn], start=True, stop=True)
                mm(bank(5)[0:ROWS, 16:16 + NCB], qb, kc[:, s % 2, 0:NCB], start=True, stop=True).then_inc(sc_done, 1)

            def importance(s):
                pe.wait_ge(cp_ready, s + 1)
                mm(bank(5)[0:ROWS, 0:NCB], ST["same"][0:ROWS, :], ssc[:, S_CMP:S_CMP + NCB], start=True, stop=True)\
                    .then_inc(imp_done, 1)

            def values(s):
                pe.wait_ge(sp_ready, s + 1)
                for b in range(3):
                    for j in range(8 if b < 2 else 4):
                        at = P * (8 * b + j) if b < 2 else S_WIN + P * j
                        last = pe.transpose(bank(1 + b)[:, ROWS * j:ROWS * (j + 1)], ssc[:, at:at + P],
                                            ident[0:ROWS, 0:ROWS])
                    last.then_inc(spt_done, 1)
                pe.transpose(bank(4)[0:NCB, 0:ROWS], ssc[:, S_CMP:S_CMP + NCB], ident[0:ROWS, 0:ROWS])
                pe.transpose(bank(4)[0:DT, 64:128], ssc[:, S_NEW:S_NEW + DT], ident[0:ROWS, 0:ROWS])
                pe.transpose(bank(4)[0:DT, 128:192], ssc[:, S_WNEW:S_WNEW + DT], ident[0:ROWS, 0:ROWS])\
                    .then_inc(spt_done, 1)
                o = bank(0)[:, 0:ROWS]
                for j in range(20):
                    if j in (0, 8, 16):
                        pe.wait_ge(spt_ready, 4 * s + j // 8 + 1)
                    lhs = page[s % 2][:, j, 384:512] if j < 16 else wcache[s % 2][:, WIN + P * (j - 16):WIN + P * (j - 15)]
                    mm(o, lhs, pts[:, j, :], start=j == 0, stop=False)
                pe.wait_ge(spt_ready, 4 * s + 4)
                mm(o, vc[:, s % 2, :], ptcs, start=False, stop=False)
                for br in range(2):
                    last = mm(o, vnew[:, br, :], ptn[:, br, :], start=False, stop=br == 1)
                last.then_inc(so_done, 1)

            pe.wait_ge(in_sample_t, 16)
            compress(0)
            compressed(0)
            for s in range(NS):
                new_rows(s)
                scores(s)
                if s < NS - 1:
                    compress(s + 1)
                importance(s)
                if s < NS - 1:
                    compressed(s + 1)
                values(s)

        def act_nsa_sample(act, own):
            f = act.activation

            def halves(s):
                act.wait_ge(w1_used, s + 2)
                for kind in range(2):
                    if s:
                        act.wait_ge(hsum_ready, 2 * s)
                    for half in range(2):
                        last = f(cab[:, kind, half, :].rearrange("p (k g c) -> p k g c", k=2, g=NPAGE),
                                 bank(6 + kind)[:, 2 * P * half:2 * P * (half + 1)]
                                 .rearrange("p (g k c) -> p k g c", k=2, g=NPAGE), ACT.Copy)
                last.then_inc(cab_ready, 1)

            def hidden(s):
                if s:
                    act.wait_ge(kvc_done, s)
                for kind in range(2):
                    act.wait_ge(hsum_ready, 2 * s + kind + 1)
                    last = f(chid[:, kind, :, 0:NCB],
                             cab[:, kind, 0, :].rearrange("p (k c) -> p k c", k=2)[:, :, 0:NCB], ACT.Silu,
                             bias=pebias[:, kind:kind + 1])
                last.then_inc(hid_ready, 1)
                act.wait_ge(kvc_done, s + 1)
                f(kc[:, s % 2, 0:NCB], bank(6)[:, 0:NCB], ACT.Copy)
                f(vc[:, s % 2, :], bank(6)[0:NCB, P:2 * P], ACT.Copy).then_inc(kvc_ready, 1)

            halves(0)
            hidden(0)
            for s in range(NS):
                act.wait_ge(vnew_done, s + 1)
                if s:
                    act.wait_ge(seq_done, s)
                f(vnew.rearrange("p b c -> p (b c)"), bank(7)[0:DT, 0:2 * P], ACT.Copy)
                f(grt, bank(7)[0:ROWS, 256:292], ACT.Copy).then_inc(vnew_ready, 1)
                act.wait_ge(cmax_ready, s + 1)
                cmp_ = ssc[:, S_CMP:S_CMP + NCB]
                f(cmp_, cmp_, ACT.Exp, bias=sst[:, 0:1], accum_out=sst[:, 1:2]).then_inc(cexp_ready, 1)
                if s < NS - 1:
                    halves(s + 1)
                    hidden(s + 1)
                act.wait_ge(smax_ready, s + 1)
                f(ssc[:, 0:PAST + DT], ssc[:, 0:PAST + DT], ACT.Exp, bias=sst[:, 3:4], accum_out=sst[:, 5:6])
                w = ssc[:, S_WIN:S_WIN + WIN + DT]
                f(w, w, ACT.Exp, bias=sst[:, 4:5], accum_out=sst[:, 6:7]).then_inc(sexp_ready, 1)
                for b in range(3):
                    n = 8 if b < 2 else 4
                    act.wait_ge(spt_done, 4 * s + b + 1)
                    f(pts[:, 8 * b:8 * b + n, :].rearrange("p j r -> p (j r)"), bank(1 + b)[:, 0:ROWS * n], ACT.Copy)\
                        .then_inc(spt_ready, 1)
                act.wait_ge(spt_done, 4 * s + 4)
                f(ptcs, bank(4)[0:NCB, 0:ROWS], ACT.Copy)
                f(ptn.rearrange("p b r -> p (b r)"), bank(4)[0:DT, 64:192], ACT.Copy).then_inc(spt_ready, 1)

        def dve_nsa_sample(dve, own):
            tt, ts = dve.tensor_tensor, dve.tensor_scalar
            dve.wait_ge(in_sample_t, 16)
            own(dve.memset(qb, 0.0))
            own(dve.memset(sel, 0.0))

            def queries(s):
                if s:
                    dve.wait_ge(sc_done, s)
                kn = slice(TP + DT * s, TP + DT * (s + 1))
                for kv in range(NKV):
                    r = slice(64 * kv, 64 * kv + 64)
                    ts(qb[r, 32 * kv:32 * kv + 24].rearrange("p (g t) -> p g t", g=NG), proj[r, Q0:Q0 + NG, kn],
                       HD ** -0.5, None, ALU.mult)
                dve.tensor_copy(vst[:, 0, :], proj[:, SV, kn])
                dve.tensor_copy(vst[:, 1, :], proj[:, WV, kn]).then_inc(qb_ready, 1)

            def half_sum(s):
                dve.wait_ge(cab_ready, s + 1)
                for kind in range(2):
                    h = [cab[:, kind, i, :].rearrange("p (k c) -> p k c", k=2) for i in range(2)]
                    tt(h[0][:, :, 0:NCB], h[0][:, :, 0:NCB], h[1][:, :, 1:NCB + 1], ALU.add).then_inc(hsum_ready, 1)

            queries(0)
            half_sum(0)
            for s in range(NS):
                cmp_ = ssc[:, S_CMP:S_CMP + NCB]
                dve.wait_ge(sc_done, s + 1)
                tt(ssc[:, S_NEW:S_NEW + DT], bank(5)[0:ROWS, 0:DT], ST["b_new"][0:ROWS, :], ALU.add)
                tt(ssc[:, S_WNEW:S_WNEW + DT], bank(5)[0:ROWS, DT:2 * DT], ST["b_new"][0:ROWS, :], ALU.add)
                own(tt(cmp_, bank(5)[0:ROWS, 16:16 + NCB], ST["b_cmp"][0:ROWS, :], ALU.add))
                dve.tensor_reduce(sst[:, 0:1], cmp_, AX.X, ALU.max, negate=True).then_inc(cmax_ready, 1)
                if s < NS - 1:
                    queries(s + 1)
                dve.wait_ge(vnew_ready, s + 1)
                own(tt(grt, grt, ST["head"][0:ROWS, :], ALU.mult))
                own(dve.tensor_reduce(gr, grt.rearrange("p (g b k) -> p b g k", g=NG, b=3), AX.XY, ALU.add))
                dve.wait_ge(cexp_ready, s + 1)
                own(dve.reciprocal(sst[:, 2:3], sst[:, 1:2]))
                ts(cmp_, cmp_, sst[:, 2:3], None, ALU.mult).then_inc(cp_ready, 1)
                dve.wait_ge(imp_done, s + 1)
                dve.memset(impc[:, NCB:P], 0.0)
                own(dve.tensor_copy(impc[:, 0:NCB], bank(5)[0:ROWS, 0:NCB]))
                own(dve.tensor_reduce(imp, view(impc, NSLC, 4), AX.X, ALU.add))
                own(tt(imp[:, 1:NSLC], imp[:, 1:NSLC], view(impc, NSLC, 4)[:, 0:NSLC - 1, 3], ALU.add))
                c = NSLC - 2
                gt, eq = view(ssc[:, 0:c * c], c, c), view(ssc[:, c * c:2 * c * c], c, c)
                each, other = bcast(imp[:, 1:1 + c], ROWS, c, c), imp[:, 1:1 + c].unsqueeze(1).to_broadcast([ROWS, c, c])
                tt(gt, other, each, ALU.is_gt)
                own(tt(eq, other, each, ALU.is_equal))
                own(tt(eq, eq, ST["lower"][0:ROWS, :, :], ALU.mult))
                own(tt(gt, gt, eq, ALU.add))
                own(dve.tensor_reduce(sel[:, 1:1 + c], gt, AX.X, ALU.add))
                own(ts(sel[:, 1:1 + c], sel[:, 1:1 + c], float(TOPN - 3), NEG, ALU.is_ge, ALU.mult))
                if s < NS - 1:
                    half_sum(s + 1)
                own(tt(ssc[:, 0:PAST], banks(0, 4)[0:ROWS, :], ST["b_slc"][0:ROWS, :], ALU.add))
                tt(ssc[:, S_WIN:S_WIN + WIN], bank(4)[0:ROWS, :], ST["b_win"][0:ROWS, :], ALU.add)
                past = view(ssc[:, 0:PAST], NSLC, 64)
                own(tt(past, past, bcast(sel, ROWS, NSLC, 64), ALU.add))
                dve.tensor_reduce(sst[:, 3:4], ssc[:, 0:PAST + DT], AX.X, ALU.max, negate=True)
                dve.tensor_reduce(sst[:, 4:5], ssc[:, S_WIN:S_WIN + WIN + DT], AX.X, ALU.max, negate=True)\
                    .then_inc(smax_ready, 1)
                dve.wait_ge(sexp_ready, s + 1)
                own(dve.reciprocal(sst[:, 8:10], sst[:, 5:7]))
                own(tt(sst[:, 8:10], sst[:, 8:10], gr[:, 0:2], ALU.mult))
                ts(ssc[:, 0:PAST + DT], ssc[:, 0:PAST + DT], sst[:, 8:9], None, ALU.mult)
                ts(ssc[:, S_WIN:S_WIN + WIN + DT], ssc[:, S_WIN:S_WIN + WIN + DT], sst[:, 9:10], None, ALU.mult)
                ts(cmp_, cmp_, gr[:, 2:3], None, ALU.mult).then_inc(sp_ready, 1)
                dve.wait_ge(so_done, s + 1)
                for kv in range(NKV):
                    r = slice(64 * kv, 64 * kv + 64)
                    last = dve.tensor_copy(mixT[r, 0:NG, TP + DT * s:TP + DT * (s + 1)],
                                           bank(0)[r, 32 * kv:32 * kv + 24].rearrange("p (g t) -> p g t", g=NG))
                last.then_inc(seq_done, 1)

        CHUNKS = [(P, slice(P * i, P * (i + 1)), 3, 3) for i in range(4)] + [(TS, slice(TP, TT_), 1, 0)]
        HB = ((0, 4), (4, 6))

        class Inverse:

            def __init__(self):
                self.pe = self.act = self.dve = 0

        def pe_gdn(pe):
            mm = pe.matmul
            n = Inverse()
            pe.wait_ge(mix_mem, 10)
            for j in range(4):
                pe.transpose(bank(0)[:, 16 * j:16 * j + 12], gproj[0:12, BA, P * j:P * (j + 1)], ident[0:12, 0:12])
            pe.transpose(bank(0)[0:TS, 64:76], gproj[0:12, BA, TP:TT_], ident[0:12, 0:12]).then_inc(ba_done, 1)
            pe.wait_ge(ban_ready, 1)

            def sums(c):
                pe.wait_ge(cn_sq, c + 1)
                if c >= 2:
                    pe.wait_ge(cn_std, c - 1)
                mm(bank(c % 2), ones, sq[:, c % 2, 0:TP], start=True, stop=True)
                mm(bank(2 + c % 2)[:, 0:TS], ones, sq[:, c % 2, TP:TT_], start=True, stop=True).then_inc(cn_ss, 1)

            for c in range(12):
                sums(c)
            pe.wait_ge(cn_ready, 12)
            for ci, (R, cols, squares, merges) in enumerate(CHUNKS):
                U, ALL = (GC["cum"], ones) if R == P else (GC["cum_s"], GC["all_s"])
                if ci:
                    pe.wait_ge(oc_ready, ci)
                    pe.wait_ge(sup_done, ci)
                pe.wait_ge(ug_ready, ci + 1)
                mm(bank(0)[0:R, 0:GH], U[0:R, 0:R], gat[0:R, ci, :], start=True, stop=True)
                mm(bank(0)[0:R, 8:8 + GH], ALL[0:R, 0:R], gat[0:R, ci, :], start=True, stop=True)
                for b, (h0, h1) in enumerate(HB):
                    last = mm(bank(1 + b)[:, 0:R * (h1 - h0)], ones[0:R, :], ug[0:R, h0:h1, 0:R], start=True, stop=True)
                last.then_inc(gc_done, 1)

                def pair(b0, lhs, rhs, width, rows=P):
                    for b, (h0, h1) in enumerate(HB):
                        for h in range(h0, h1):
                            o = bank(b0[b])[0:rows, width * (h - h0):width * (h - h0 + 1)]
                            last = mm(o, lhs(h), rhs(h), start=True, stop=True)
                    return last

                kT = lambda h: gproj[:, GK + h, cols]
                qT = lambda h: gproj[:, GQ + h, cols]
                pair((3, 4), kT, kT, R, R)
                pair((5, 6), qT, kT, R, R).then_inc(kq_done, 1)
                pe.wait_ge(bm_ready, ci + 1)
                for b, (h0, h1) in enumerate(HB):
                    for h in range(h0, h1):
                        x = slice(R * (h - h0), R * (h - h0 + 1))
                        y = slice(P * (h - h0), P * (h - h0 + 1))
                        pe.transpose(bank(3 + b)[0:R, x], bm[0:R, h, 0:R], ident[0:R, 0:R])
                        pe.transpose(bank(5 + b)[0:R, x], qd[0:R, h, 0:R], ident[0:R, 0:R])
                        pe.transpose(bank(b)[0:R, y], kT(h), ident)
                        last = pe.transpose(bank((2, 7)[b])[0:R, y], gproj[:, GV + h, cols], ident)
                last.then_inc(tr_done, 1)
                n.dve += 1
                sub = lambda t: (lambda h: t[0:R, h, 0:R])
                for k in range(squares):
                    pe.wait_ge(inv_dve, n.dve)
                    if not k:
                        pe.wait_ge(tr_ready, ci + 1)
                    pair((3, 4), sub(pwt), sub(pw), R, R).then_inc(inv_pe, 1)
                    if k < squares - 1:
                        pair((5, 6), sub(pw), sub(pwt), R, R).then_inc(inv_pe, 1)
                    n.act += 1
                    pe.wait_ge(inv_act, n.act)
                    pair((0, 1), sub(pw), sub(tt_), R, R).then_inc(inv_pe, 1)
                    n.dve += 1
                if merges:
                    pe.wait_ge(inv_dve, n.dve)
                    for b, (h0, h1) in enumerate(HB):
                        for h in range(h0, h1):
                            last = pe.transpose(bank(5 + b)[:, P * (h - h0):P * (h - h0 + 1)], tt_[:, h, :], ident)
                    last.then_inc(inv_pe, 1)
                    n.act += 1
                for k in range(merges):
                    pe.wait_ge(inv_dve, n.dve)
                    pair((3, 4), sub(pw), sub(tt_), R, R).then_inc(inv_pe, 1)
                    n.act += 1
                    pe.wait_ge(inv_act, n.act)
                    last = pair((0, 1), sub(tn), sub(zz), R, R)
                    if k < merges - 1:
                        last = pair((5, 6), sub(zz), sub(tn), R, R)
                    last.then_inc(inv_pe, 1)
                    n.dve += 1
                pe.wait_ge(inv_dve, n.dve)
                pair((2, 7), lambda h: kbg[0:R, h, :], sub(tt_), R).then_inc(wt_done, 1)
                pe.wait_ge(nwt_ready, ci + 1)
                if R == P:
                    for b, (h0, h1) in enumerate(HB):
                        for h in range(h0, h1):
                            o = bank(3 + b)[:, P * (h - h0):P * (h - h0 + 1)]
                            mm(o, tt_[:, h, :], vb[:, h, :], start=True, stop=False)
                            last = mm(o, nwt[:, h, :], st_p[:, h, :], start=False, stop=True)
                    last.then_inc(vn_done, 1)
                    pe.wait_ge(vn_ready, ci + 1)
                    for b, (h0, h1) in enumerate(HB):
                        for h in range(h0, h1):
                            o = bank(5 + b)[:, P * (h - h0):P * (h - h0 + 1)]
                            mm(o, st_p[:, h, :], qg[:, h, :], start=True, stop=False)
                            last = mm(o, vnw[:, h, :], qt_[:, h, :], start=False, stop=True)
                    last.then_inc(oc_done, 1)
                    pair((0, 1), lambda h: kdec[:, h, :], lambda h: vnw[:, h, :], P).then_inc(sup_mm, 1)
                    continue
                pe.wait_ge(wm_ready, 1)
                for h in range(GH):
                    s0 = sg[h % 2]
                    pe.wait_ge(in_state[h % 2], 16 * (h // 2 + 1))
                    v = bank(3 + h % 2)[0:R, 0:P]
                    mm(v, tt_[0:R, h, 0:R], vb[0:R, h, :], start=True, stop=False)
                    for s in range(NS):
                        last = mm(v, wm[:, h, TS * s:TS * (s + 1)], s0[:, s, :], start=False, stop=s == NS - 1)
                    last.then_inc(vns_done, 1)
                    o = bank(5)[:, TS * h:TS * (h + 1)]
                    for s in range(NS):
                        mm(o[:, DT * s:DT * (s + 1)], s0[:, s, :], qg[:, h, DT * s:DT * (s + 1)], start=s == 0,
                           stop=False, skip_group_check=True)
                    pe.wait_ge(vns_ready, h + 1)
                    last = mm(o, vnw[0:R, h, :], qt_[0:R, h, 0:R], start=False, stop=True, skip_group_check=True)
                    if h == GH - 1:
                        last.then_inc(oc_done, 1)
                    pe.wait_ge(vx_ready, h + 1)
                    if h:
                        pe.wait_ge(snew_ready, h)
                    for b in range(2):
                        last = mm(bank(6 + b), kdec[0:R, h, :], vx[:, 4 * b:4 * b + 4, :], start=True, stop=True)
                    last.then_inc(snew_mm, 1)
            pe.wait_ge(oc_ready, 5)
            for c in range(12, 18):
                sums(c)
            pe.wait_ge(cn_ready, 18)

        def act_gdn(act, own):
            f = act.activation
            n = Inverse()
            for c in range(18):
                act.wait_ge(conv_acc, c + 1)
                f(gproj[:, c, 0:TP], cacc[:, c % 2, :], ACT.Silu).then_inc(conv_done, 1)
            act.wait_ge(conv_acc, 19)
            f(gproj[:, 0:18, TP:TT_], sacc.rearrange("p c s t -> p c (s t)"), ACT.Silu).then_inc(conv_done, 1)
            act.wait_ge(mix_mem, 10)
            f(gproj[:, GZ:GZ + GH, :], gproj[:, GZ:GZ + GH, :], ACT.Silu).then_inc(conv_done, 1)
            act.wait_ge(gate_pre, 1)
            f(beta, ban[:, :, 0:GH], ACT.Sigmoid)
            own(f(nea, C["a_log"], ACT.Exp))
            own(f(spl, spl, ACT.Exp, scale=-1.0))
            f(spl, spl, ACT.Ln, bias=C["one"]).then_inc(gat_ready, 1)

            def column_norms(lo, hi, src_, scale):
                def square(c):
                    if c >= 2:
                        act.wait_ge(cn_ss, c - 1)
                    f(sq[:, c % 2, :], src_(c), ACT.Square).then_inc(cn_sq, 1)

                square(lo)
                for c in range(lo, hi):
                    if c + 1 < hi:
                        square(c + 1)
                    act.wait_ge(cn_ss, c + 1)
                    if c:
                        act.wait_ge(cn_ready, c)
                    f(rstd[:, 0:TP], bank(c % 2), ACT.Sqrt, bias=C["eps"], scale=scale)
                    f(rstd[:, TP:TT_], bank(2 + c % 2)[:, 0:TS], ACT.Sqrt, bias=C["eps"], scale=scale)\
                        .then_inc(cn_std, 1)

            act.wait_ge(conv_done, 19)
            column_norms(0, 12, lambda c: gproj[:, c, :], 1.0)
            for ci, (R, cols, squares, merges) in enumerate(CHUNKS):
                act.wait_ge(gc_ready, ci + 1)
                f(dec[0:R, :, 0:R], dec[0:R, :, 0:R], ACT.Exp, scale=-1.0)
                f(egr[:, :, 0:R], grs[:, :, 0:R], ACT.Exp)
                f(egc[0:R, :], gcn[0:R, 0, 0:GH], ACT.Exp)
                f(kde[0:R, :], kde[0:R, :], ACT.Exp).then_inc(dexp_ready, 1)
                act.wait_ge(tr_done, ci + 1)
                act.wait_ge(bm_ready, ci + 1)
                act.wait_ge(dexp_ready, ci + 1)
                for b, (h0, h1) in enumerate(HB):
                    for h in range(h0, h1):
                        x = bank(b)[0:R, P * (h - h0):P * (h - h0 + 1)]
                        f(kbg[0:R, h, :], x, ACT.Copy, scale=bex[0:R, h:h + 1])
                        last = f(kdec[0:R, h, :], x, ACT.Copy, scale=kde[0:R, h:h + 1])
                last.then_inc(tr_ready, 1)

                def out(dst, b0, width, rows=P, scale=1.0):
                    for b, (h0, h1) in enumerate(HB):
                        last = f(dst[0:rows, h0:h1, 0:width],
                                 view(bank(b0[b])[0:rows, 0:width * (h1 - h0)], h1 - h0, width), ACT.Copy, scale=scale)
                    return last

                for k in range(squares):
                    n.pe += 1 if k == squares - 1 else 2
                    act.wait_ge(inv_pe, n.pe)
                    out(pw, (3, 4), R, R).then_inc(inv_act, 1)
                    n.pe += 1
                if merges:
                    n.pe += 1
                    act.wait_ge(inv_pe, n.pe)
                    out(tn, (5, 6), R, R).then_inc(inv_act, 1)
                for k in range(merges):
                    n.pe += 1
                    act.wait_ge(inv_pe, n.pe)
                    out(zz, (3, 4), R, R).then_inc(inv_act, 1)
                    n.pe += 1
                act.wait_ge(wt_done, ci + 1)
                out(nwt, (2, 7), R, scale=-1.0).then_inc(nwt_ready, 1)
                if R == P:
                    act.wait_ge(vn_done, ci + 1)
                    out(vnw, (3, 4), P).then_inc(vn_ready, 1)
                    act.wait_ge(oc_done, ci + 1)
                    out(mixT[:, :, cols], (5, 6), P).then_inc(oc_ready, 1)
                    continue
                for h in range(GH):
                    act.wait_ge(vns_done, h + 1)
                    f(vnw[0:R, h, :], bank(3 + h % 2)[0:R, 0:P], ACT.Copy).then_inc(vns_ready, 1)
                act.wait_ge(oc_done, 5)
                f(mixT[:, 0:GH, cols], view(bank(5)[:, 0:GH * TS], GH, TS), ACT.Copy).then_inc(oc_ready, 1)
            act.wait_ge(oc_ready, 5)
            column_norms(12, 18, lambda c: mixT[:, c - 12, :], 1.0 / P)

        def dve_gdn(dve, own):
            tt, ts, stt = dve.tensor_tensor, dve.tensor_scalar, dve.scalar_tensor_tensor
            n = Inverse()
            w = C["conv_w"]
            dve.tensor_copy(cout_p, gproj[:, 0:18, TP - 3:TP]).then_inc(couts_ready, 1)
            for c in range(18):
                x, acc = gproj[:, c, 0:TP], cacc[:, c % 2, :]
                if c >= 2:
                    dve.wait_ge(conv_done, c - 1)
                own(ts(acc, x, w[:, c, 3:4], None, ALU.mult))
                for i in range(1, 4):
                    last = stt(out=acc[:, i:TP], in0=x[:, 0:TP - i], scalar=w[:, c, 3 - i:4 - i], in1=acc[:, i:TP],
                               op0=ALU.mult, op1=ALU.add)
                    if i < 3:
                        own(last)
                last.then_inc(conv_acc, 1)
            dve.wait_ge(in_conv, 16)
            dve.tensor_copy(xs[:, :, :, 0:3], cbuf)
            own(dve.tensor_copy(xs[:, :, :, 3:7], gproj[:, 0:18, TP:TT_].rearrange("p c (s t) -> p c s t", s=NS)))
            dve.tensor_copy(cout_s, xs[:, :, :, DT:DT + 3]).then_inc(couts_ready, 1)
            wi = lambda i: bcast(w[:, :, i], P, 18, NS, DT)
            own(tt(sacc, xs[:, :, :, 0:DT], wi(0), ALU.mult))
            for i in range(1, 4):
                own(tt(stmp, xs[:, :, :, i:i + DT], wi(i), ALU.mult))
                last = tt(sacc, sacc, stmp, ALU.add)
                if i < 3:
                    own(last)
            last.then_inc(conv_acc, 1)
            own(dve.memset(ban, 0.0))
            dve.wait_ge(ba_done, 1)
            dve.tensor_copy(ban[:, 0:4, :], view(bank(0)[:, 0:64], 4, 16)[:, :, 0:12])
            own(dve.tensor_copy(ban[0:TS, 4, :], bank(0)[0:TS, 64:76]))
            a_ = ban[:, :, GH:2 * GH]
            own(tt(a_, a_, C["dt_bias"].unsqueeze(1).to_broadcast([P, 5, GH]), ALU.add))
            own(ts(gat, a_, 0.0, None, ALU.max))
            stt(out=spl, in0=a_, scalar=-1.0, in1=a_, op0=ALU.mult, op1=ALU.max).then_inc(gate_pre, 1)
            dve.wait_ge(gate_pre, 1)
            dve.tensor_copy(sst1, C["one"]).then_inc(ban_ready, 1)
            dve.wait_ge(gat_ready, 1)
            own(tt(gat, gat, spl, ALU.add))
            own(stt(out=gat, in0=gat, scalar=-1.0, in1=nea.unsqueeze(1).to_broadcast([P, 5, GH]), op0=ALU.mult,
                    op1=ALU.mult))

            for c in range(12):
                dve.wait_ge(cn_std, c + 1)
                own(dve.reciprocal(rstd, rstd))
                stt(out=gproj[:, c, :], in0=gproj[:, c, :], scalar=P ** -0.5 if c < GK else 1.0, in1=rstd,
                    op0=ALU.mult, op1=ALU.mult).then_inc(cn_ready, 1)
            dve.wait_ge(cn_ready, 12)
            dve.wait_ge(in_gdn_t, 16)
            dve.wait_ge(conv_stored, 32)
            own(dve.memset(st_p, 0.0))
            own(dve.memset(wm, 0.0))
            for ci, (R, cols, squares, merges) in enumerate(CHUNKS):
                U, MASK, STRICT = (GC["cum"], GC["mask"], GC["strict"]) if R == P else \
                    (GC["cum_s"], GC["mask_s"], GC["strict_s"])
                heads = lambda t: t[0:R, 0:R].unsqueeze(1).to_broadcast([R, GH, R])
                bt, sub = beta[0:R, ci, :], (lambda t: t[0:R, :, 0:R])
                if ci:
                    dve.wait_ge(oc_ready, ci)
                tt(sub(ug), heads(U), bcast(gat[0:R, ci, :], R, GH, R), ALU.mult).then_inc(ug_ready, 1)
                dve.wait_ge(gc_done, ci + 1)
                dve.tensor_copy(gcn[0:R, :, 0:GH], view(bank(0)[0:R, 0:16], 2, 8)[:, :, 0:GH])
                for b, (h0, h1) in enumerate(HB):
                    last = dve.tensor_copy(grs[:, h0:h1, 0:R], view(bank(1 + b)[:, 0:R * (h1 - h0)], h1 - h0, R))
                own(last)
                tt(kde[0:R, :], gcn[0:R, 1, 0:GH], gcn[0:R, 0, 0:GH], ALU.subtract)
                for h in range(GH):
                    last = stt(out=dec[0:R, h, 0:R], in0=grs[0:R, h, 0:R], scalar=gcn[0:R, 0, h:h + 1],
                               in1=MASK[0:R, 0:R], op0=ALU.subtract, op1=ALU.subtract)
                last.then_inc(gc_ready, 1)
                dve.wait_ge(dexp_ready, ci + 1)
                tt(qg[:, :, 0:R], gproj[:, GQ:GQ + GH, cols], egr[:, :, 0:R], ALU.mult)
                tt(bex[0:R, :], bt, egc[0:R, :], ALU.mult)
                dve.wait_ge(kq_done, ci + 1)
                for b, (h0, h1) in enumerate(HB):
                    for h in range(h0, h1):
                        last = stt(out=bm[0:R, h, 0:R], in0=bank(3 + b)[0:R, R * (h - h0):R * (h - h0 + 1)],
                                   scalar=bt[:, h:h + 1], in1=dec[0:R, h, 0:R], op0=ALU.mult, op1=ALU.mult)
                    tt(qd[0:R, h0:h1, 0:R], view(bank(5 + b)[0:R, 0:R * (h1 - h0)], h1 - h0, R), dec[0:R, h0:h1, 0:R],
                       ALU.mult)
                own(last)
                tt(sub(bm), sub(bm), heads(STRICT), ALU.mult).then_inc(bm_ready, 1)
                dve.wait_ge(bm_ready, ci + 1)
                dve.wait_ge(tr_done, ci + 1)
                for b, (h0, h1) in enumerate(HB):
                    dve.tensor_copy(bmt[0:R, h0:h1, 0:R], view(bank(3 + b)[0:R, 0:R * (h1 - h0)], h1 - h0, R))
                    dve.tensor_copy(qt_[0:R, h0:h1, 0:R], view(bank(5 + b)[0:R, 0:R * (h1 - h0)], h1 - h0, R))
                    for h in range(h0, h1):
                        last = ts(vb[0:R, h, :], bank((2, 7)[b])[0:R, P * (h - h0):P * (h - h0 + 1)], bt[:, h:h + 1],
                                  None, ALU.mult)
                own(last)
                tt(sub(pw), sub(bm), heads(GC["diag"]), ALU.mult)
                own(tt(sub(pwt), sub(bmt), heads(GC["diag"]), ALU.mult))
                tt(sub(tt_), sub(pwt), heads(ident), ALU.add).then_inc(inv_dve, 1)
                n.dve += 1

                def add(t, b0):
                    for b, (h0, h1) in enumerate(HB):
                        last = tt(t[0:R, h0:h1, 0:R], t[0:R, h0:h1, 0:R],
                                  view(bank(b0 + b)[0:R, 0:R * (h1 - h0)], h1 - h0, R), ALU.add)
                    return last

                for k in range(squares + merges):
                    if k < squares - 1:
                        n.pe += 2
                        dve.wait_ge(inv_pe, n.pe)
                        for b, (h0, h1) in enumerate(HB):
                            dve.tensor_copy(pwt[0:R, h0:h1, 0:R], view(bank(5 + b)[0:R, 0:R * (h1 - h0)], h1 - h0, R))
                    else:
                        n.pe += 2 if k == squares and merges else 1
                    n.pe += 1
                    dve.wait_ge(inv_pe, n.pe)
                    dve.wait_ge(inv_dve, n.dve)
                    if squares - 1 <= k < squares + merges - 1:
                        tt(sub(pw), sub(bm), heads(GC["off"][:, k - squares + 1, :]), ALU.mult)
                    if squares <= k < squares + merges - 1:
                        add(tn, 5)
                    add(tt_, 0).then_inc(inv_dve, 1)
                    n.dve += 1
                if R == P:
                    dve.wait_ge(sup_mm, ci + 1)
                    for b, (h0, h1) in enumerate(HB):
                        for h in range(h0, h1):
                            last = stt(out=st_p[:, h, :], in0=st_p[:, h, :], scalar=egr[:, h, P - 1:P],
                                       in1=bank(b)[:, P * (h - h0):P * (h - h0 + 1)], op0=ALU.mult, op1=ALU.add)
                    last.then_inc(sup_done, 1)
                    continue
                dve.wait_ge(nwt_ready, ci + 1)
                dve.tensor_copy(wm.rearrange("p h (s c) -> p h s c", s=NS)[:, :, :, 0:DT],
                                nwt[:, :, 0:TS].rearrange("p h (s t) -> p h s t", s=NS)).then_inc(wm_ready, 1)
                for h in range(GH):
                    dve.wait_ge(vns_ready, h + 1)
                    tt(vx, vnw[0:R, h, :].unsqueeze(1).to_broadcast([R, NS, P]), bcast(GC["seq"][0:R, :], R, NS, P),
                       ALU.mult).then_inc(vx_ready, 1)
                    dve.wait_ge(snew_mm, h + 1)
                    egl = egr[:, h, 0:TS].rearrange("p (s t) -> p s t", t=DT)[:, :, DT - 1]
                    own(tt(sg[h % 2], sg[h % 2], bcast(egl, P, NS, P), ALU.mult))
                    tt(sg[h % 2], sg[h % 2], view(banks(6, 2), NS, P), ALU.add).then_inc(snew_ready, 1)
            dve.wait_ge(conv_done, 20)
            for c in range(12, 18):
                h = c - 12
                dve.wait_ge(cn_std, c + 1)
                own(dve.reciprocal(rstd, rstd))
                own(stt(out=mixT[:, h, :], in0=mixT[:, h, :], scalar=C["g_o"], in1=rstd, op0=ALU.mult, op1=ALU.mult))
                tt(mixT[:, h, :], mixT[:, h, :], gproj[:, GZ + h, :], ALU.mult).then_inc(cn_ready, 1)

        @block.tensor
        def _(pe):
            mm = pe.matmul

            def gemm(name, ktiles, rhs):
                wb, tiles, eb = wbase[name], TILES[name], evac_base[name]
                evac = act_out if name in ("nsa_in", "up0", "gdn_in", "up1") else dve_out
                per = 8 if ktiles == KT else 2

                def tile(i, j, t):
                    if not isinstance(t, int) or t >= 2:
                        pe.wait_ge(evac, eb + t - 1)
                    for k in range(ktiles):
                        hp = j // 2 if ktiles == KT else 2 * j + k // 16
                        slot = (wb + hp) % 4
                        if (ktiles == KT and j % 2 == 0 and k == 0) or (ktiles != KT and k % 16 == 0):
                            pe.wait_ge(in_panel[slot], 16 * (panel_uses(slot, wb + hp) + i))
                        if ktiles == KT:
                            lhs = view(ring[slot], KT, 256)[:, k, P * (j % 2):P * (j % 2 + 1)]
                        else:
                            lhs = view(ring[slot], 16, P)[:, k % 16, :]
                        mm(bank(j % 2), lhs, rhs[:, k, 0:TP], start=k == 0, stop=k == ktiles - 1)
                        last = mm(bank(2 + j % 2)[:, 0:TS], lhs, rhs[:, k, TP:TT_], start=k == 0, stop=k == ktiles - 1)
                    last.then_inc(pe_out, 1)

                trips = tiles // per if tiles >= 2 * per else 0
                if trips:
                    with pe.Fori(0, trips) as i:
                        for j in range(per):
                            tile(i, j, i * per + j)
                for t in range(trips * per, tiles):
                    tile(t // per, t % per, t)

            def norm(n):
                for k in range(KT):
                    pe.wait_ge(sq_ready, n * KT + k + 1)
                    mm(bank(0), ones, sq[:, k % 2, 0:TP], start=k == 0, stop=k == KT - 1)
                    last = mm(bank(1)[:, 0:TS], ones, sq[:, k % 2, TP:TT_], start=k == 0, stop=k == KT - 1)
                    last.then_inc(sq_used, 1)

            def memory_kv():
                pe.wait_ge(in_common, 16)
                pe.wait_ge(mem_sq, KT)
                for k in range(KT):
                    last = mm(bank(0)[:, 0:MEM], ones, sqm[:, k, :], start=k == 0, stop=k == KT - 1)
                last.then_inc(mem_ss, 1)
                for l in range(2):
                    pe.wait_ge(memn_ready, KT * (l + 1))
                    pe.wait_ge(in_panel[2 * l], 16)
                    wk, wv = view(ring[2 * l], KT, MEM), view(ring[2 * l + 1], KT, MEM)
                    for hp in range(2):
                        for k in range(KT):
                            last = mm(bank(1 + 2 * l)[:, MEM * hp:MEM * (hp + 1)], wk[:, k, P * hp:P * (hp + 1)],
                                      memn[:, l, k, :], start=k == 0, stop=k == KT - 1)
                    last.then_inc(pe_out, 1)
                    pe.wait_ge(in_panel[2 * l + 1], 16)
                    for m in range(2):
                        for k in range(KT):
                            last = mm(bank(2 + 2 * l)[:, MEM * m:MEM * (m + 1)], memn[:, l, k, P * m:P * (m + 1)],
                                      wv[:, k, :], start=k == 0, stop=k == KT - 1)
                    last.then_inc(pe_out, 1)

            def memory_attention(l):
                pr = (proj, gproj)[l]
                xq = (XQ0, XQ1)[l]
                kmem, vmem = view(mkv[l][:, 0:512], 2, MEM), view(mkv[l][:, 512:1024], 2, MEM)
                b = mb[l]
                pe.wait_ge(act_out, (NSA_T, NSA_T + 32 + GDN_T)[l])
                if l:
                    pe.wait_ge(in_mkv1, 16)
                else:
                    pe.wait_ge(memkv_ready, 2)

                def scores(qt):
                    if qt >= 2:
                        pe.wait_ge(xs_ready, 5 * l + qt - 1)
                    for hh in range(2):
                        for hp in range(2):
                            last = mm(bank(2 * (qt % 2) + hh)[:, MEM * hp:MEM * (hp + 1)],
                                      pr[64 * hh:64 * hh + 64, xq + hp, P * qt:P * (qt + 1)],
                                      kmem[64 * hh:64 * hh + 64, hp, :], start=True, stop=True)
                    last.then_inc(xm_ready, 1)

                def sample_scores():
                    pe.wait_ge(in_mcache, 16 * (l + 1))
                    pe.wait_ge(qm_ready, l + 1)
                    pe.wait_ge(xs_ready, 5 * l + 3)
                    for s in range(NS):
                        for hp in range(2):
                            last = mm(bank(0)[:, 0:MEM], b["qm"][:, MEM * s + P * hp:MEM * s + P * (hp + 1)],
                                      mcache[l][:, s, MEM * hp:MEM * (hp + 1)],
                                      start=s == hp == 0, stop=s == NS - 1 and hp == 1)
                    last.then_inc(xm_ready, 1)

                def values(n):
                    pe.wait_ge(xp_ready, 5 * l + n + 1)
                    if n:
                        pe.wait_ge(xpt_ready, 5 * l + n)
                    sm = b["sm"][n % 2]
                    for m in range(2):
                        for r in range(4 if n < 4 else 1):
                            last = pe.transpose(bank(4 + m)[:, P * r:P * (r + 1)], sm[:, r, P * m:P * (m + 1)], ident)
                    last.then_inc(xt_done, 1)
                    pe.wait_ge(xpt_ready, 5 * l + n + 1)
                    if n:
                        pe.wait_ge(mix_mem, 5 * l + n)
                    pt = b["pt"][n % 2]
                    if n < 4:
                        for hh in range(2):
                            for hp in range(2):
                                for m in range(2):
                                    last = mm(bank(6)[64 * hh:64 * hh + 64, P * hp:P * (hp + 1)],
                                              vmem[:, m, P * hp + 64 * hh:P * hp + 64 * hh + 64],
                                              pt[:, m, 2 * hh + hp, :], start=m == 0, stop=m == 1)
                    else:
                        for s in range(NS):
                            for hp in range(2):
                                for m in range(2):
                                    last = mm(bank(6)[:, 64 * hp + 8 * s:64 * hp + 8 * s + 8],
                                              mcache[l][:, s, 512 + MEM * m + P * hp:512 + MEM * m + P * (hp + 1)],
                                              pt[:, m, 0, 16 * s + 8 * hp:16 * s + 8 * hp + 8],
                                              start=m == 0, stop=m == 1)
                    last.then_inc(xo_done, 1)

                scores(0)
                scores(1)
                for n in range(5):
                    values(n)
                    if n < 2:
                        scores(n + 2)
                    elif n == 2:
                        sample_scores()

            memory_kv()
            norm(0)
            pe.wait_ge(h_ready, KT)
            gemm("nsa_in", KT, hT)
            memory_attention(0)
            pe_nsa_prompt(pe)
            pe_nsa_sample(pe)
            pe.wait_ge(seq_done, NS)
            gemm("out0", KT, mixT)
            norm(1)
            pe.wait_ge(h_ready, 2 * KT)
            gemm("up0", KT, hT)
            pe.wait_ge(u_ready, FFT)
            gemm("down0", FFT, u)
            norm(2)
            pe.wait_ge(h_ready, 3 * KT)
            gemm("gdn_in", KT, hT)
            memory_attention(1)
            pe_gdn(pe)
            gemm("out1", KT, mixT)
            norm(3)
            pe.wait_ge(h_ready, 4 * KT)
            gemm("up1", KT, hT)
            pe.wait_ge(u_ready, 2 * FFT)
            gemm("down1", FFT, u)
            norm(4)

        @block.scalar
        def _(act):
            own = Chain(act, chain_act)
            f = act.activation

            def norm(n):
                if n == 0:
                    act.wait_ge(in_x, 16)
                else:
                    act.wait_ge(dve_out, 8 * n)
                for k in range(KT):
                    if n or k >= 2:
                        act.wait_ge(sq_used, n * KT + k - 1)
                    f(sq[:, k % 2, :], xT[:, k, :], ACT.Square).then_inc(sq_ready, 1)
                act.wait_ge(sq_used, (n + 1) * KT)
                if n:
                    act.wait_ge(h_ready, n * KT)
                f(rstd[:, 0:TP], bank(0), ACT.Sqrt, bias=C["eps"], scale=1.0 / D).then_inc(std_ready, 1)
                f(rstd[:, TP:TT_], bank(1)[:, 0:TS], ACT.Sqrt, bias=C["eps"], scale=1.0 / D).then_inc(std_ready, 1)

            def copy_out(name, dst):
                for t in range(TILES[name]):
                    act.wait_ge(pe_out, obase[name] + t + 1)
                    f(dst[:, t, 0:TP], bank(t % 2), ACT.Copy)
                    f(dst[:, t, TP:TT_], bank(2 + t % 2)[:, 0:TS], ACT.Copy).then_inc(act_out, 1)

            def up_out(l):
                with act.Fori(0, 16) as i:
                    for j in range(2):
                        dst = u[:, bass.ds(2 * i + j, 1), :].rearrange("p a n -> p (a n)")
                        act.wait_ge(pe_out, obase[f"up{l}"] + 1 + j + 2 * i)
                        act.nop(nofuse=True)
                        f(dst[:, 0:TP], bank(j), ACT.Relu)
                        f(dst[:, TP:TT_], bank(2 + j)[:, 0:TS], ACT.Relu).then_inc(act_out, 1)
                        act.wait_ge(act_out, evac_base[f"up{l}"] + 1 + j + 2 * i)
                        act.nop(nofuse=True)
                        f(dst, dst, ACT.Square).then_inc(u_ready, 1)

            def memory_kv():
                act.wait_ge(in_mem, 16)
                for k in range(KT):
                    f(sqm[:, k, :], memT[:, k, :], ACT.Square).then_inc(mem_sq, 1)
                act.wait_ge(mem_ss, 1)
                f(rstdm, bank(0)[:, 0:MEM], ACT.Sqrt, bias=C["eps"], scale=1.0 / D).then_inc(mem_std, 1)
                for l in range(2):
                    for half in range(2):
                        act.wait_ge(pe_out, 2 * l + half + 1)
                        f((mkv0, mkv1_tmp)[l][:, 512 * half:512 * (half + 1)], bank(1 + 2 * l + half), ACT.Copy)\
                            .then_inc(memkv_ready, 1)

            def memory_attention(l):
                b = mb[l]
                for n in range(5):
                    heads = 4 if n < 4 else 1
                    act.wait_ge(xmax_ready, 5 * l + n + 1)
                    if n >= 2:
                        act.wait_ge(xt_done, 5 * l + n - 1)
                    for r in range(heads):
                        last = f(b["sm"][n % 2][:, r, :], bank(2 * (n % 2) + r // 2)[:, MEM * (r % 2):MEM * (r % 2 + 1)]
                                 if n < 4 else bank(0)[:, 0:MEM], ACT.Exp, scale=HD ** -0.5,
                                 bias=b["stat"][:, n % 2, r:r + 1], accum_out=b["stat"][:, n % 2, 4 + r:5 + r])
                    own(last)
                    f(b["stat"][:, n % 2, 12:13], b["stat"][:, n % 2, 4:5], ACT.Copy).then_inc(xs_ready, 1)
                    act.wait_ge(xt_done, 5 * l + n + 1)
                    if n >= 2:
                        act.wait_ge(xo_done, 5 * l + n - 1)
                    for m in range(2):
                        last = f(b["pt"][n % 2][:, m, 0:heads, :].rearrange("p r q -> p (r q)"),
                                 bank(4 + m)[:, 0:P * heads], ACT.Copy)
                    last.then_inc(xpt_ready, 1)

            memory_kv()
            norm(0)
            copy_out("nsa_in", proj)
            memory_attention(0)
            act_nsa_prompt(act, own)
            act_nsa_sample(act, own)
            norm(1)
            up_out(0)
            norm(2)
            copy_out("gdn_in", gproj)
            memory_attention(1)
            act_gdn(act, own)
            norm(3)
            act.wait_ge(stored, 32)
            for b in range(2):
                act.wait_ge(state_stored[b], 16 * (GH // 2))
            up_out(1)
            norm(4)

        @block.vector
        def _(dve):
            own = Chain(dve, chain_dve)
            tt, ts, stt = dve.tensor_tensor, dve.tensor_scalar, dve.scalar_tensor_tensor

            def norm(n, gain):
                dve.wait_ge(std_ready, 2 * n + 2)
                own(dve.reciprocal(rstd, rstd))
                for k in range(KT):
                    stt(out=hT[:, k, :], in0=xT[:, k, :], scalar=gain[:, k:k + 1], in1=rstd, op0=ALU.mult,
                        op1=ALU.mult).then_inc(h_ready, 1)

            def residual(name):
                for t in range(8):
                    dve.wait_ge(pe_out, obase[name] + t + 1)
                    tt(xT[:, t, 0:TP], xT[:, t, 0:TP], bank(t % 2), ALU.add)
                    tt(xT[:, t, TP:TT_], xT[:, t, TP:TT_], bank(2 + t % 2)[:, 0:TS], ALU.add).then_inc(dve_out, 1)

            def memory_kv():
                dve.wait_ge(mem_std, 1)
                own(dve.reciprocal(rstdm, rstdm))
                for l in range(2):
                    for k in range(KT):
                        stt(out=memn[:, l, k, :], in0=memT[:, k, :], scalar=C["g_mem"][:, l, k:k + 1], in1=rstdm,
                            op0=ALU.mult, op1=ALU.mult).then_inc(memn_ready, 1)

            def memory_attention(l):
                b = mb[l]
                pr, xq = (proj, gproj)[l], (XQ0, XQ1)[l]
                own(dve.memset(b["qm"], 0.0))
                dve.wait_ge(act_out, (NSA_T, NSA_T + 32 + GDN_T)[l])
                for hp in range(2):
                    for hh in range(2):
                        r = slice(64 * hh, 64 * hh + 64)
                        dst = b["qm"][r, :].rearrange("p (s c) -> p s c", s=NS)
                        at = P * hp + 8 * hp + 4 * hh
                        last = dve.tensor_copy(dst[:, :, at:at + DT],
                                               pr[r, xq + hp, TP:TT_].rearrange("p (s t) -> p s t", s=NS))
                last.then_inc(qm_ready, 1)
                for n in range(5):
                    heads, st = (4 if n < 4 else 1), b["stat"][:, n % 2, :]
                    dve.wait_ge(xm_ready, 5 * l + n + 1)
                    own(dve.tensor_reduce(st[:, 0:heads], banks(2 * (n % 2), 2).rearrange("p (r c) -> p r c", r=4)
                                          if n < 4 else bank(0)[:, 0:MEM], AX.X, ALU.max))
                    ts(st[:, 0:heads], st[:, 0:heads], -HD ** -0.5, None, ALU.mult).then_inc(xmax_ready, 1)
                    dve.wait_ge(xs_ready, 5 * l + n + 1)
                    own(dve.reciprocal(st[:, 8:8 + heads], st[:, 4:4 + heads]))
                    sm = b["sm"][n % 2][:, 0:heads, :]
                    tt(sm, sm, bcast(st[:, 8:8 + heads], P, heads, MEM), ALU.mult).then_inc(xp_ready, 1)
                    dve.wait_ge(xo_done, 5 * l + n + 1)
                    if n < 4:
                        dve.tensor_copy(mixT[:, 6:8, P * n:P * (n + 1)], view(bank(6)[:, 0:2 * P], 2, P))\
                           .then_inc(mix_mem, 1)
                    else:
                        for hh in range(2):
                            r = slice(64 * hh, 64 * hh + 64)
                            o = bank(6)[r, 0:P].rearrange("p (h s c) -> p h s c", h=2, s=NS)
                            last = dve.tensor_copy(
                                mixT[r, 6:8, TP:TT_].rearrange("p h (s t) -> p h s t", s=NS),
                                o[:, :, :, 4 * hh:4 * hh + DT])
                        last.then_inc(mix_mem, 1)

            memory_kv()
            norm(0, C["g_mix"][:, 0, :])
            memory_attention(0)
            dve_nsa_prompt(dve, own)
            dve_nsa_sample(dve, own)
            residual("out0")
            norm(1, C["g_ffn"][:, 0, :])
            residual("down0")
            norm(2, C["g_mix"][:, 1, :])
            memory_attention(1)
            dve_gdn(dve, own)
            residual("out1")
            norm(3, C["g_ffn"][:, 1, :])
            residual("down1")
            norm(4, C["g_fin"])


def constants():
    f = np.float32
    ar = np.arange
    c = {}
    slopes = np.exp2(f(-8.0) * ar(1, 13, dtype=f) / f(12)).astype(f)
    c["ident"], c["ones"] = np.eye(P, dtype=f), np.ones((P, P), f)
    c["eps"], c["one"] = np.full((P, 1), EPS, f), np.ones((P, 1), f)
    d = ar(P)[:, None] + TP - P - ar(TP)[None]
    c["dist"] = np.where(d >= 0, d, -NEG).astype(f)
    pos = ar(P)[:, None, None] + P * ar(4)[None, :, None]
    d = pos - (16 * ar(NCP) + 31)[None, None]
    c["cdist"] = np.where(d >= 0, d, -NEG).astype(f)
    c["cvis"] = (pos[:, :, 0] >= 31).astype(f)
    c["nslope"] = np.tile(-slopes, (P, 1))
    row = ar(ROWS)
    kv, g, t = row // 32, row % 32 // 4, row % 4
    real = g < NG
    sl = np.where(real, slopes[np.minimum(6 * kv + g, 11)], 0).astype(f)[:, None]

    def rows(a):
        return np.concatenate([a.astype(f), np.zeros((P - a.shape[0],) + a.shape[1:], f)])

    pos = (PAST + t)[:, None]
    c["b_slc"] = rows(-sl * (pos - ar(PAST)[None]).astype(f))
    wp = PAST - WIN + ar(WIN)[None]
    c["b_win"] = rows(np.where(pos - wp < WIN, -sl * (pos - wp).astype(f), f(NEG)))
    c["b_cmp"] = rows(-sl * (pos - (16 * ar(NCB) + 31)[None]).astype(f))
    d = t[:, None] - ar(DT)[None]
    c["b_new"] = rows(np.where(d >= 0, -sl * d.astype(f), f(NEG)))
    c["same"] = rows((kv[:, None] == kv) & (t[:, None] == t) & real[:, None])
    tok = ar(TS)[:, None, None]
    c["pick"] = rows(tok == DT * ar(NS)[None, :, None] + t[None, None])
    col = ar(36)
    c["head"] = rows(real[:, None] & (col[None] // 6 == g[:, None]) & (col[None] % 2 == kv[:, None]))
    n = ar(30)
    c["lower"] = np.broadcast_to((n[None] < n[:, None]).astype(f), (P, 30, 30))
    i, j = ar(P)[:, None], ar(P)[None]
    c["cum"] = (i <= j).astype(f)
    si, sj = ar(TS)[:, None], ar(TS)[None]
    same = si // DT == sj // DT
    c["cum_s"], c["all_s"] = rows(same & (si <= sj)), rows(same)
    c["mask"], c["strict"] = np.where(j <= i, 0, NEG).astype(f), np.where(j < i, -1, 0).astype(f)
    c["mask_s"], c["strict_s"] = rows(np.where(same & (sj <= si), 0, NEG)), rows(np.where(same & (sj < si), -1, 0))
    c["diag"] = (i // 16 == j // 16).astype(f)
    c["off"] = np.stack([(i // (2 * m) == j // (2 * m)) & (i // m > j // m) for m in (16, 32, 64)], 1).astype(f)
    c["seq"] = rows(si // DT == ar(NS)[None])
    return c


def pack(tb, parts):
    out = [np.ascontiguousarray(np.asarray(parts[k], np.float32).reshape(P, -1)) for k in tb.at]
    assert [a.shape[1] for a in out] == [int(np.prod(s)) for _, s in tb.at.values()], [a.shape for a in out]
    return np.concatenate(out, 1)


def kernel(**inputs):
    import concourse.bacc as bacc
    from concourse.bass_utils import run_bass_kernel_spmd

    a = {k: np.asarray(v) for k, v in inputs.items()}
    c = constants()
    chan = lambda v: v.reshape(v.shape[:-1] + (KT, P)).transpose(v.ndim, *range(v.ndim))
    cols = lambda x: x.T.reshape(KT, P, -1).transpose(1, 0, 2)

    for name, key in (("g_mix", "norm_mix_g"), ("g_mem", "norm_mem_g"), ("g_ffn", "norm_ffn_g")):
        c[name] = chan(a[key])
    c["g_fin"] = chan(a["final_norm_g"])
    lpair = lambda w: w.reshape(16, 2 * HD, -1).transpose(1, 0, 2)
    c["pe"] = np.stack([lpair(a[k][0].reshape(32, HD, 1))[:, :, 0] for k in ("cmp_pe_k", "cmp_pe_v")], 1)
    c["w2"] = np.stack([a["cmp_w2_k"][0], a["cmp_w2_v"][0]], 1)
    c["conv_w"] = a["gdn_conv_w"][0].reshape(4, 18, P).transpose(2, 1, 0)
    c["g_o"] = a["gdn_norm_g"][0][:, None]
    c["a_log"], c["dt_bias"] = (np.broadcast_to(a[k][0], (P, GH)) for k in ("gdn_a_log", "gdn_dt_bias"))

    def wide(w):
        n = -(-w.shape[1] // 256)
        w = np.concatenate([w, np.zeros((D, 256 * n - w.shape[1]), w.dtype)], 1)
        return w.reshape(KT, P, n, 256).transpose(2, 1, 0, 3).reshape(n, P, 2048)

    def tall(w):
        return w.reshape(2, 16, P, KT, P).transpose(3, 0, 2, 1, 4).reshape(16, P, 2048)

    w = a["nsa_w_in"][0]
    heads = lambda x: x.reshape(-1, NKV, NG, HD).transpose(0, 2, 1, 3).reshape(x.shape[0], -1)
    gates = w[:, 1536:1572].reshape(D, NKV, NG, 3)[..., [1, 2, 0]].transpose(0, 2, 3, 1).reshape(D, 36)
    nsa_in = np.concatenate([heads(w[:, 0:768]), w[:, 768:1536], w[:, 1572:1828], gates], 1)
    w = a["gdn_w_in"][0]
    gdn_w = np.concatenate([w[:, 0:3072], w[:, 3084:3340], w[:, 3072:3084]], 1)
    wo = a["w_out"]
    out0 = np.concatenate([heads(wo[0][:768].T).T, wo[0][768:]], 0)
    w1 = np.stack([lpair(a[k][0]).reshape(P, 2048) for k in ("cmp_w1_k", "cmp_w1_v")])
    panels = np.concatenate([wide(a["w_mem_kv"][0]), wide(a["w_mem_kv"][1]), wide(nsa_in), w1, wide(out0),
                             wide(a["w_up"][0]), tall(a["w_down"][0]), wide(gdn_w), wide(wo[1]),
                             wide(a["w_up"][1]), tall(a["w_down"][1])])

    kv = a["cache_nsa_kv"][:, :, 0]
    ck = kv[:, :, 0:2].reshape(NPHYS, 8, 8, 2, 2, NKV, HD).transpose(0, 3, 6, 4, 2, 5, 1).reshape(NPHYS, P, 256)
    pages = np.concatenate([ck, kv[:, :, 2].reshape(NPHYS, PAGE, P).transpose(0, 2, 1), kv[:, :, 3].reshape(NPHYS, PAGE, P)], 2)
    wn = a["cache_nsa_win"][:, 0]
    win = np.concatenate([wn[:, :, 0].reshape(NS, WIN, P).transpose(0, 2, 1),
                          wn[:, :, 1].reshape(NS, 4, P, P).transpose(0, 2, 1, 3).reshape(NS, P, 512)], 2)
    mc = a["cache_mem_kv"].transpose(1, 0, 2, 3, 4, 5)
    mk = mc[:, :, :, 0].reshape(2, NS, MEM, 2, P).transpose(0, 1, 4, 3, 2).reshape(2, NS, P, 512)
    mv = mc[:, :, :, 1].reshape(2, NS, 2, P, MEM).transpose(0, 1, 3, 2, 4).reshape(2, NS, P, 512)

    arrays = dict(
        x=np.concatenate([cols(a["x_prompt"][0]), cols(a["x_sample"].reshape(TS, D))], 2),
        mem=cols(a["mem_prompt"][0]), w=panels, common=pack(COMMON, c), prompt=pack(PROMPT_T, c),
        sample=pack(SAMPLE_T, c), gdn=pack(GDN_TB, c), pages=pages, win=win, mcache=np.concatenate([mk, mv], 3),
        conv=a["state_gdn_conv"][:, 0].reshape(NS, 3, 18, P).transpose(3, 2, 0, 1),
        state=a["state_gdn_s"][:, 0].transpose(1, 2, 0, 3), table=a["page_table"].reshape(1, NS * NPAGE))
    outs = dict(y=(P, KT, TT_), kv=(P, 6, TT_), win_o=(NS, P, 1024), conv_p=(P, 18, 3), conv_s=(P, 18, NS, 3),
                state_p=(P, GH, P), state_s=(GH, P, NS, P), mem_o=(2, P, 1024))
    nc = bacc.Bacc("TRN2", target_bir_lowering=False, num_devices=1)
    ins, args = {}, []
    for name, v in arrays.items():
        v = np.ascontiguousarray(v)
        ins[f"in_{name}"] = v
        args.append(nc.dram_tensor(f"in_{name}", v.shape, mybir.dt.from_np(v.dtype), kind="ExternalInput").ap())
    for name, shape in outs.items():
        args.append(nc.dram_tensor(f"out_{name}", shape, F32, kind="ExternalOutput").ap())
    build(nc, *args)
    r = run_bass_kernel_spmd(nc, [ins], core_ids=[0]).results[0]
    o = {k: np.asarray(r[f"out_{k}"]) for k in outs}

    y = o["y"].transpose(2, 1, 0).reshape(TT_, D)
    kvr = o["kv"].transpose(2, 1, 0).reshape(TT_, 6, NKV, HD)
    wk = o["win_o"][:, :, 0:512].transpose(0, 2, 1)
    wv = o["win_o"][:, :, 512:].reshape(NS, P, 4, P).transpose(0, 2, 1, 3).reshape(NS, WIN, P)
    old = np.stack([wk, wv], 2).reshape(NS, WIN, 2, NKV, HD)
    new = kvr[TP:, 4:6].reshape(NS, DT, 2, NKV, HD)
    mo = o["mem_o"]
    mkp = mo[:, :, 0:512].reshape(2, P, 2, MEM).transpose(0, 3, 2, 1).reshape(2, MEM, XH, HD)
    mvp = mo[:, :, 512:].reshape(2, P, 2, MEM).transpose(0, 2, 1, 3).reshape(2, MEM, XH, HD)
    res = (y[:TP][None], y[TP:].reshape(NS, DT, D), kvr[:TP, 0:4][None, :, None], kvr[TP:, 0:4].reshape(NS, DT, 1, 4, NKV, HD),
           kvr[:TP, 4:6][None, None], np.concatenate([old[:, DT:], new], 1)[:, None],
           o["state_p"].transpose(1, 0, 2)[None, None], o["state_s"].transpose(2, 0, 1, 3)[:, None],
           o["conv_p"].transpose(2, 1, 0).reshape(1, 1, 3, 2304),
           o["conv_s"].transpose(2, 3, 1, 0).reshape(NS, 1, 3, 2304),
           np.stack([mkp, mvp], 2)[None])
    return tuple(np.ascontiguousarray(x) for x in res)
```

```python
from contextlib import ExitStack

import numpy as np

import concourse.bass as bass
from concourse import mybir

F32 = mybir.dt.float32
I32 = mybir.dt.int32
ALU = mybir.AluOpType
ACT = mybir.ActivationFunctionType
AX = mybir.AxisListType

P = 128
D = 1024
KT = D // P
TP, NS, DT = 512, 8, 4
TS = NS * DT
TT_ = TP + TS
HALF = TT_ // 2
MEM = 256
NKV, NG, HD = 2, 6, 64
NPAGE, PAGE = 16, 128
PAST = NPAGE * PAGE
NPHYS = (NS * NPAGE * 5 + 3) // 4
NCB = PAST // 16 - 1
NCP = TP // 16 - 1
NSLC = PAST // 64
TOPN = 16
WIN = 512
XH = 4
GH = 6
EPS = 1e-6
NEG = -1e30
FFT = 4 * D // P
NSA_T, GDN_T = 15, 27
ROWS = 64
PAST2 = PAST // 2

Q0, CK, CV, SK, SV, WK, WV, XQ0, GT = 0, 6, 7, 8, 9, 10, 11, 12, 14
GQ, GK, GV, GZ, XQ1, BA = 0, 6, 12, 18, 24, 26


class Table:

    def __init__(self, *parts):
        self.at, self.size = {}, 0
        for name, *shape in parts:
            n = int(np.prod(shape))
            self.at[name] = (self.size, tuple(shape))
            self.size += n


COMMON = Table(("ident", P), ("ones", P), ("g_mix", 2, KT), ("g_mem", 2, KT), ("g_ffn", 2, KT), ("g_fin", KT),
               ("pe", 2, 16), ("w2", 2, HD), ("conv_w", 18, 4), ("g_o", 1), ("a_log", GH), ("dt_bias", GH),
               ("eps", 1), ("one", 1), ("onecol", 47))
PROMPT_T = Table(("dist", TP), ("cdist", 4, NCP), ("cvis", 4), ("nslope", 12))
SAMPLE_T = Table(("b_slc", PAST // 2), ("b_win", WIN), ("b_cmp", NCB), ("b_new", DT), ("same", P), ("pick", NS, ROWS),
                 ("head", 36), ("lower", NSLC // 2, NSLC - 2), ("drop", NSLC // 2))
GDN_TB = Table(("cum", P), ("cum_s", TS), ("all_s", TS), ("mask", P), ("mask_s", TS), ("strict", P), ("strict_s", TS),
               ("diag", P), ("off", 3, P), ("seq", NS))


def view(ap, *shape):
    if len(shape) < 2:
        return ap
    names = "abcd"[:len(shape)]
    return ap.rearrange(f"p ({' '.join(names)}) -> p {' '.join(names)}", **dict(zip(names[1:], shape[1:])))


class Arena:

    def __init__(self, t, lo, hi):
        self.t, self.lo, self.hi = t, lo, hi

    def take(self, *shape, rows=P):
        n = int(np.prod(shape))
        assert self.lo + n <= self.hi, (self.lo, n, self.hi)
        ap = self.t[0:rows, self.lo:self.lo + n]
        self.lo += n
        return view(ap, *shape)

    def table(self, tb):
        ap = self.take(tb.size)
        return ap, {k: view(ap[:, o:o + int(np.prod(s))], *s) for k, (o, s) in tb.at.items()}


class Chain:

    def __init__(self, eng, sem):
        self.eng, self.sem, self.n = eng, sem, 0

    def __call__(self, ins):
        ins.then_inc(self.sem, 1)
        self.n += 1
        self.eng.wait_ge(self.sem, self.n)


def bcast(ap, *shape):
    while len(ap.shape) < len(shape):
        ap = ap.unsqueeze(len(ap.shape))
    return ap.to_broadcast(list(shape))


def build(nc, x_in, mem_in, w_in, common_in, prompt_in, sample_in, gdn_in, pages_in, win_in, mcache_in, conv_in,
          state_in, table_in, y_out, kv_out, win_out, conv_out_p, conv_out_s, state_out_p, state_out_s, mem_out):
    with ExitStack() as ctx:
        sem = lambda name: ctx.enter_context(nc.semaphore(name))
        TOTAL = 53060
        sbuf = ctx.enter_context(nc.sbuf_tensor("sbuf", [P, TOTAL], F32))
        pages_sb = ctx.enter_context(nc.sbuf_tensor("page_table", [1, NS * NPAGE], I32))
        psum = ctx.enter_context(nc.psum_tensor("psum", [P, 8, 512], F32))
        bank = lambda b: psum[:, b, :]
        both = lambda j: psum[:, 2 * j:2 * j + 2, 0:HALF]
        halves_of = lambda ap: view(ap, 2, HALF)
        banks = lambda b, n: psum[:, b:b + n, :].rearrange("p a n -> p (a n)")

        top = Arena(sbuf, 0, TOTAL)
        _, C = top.table(COMMON)
        common_ap = sbuf[:, 0:COMMON.size]
        xT = top.take(KT, TT_)
        hT = top.take(KT, TT_)
        ring = [top.take(2048) for _ in range(4)]
        big0 = top.lo
        top.lo += 16384
        pj0 = top.lo
        top.lo += 8192
        work0 = top.lo
        big = lambda: Arena(sbuf, big0, big0 + 16384)
        pj = lambda: Arena(sbuf, pj0, pj0 + NSA_T * TT_)
        rest = lambda: Arena(sbuf, work0, TOTAL)
        mixT = hT

        a = rest()
        sq = a.take(2, TT_)
        rstd = a.take(TT_)
        norm_end = a.lo
        after_norm = lambda: Arena(sbuf, norm_end, TOTAL)

        persist = after_norm()
        gsamp = persist.take(36, rows=TS)
        pebias = persist.take(2)
        free0 = persist.lo
        free = lambda: Arena(sbuf, free0, TOTAL)

        a = free()
        mkv0 = a.take(1024)
        mkv0_end = a.lo
        memT = a.take(KT, MEM)
        a = big()
        sqm = a.take(KT, MEM)
        memn = a.take(2, KT, MEM)
        rstdm = a.take(MEM)
        mkv1_tmp = a.take(1024)

        proj = pj().take(NSA_T, TT_)
        page = [view(sbuf[:, big0 + 8192 * s:big0 + 8192 * (s + 1)], NPAGE, 512) for s in range(2)]
        mcache = [view(sbuf[:, big0 + 8192:big0 + 16384], NS, 1024), None]

        def memory_buffers(a):
            return dict(sm=[a.take(4, MEM) for _ in range(2)], pt=[a.take(2, 4, P) for _ in range(2)],
                        stat=a.take(2, 16), qm=a.take(NS * (2 * P + 16)))

        a = Arena(sbuf, mkv0_end, TOTAL)
        mb = [memory_buffers(a), None]
        CX = NKV * TP // 16 + 2
        xtp = a.take(2, 8, CX)
        pab = a.take(2, 2, CX)
        phid = a.take(2, 2, 32)
        mkv = [mkv0, None]

        a = Arena(sbuf, big0 + 8192, big0 + 16384)
        prompt_ap, PT = a.table(PROMPT_T)
        s_sb = [a.take(4, TP) for _ in range(2)] + [None]
        qs = a.take(2, TP)
        vn = a.take(2, 4, P)
        a = free()
        s_sb[2] = a.take(4, TP)
        scp = [a.take(2, 32) for _ in range(3)]
        ptp = [a.take(4, P) for _ in range(3)]
        ptc = a.take(2, P, rows=NCP)
        stp = a.take(3, 24)
        gnat = a.take(4, 36)
        kcp = a.take(2, NCP)
        vcp = a.take(P, rows=NCP)

        a = free()
        sample_ap, ST = a.table(SAMPLE_T)
        S_NEW, S_WIN, S_WNEW, S_CMP = PAST2, PAST2 + DT, PAST2 + DT + WIN, PAST2 + 2 * DT + WIN
        ssc = a.take(S_CMP + NCB + 1)
        low, high = ssc[0:ROWS, :], ssc[ROWS:P, :]
        pts = a.take(20, ROWS)
        ptcs = a.take(ROWS, rows=NCB)
        rank = ring[3]
        cab = a.take(2, 2, 2 * P)
        a.lo = work0
        chid = a.take(2, 2, P)
        kc = a.take(2, P)
        vc = a.take(2, P, rows=NCB)
        vnew = a.take(2, P, rows=DT)
        ptn = a.take(2, ROWS, rows=DT)
        imp = a.take(NSLC)
        imph = a.take(NSLC // 2)
        sel = a.take(NSLC // 2)
        impc = rank[:, 1800:1800 + P]
        qb = a.take(ROWS)
        vst = a.take(2, DT)
        gr = a.take(3, rows=ROWS)
        grt = a.take(36, rows=ROWS)
        sst = a.take(16)
        stl = sst[0:ROWS, :]
        assert a.lo <= norm_end
        wcache = [ring[2][:, 1024 * s:1024 * (s + 1)] for s in range(2)]
        u = view(sbuf[:, pj0 + 8192 - FFT * TT_:pj0 + 8192], FFT, TT_)

        a = big()
        gproj = a.take(GDN_T, TT_)
        gdn_b = a
        mcache[1] = view(sbuf[:, pj0:pj0 + 8192], NS, 1024)
        a = free()
        gdn_ap, GC = a.table(GDN_TB)
        sst1 = a.take(1)
        ban = a.take(5, 12)
        beta = a.take(5, GH)
        gat = a.take(5, GH)
        spl = a.take(5, GH)
        nea = a.take(GH)
        small_end = a.lo
        mkv[1] = a.take(1024)
        mb[1] = memory_buffers(a)
        cbuf = a.take(18, NS, 3)
        cout_s = gdn_b.take(18, NS, 3)
        cout_p = gdn_b.take(18, 3)
        a = rest()
        sacc, stmp = a.take(18, NS, DT), a.take(18, NS, DT)
        cacc = gdn_b.take(2, TP)
        rinv = rstd[:, 0:HALF]
        a = Arena(sbuf, small_end, TOTAL)
        cw = lambda a: a.take(GH, P)
        ug, dec, egr, bm, qt_, kbg, kdec, vb, pw = [cw(a) for _ in range(9)]
        gcn = a.take(2, 8)
        egc, bex, kde = a.take(GH), a.take(GH), a.take(GH)
        sg = [view(cacc.rearrange("p a n -> p (a n)"), NS, P), None, a.take(NS, P)]
        a = pj()
        a.hi = pj0 + 8192
        pwt, tt_, nwt, qg, st_p = [cw(a) for _ in range(5)]
        wm = a.take(GH, NS * (TS + DT))
        vx = a.take(NS, P, rows=TS)
        sg[1] = a.take(NS, P)
        qd, tn, vnw, zz = pw, nwt, dec, pwt

        in_common, in_x, in_mem, in_table = sem("in_common"), sem("in_x"), sem("in_mem"), sem("in_table")
        in_prompt_t, in_sample_t, in_gdn_t = sem("in_prompt_t"), sem("in_sample_t"), sem("in_gdn_t")
        in_panel = [sem(f"in_panel{s}") for s in range(4)]
        in_cmp = [sem(f"in_cmp{s}") for s in range(2)]
        in_pages = [sem(f"in_pages{s}") for s in range(2)]
        in_mcache, in_mkv1, in_conv = sem("in_mcache"), sem("in_mkv1"), sem("in_conv")
        in_state = [sem(f"in_state{i}") for i in range(3)]
        stored, mem_stored = sem("stored"), sem("mem_stored")
        state_stored = [sem(f"state_stored{i}") for i in range(3)]
        chain_act, chain_dve = sem("chain_act"), sem("chain_dve")
        mem_sq, mem_ss, mem_std, memn_ready, memkv_ready = map(sem, ("mem_sq", "mem_ss", "mem_std", "memn_ready",
                                                                     "memkv_ready"))
        pe_out = sem("pe_out")
        act_out = sem("act_out")
        dve_out = sem("dve_out")
        u_ready = sem("u_ready")
        sq_ready, sq_used, ss_done, std_ready, h_ready = map(sem, ("sq_ready", "sq_used", "ss_done", "std_ready",
                                                                   "h_ready"))
        xs_ready, xm_ready, xp_ready, xt_done, xpt_ready, xo_done, mix_mem = map(
            sem, ("xs_ready", "xm_ready", "xp_ready", "xt_done", "xpt_ready", "xo_done", "mix_mem"))
        qm_ready, xmax_ready = sem("qm_ready"), sem("xmax_ready")
        vg_done, vg_ready, w1_used, pab_ready, phid_ready, pkv_done, pkv_ready = map(
            sem, ("vg_done", "vg_ready", "w1_used", "pab_ready", "phid_ready", "pkv_done", "pkv_ready"))
        xtp_ready, psum_ready, kcp_zeroed = sem("xtp_ready"), sem("psum_ready"), sem("kcp_zeroed")
        qs_ready, ps_done, ps_read, pmax_ready, pexp_ready, pp_ready = map(
            sem, ("qs_ready", "ps_done", "ps_read", "pmax_ready", "pexp_ready", "pp_ready"))
        pt_done, pt_ready, po_done, prompt_done = map(sem, ("pt_done", "pt_ready", "po_done", "prompt_done"))
        cab_ready, hsum_ready, hid_ready, kvc_done, kvc_ready = map(
            sem, ("cab_ready", "hsum_ready", "hid_ready", "kvc_done", "kvc_ready"))
        qb_ready, vnew_done, vnew_ready, sc_done, cmax_ready, cexp_ready, cp_ready, imp_done = map(
            sem, ("qb_ready", "vnew_done", "vnew_ready", "sc_done", "cmax_ready", "cexp_ready", "cp_ready",
                  "imp_done"))
        smax_ready, sexp_ready, sp_ready, spt_done, spt_ready, so_done, seq_done = map(
            sem, ("smax_ready", "sexp_ready", "sp_ready", "spt_done", "spt_ready", "so_done", "seq_done"))
        wmax_ready, wexp_ready, slc_biased = map(sem, ("wmax_ready", "wexp_ready", "slc_biased"))
        win_stored = [sem("win_stored0"), sem("win_stored1")]
        conv_acc, conv_done, couts_ready, conv_stored = map(sem, ("conv_acc", "conv_done", "couts_ready", "conv_stored"))
        ba_done, ban_ready, gate_pre, gat_ready = map(sem, ("ba_done", "ban_ready", "gate_pre", "gat_ready"))
        cn_sq, cn_ss, cn_std, cn_rec, cn_bc, cn_ready = map(sem, ("cn_sq", "cn_ss", "cn_std", "cn_rec", "cn_bc",
                                                                  "cn_ready"))
        bex_ready, kv_done, vb_ready = map(sem, ("bex_ready", "kv_done", "vb_ready"))
        qs_done, qs_read = sem("qs_done"), sem("qs_read")
        ug_ready, gc_done, gc_ready, dexp_ready, kq_done, bm_ready, tr_done, tr_ready, trd_ready = map(
            sem, ("ug_ready", "gc_done", "gc_ready", "dexp_ready", "kq_done", "bm_ready", "tr_done",
                  "tr_ready", "trd_ready"))
        inv_pe, inv_act, inv_dve = [[sem(f"inv_{e}{x}") for x in range(2)] for e in ("pe", "act", "dve")]
        wt_done, nwt_ready, vn_done, vn_ready, oc_done, oc_ready, sup_mm, sup_done = map(
            sem, ("wt_done", "nwt_ready", "vn_done", "vn_ready", "oc_done", "oc_ready", "sup_mm", "sup_done"))
        wm_ready, vx_ready, snew_mm, snew_ready, vns_done, vns_ready = map(
            sem, ("wm_ready", "vx_ready", "snew_mm", "snew_ready", "vns_done", "vns_ready"))

        GEMMS = [("mem", 4), ("nsa_in", 8), ("w1", 2), ("window", 1), ("out0", 4), ("up0", 16), ("down0", 16),
                 ("gdn_in", 14), ("out1", 4), ("up1", 16), ("down1", 16)]
        TILES = dict(mem=4, nsa_in=NSA_T, out0=8, up0=32, down0=8, gdn_in=GDN_T, out1=8, up1=32, down1=8)
        wbase, obase, src, free_at = {}, {}, [], []
        w = o = n_src = 0
        for name, n in GEMMS:
            wbase[name], obase[name] = w, o
            for j in range(n):
                src.append(None if name == "window" else n_src)
                n_src += name != "window"
                if name in ("w1", "window"):
                    free_at.append(name)
                elif name == "mem":
                    free_at.append(o + j + 1)
                elif name.startswith("down"):
                    free_at.append(o + j // 2 + 1)
                else:
                    free_at.append(o + min(2 * j + 2, TILES[name]))
            w += n
            o += TILES.get(name, 0)
        n_panels = w
        evac_base = dict(nsa_in=0, up0=NSA_T, gdn_in=NSA_T + 32, up1=NSA_T + 32 + GDN_T,
                         out0=0, down0=8, out1=16, down1=24)

        def panel_uses(slot, i):
            return i // 4 + 1 - (1 if slot == 2 and i > wbase["window"] else 0)

        ident, ones = C["ident"], C["ones"]
        block = ctx.enter_context(nc.Block())

        @block.sync
        def _(sp):
            sp.dma_start(common_ap, common_in).then_inc(in_common, 16)
            sp.dma_start(memT, mem_in).then_inc(in_mem, 16)

            def panel(i):
                slot = i % 4
                if i >= 4:
                    f = free_at[i - 4]
                    if f == "w1":
                        sp.wait_ge(w1_used, NS + 1)
                    elif f == "window":
                        sp.wait_ge(seq_done, NS)
                        for b in range(2):
                            sp.wait_ge(win_stored[b], 16 * (NS // 2))
                    else:
                        sp.wait_ge(pe_out, f)
                sp.dma_start(ring[slot], w_in[src[i]]).then_inc(in_panel[slot], 16)

            panel(0)
            sp.dma_start(xT, x_in).then_inc(in_x, 16)
            for i in range(1, 4):
                panel(i)
            sp.dma_start(pages_sb[:, :], table_in).then_inc(in_table, 16)
            for i in range(4, 14):
                panel(i)
                if i == 8:
                    sp.wait_ge(memn_ready, 2 * KT)
                    sp.wait_ge(mem_stored, 32)
                    sp.dma_start(mcache[0], mcache_in[0].rearrange("s p n -> p s n")).then_inc(in_mcache, 16)
            sp.wait_ge(in_table, 16)

            def sequence(s):
                at = [sp.value_load(pages_sb[0:1, s * NPAGE + p:s * NPAGE + p + 1], min_val=0, max_val=NPHYS - 1)
                      for p in range(NPAGE)]

                def pages(cols, landed):
                    for p in range(NPAGE):
                        sp.dma_start(page[s % 2][:, p, cols],
                                     pages_in[bass.ds(at[p], 1), :, cols].rearrange("a p n -> (a p) n"))\
                            .then_inc(landed[s % 2], 16)

                if s >= 2:
                    sp.wait_ge(w1_used, s)
                pages(slice(0, 2 * P), in_cmp)
                if s >= 2:
                    sp.wait_ge(seq_done, s - 1)
                pages(slice(2 * P, 4 * P), in_pages)
                if s == 0:
                    sp.wait_ge(pe_out, 4 + NSA_T)
                if s >= 2:
                    sp.wait_ge(win_stored[s % 2], 16 * (s // 2))
                sp.dma_start(wcache[s % 2], win_in[s]).then_inc(in_pages[s % 2], 16)

            sp.wait_ge(mix_mem, 5)
            sp.dma_start(prompt_ap, prompt_in).then_inc(in_prompt_t, 16)
            sequence(0)
            sp.wait_ge(prompt_done, 24)
            sp.dma_start(sample_ap, sample_in).then_inc(in_sample_t, 16)
            for s in range(1, NS):
                sequence(s)
            for i in range(15, wbase["gdn_in"] + 14):
                if i == 15:
                    sp.wait_ge(smax_ready, NS)
                panel(i)
                if i == wbase["gdn_in"] + 3:
                    sp.wait_ge(pe_out, obase["gdn_in"])
                    sp.wait_ge(dve_out, 16)
                    sp.dma_start(mcache[1], mcache_in[1].rearrange("s p n -> p s n")).then_inc(in_mcache, 16)
                    sp.dma_start(gdn_ap, gdn_in).then_inc(in_gdn_t, 16)
                    sp.dma_start(mkv[1], mem_out[1]).then_inc(in_mkv1, 16)
                    sp.dma_start(cbuf, conv_in).then_inc(in_conv, 16)
            for i in range(wbase["out1"], wbase["out1"] + 4):
                panel(i)
            for h in range(GH):
                if h == 0:
                    sp.wait_ge(conv_done, 19)
                    sp.wait_ge(mix_mem, 10)
                    sp.wait_ge(conv_stored, 32)
                if h >= 3:
                    sp.wait_ge(state_stored[h % 3], 16 * (h // 3))
                sp.dma_start(sg[h % 3], state_in[h]).then_inc(in_state[h % 3], 16)
            for i in range(wbase["up1"], n_panels):
                panel(i)

        @block.gpsimd
        def _(pool):
            for l in range(2):
                pool.wait_ge(memkv_ready, 2 * l + 2)
                pool.dma_start(mem_out[l], (mkv0, mkv1_tmp)[l]).then_inc(mem_stored, 16)
            pool.wait_ge(act_out, 12)
            pool.dma_start(kv_out, proj[:, CK:WV + 1, :]).then_inc(stored, 16)
            for s in range(NS):
                pool.wait_ge(in_pages[s % 2], 16 * (NPAGE + 1) * (s // 2 + 1))
                pool.dma_start(win_out[s], wcache[s % 2]).then_inc(win_stored[s % 2], 16)
            pool.wait_ge(conv_done, 19)
            pool.wait_ge(couts_ready, 1)
            pool.dma_start(conv_out_p, cout_p).then_inc(conv_stored, 16)
            pool.dma_start(conv_out_s, cout_s).then_inc(conv_stored, 16)
            pool.wait_ge(sup_done, 8)
            pool.dma_start(state_out_p, st_p).then_inc(stored, 16)
            for h in range(GH):
                pool.wait_ge(snew_ready, h + 1)
                pool.dma_start(state_out_s[h], sg[h % 3]).then_inc(state_stored[h % 3], 16)
            for k in range(KT):
                pool.wait_ge(h_ready, 4 * KT + k + 1)
                pool.dma_start(y_out[:, k, :], hT[:, k, :]).then_inc(stored, 16)
            pool.wait_ge(stored, 16 * (2 + KT))
            pool.wait_ge(mem_stored, 32)
            pool.wait_ge(conv_stored, 32)
            for b in range(2):
                pool.wait_ge(win_stored[b], 16 * (NS // 2))
            for b in range(3):
                pool.wait_ge(state_stored[b], 16 * (GH // 3))

        ident, ones = C["ident"], C["ones"]


        groups = lambda n: sum(m % 4 + 2 for m in range(n))

        def compress_prompt(pe):
            w1 = [view(ring[kind], 16, P) for kind in range(2)]
            pe.wait_ge(in_panel[0], 16 * panel_uses(0, wbase["w1"]))
            pe.wait_ge(in_panel[1], 16 * panel_uses(1, wbase["w1"] + 1))
            pe.wait_ge(xtp_ready, 1)
            for kind in range(2):
                for half in range(2):
                    at = CX * (2 * kind + half)
                    for lp in range(8):
                        last = pe.matmul(bank(7)[:, at:at + CX], w1[kind][:, 8 * half + lp, :], xtp[:, kind, lp, :],
                                         start=lp == 0, stop=lp == 7)
            last.then_inc(w1_used, 1)

        def chunks_of_prompt(dve):
            dve.wait_ge(act_out, CV + 1)
            for kind in range(2):
                for kv in range(NKV):
                    src_ = proj[64 * kv:64 * kv + 64, CK + kind, 0:TP].rearrange("p (c l two) -> p two l c", two=2, l=8)
                    for two in range(2):
                        dve.tensor_copy(xtp[64 * two:64 * two + 64, kind, :, 32 * kv:32 * kv + 32], src_[:, two, :, :])
                last = dve.tensor_copy(xtp[:, kind, :, 64:66],
                                       C["pe"][:, kind, :].rearrange("p (half l) -> p l half", half=2))
            last.then_inc(xtp_ready, 1)

        def block_sums_of_prompt(dve, own):
            dve.wait_ge(pab_ready, 1)
            own(dve.tensor_tensor(pebias, pab[:, :, 0, 64], pab[:, :, 1, 65], ALU.add))
            for kind in range(2):
                part = pab[:, kind, :, 0:64].rearrange("p h (k c) -> p h k c", k=2)
                dve.tensor_tensor(phid[:, kind, :, 0:NCP], part[:, 0, :, 0:NCP], part[:, 1, :, 1:NCP + 1], ALU.add)\
                    .then_inc(psum_ready, 1)

        def pe_nsa_prompt(pe):
            mm = pe.matmul
            pe.wait_ge(mix_mem, 5)
            for j in range(4):
                pe.transpose(bank(0)[:, 48 * j:48 * j + 36], proj[0:36, GT, P * j:P * (j + 1)], ident[0:36, 0:36])
            pe.transpose(bank(0)[0:TS, 192:228], proj[0:36, GT, TP:TT_], ident[0:36, 0:36])
            for br, tile in enumerate((SV, WV)):
                for j in range(4):
                    last = pe.transpose(bank(1 + br)[:, P * j:P * (j + 1)], proj[:, tile, P * j:P * (j + 1)], ident)
            last.then_inc(vg_done, 1)
            pe.wait_ge(phid_ready, 2)
            for kv in range(NKV):
                mm(bank(6)[64 * kv:64 * kv + 64, 0:NCP], C["w2"][:, 0, :], phid[:, 0, kv, 0:NCP], start=True, stop=True)
            for kv in range(NKV):
                last = mm(bank(7)[0:NCP, 64 * kv:64 * kv + 64], phid[:, 1, kv, 0:NCP], C["w2"][:, 1, :],
                          start=True, stop=True)
            last.then_inc(pkv_done, 1)
            pe.wait_ge(pkv_ready, 1)
            pe.wait_ge(kcp_zeroed, 1)
            pe.wait_ge(vg_ready, 1)

            def scores(n):
                g, qt = n // 4, n % 4
                pe.wait_ge(qs_ready, g + 1)
                if n:
                    pe.wait_ge(ps_read, n)
                nk = P * (qt + 1)
                for kv in range(NKV):
                    r = slice(64 * kv, 64 * kv + 64)
                    q = qs[r, g % 2, P * qt:P * (qt + 1)]
                    mm(bank(kv)[:, 0:nk], q, proj[r, SK, 0:nk], start=True, stop=True)
                    mm(bank(2 + kv)[:, 0:nk], q, proj[r, WK, 0:nk], start=True, stop=True)
                mm(bank(4)[:, 0:2 * NCP], qs[:, g % 2, P * qt:P * (qt + 1)], kcp, start=True, stop=True)\
                    .then_inc(ps_done, 1)

            def values(n):
                g, qt = n // 4, n % 4
                pe.wait_ge(pp_ready, n + 1)

                def turn(q):
                    pt = bank(5 + (groups(n) + q) % 2)
                    if groups(n) + q > 1:
                        pe.wait_ge(pt_ready, groups(n) + q - 1)
                    if q <= qt:
                        for r in range(4):
                            last = pe.transpose(pt[:, P * r:P * (r + 1)], s_sb[n % 3][:, r, P * q:P * (q + 1)], ident)
                    else:
                        for kv in range(NKV):
                            last = pe.transpose(pt[0:NCP, P * kv:P * (kv + 1)], scp[n % 3][:, kv, 0:NCP], ident)
                    last.then_inc(pt_done, 1)

                turn(0)
                if n:
                    pe.wait_ge(prompt_done, n)
                for q in range(qt + 2):
                    if q <= qt:
                        turn(q + 1)
                    pe.wait_ge(pt_ready, groups(n) + q + 1)
                    for kv in range(NKV):
                        o = bank(7)[64 * kv:64 * kv + 64, 0:P]
                        if q <= qt:
                            for br in range(2):
                                mm(o, vn[:, br, q, 64 * kv:64 * kv + 64], ptp[(groups(n) + q) % 3][:, 2 * br + kv, :],
                                   start=q == br == 0, stop=False)
                        else:
                            last = mm(o, vcp[:, 64 * kv:64 * kv + 64], ptc[:, kv, :], start=False, stop=True)
                last.then_inc(po_done, 1)

            scores(0)
            scores(1)
            for n in range(24):
                if n < 22:
                    scores(n + 2)
                values(n)

        def act_nsa_prompt(act, own):
            f = act.activation
            act.wait_ge(vg_done, 1)
            f(gnat, view(bank(0)[:, 0:192], 4, 48)[:, :, 0:36], ACT.Sigmoid)
            f(gsamp, bank(0)[0:TS, 192:228], ACT.Sigmoid)
            for br in range(2):
                last = f(vn[:, br, :, :].rearrange("p j c -> p (j c)"), bank(1 + br), ACT.Copy)
            last.then_inc(vg_ready, 1)
            for kind in range(2):
                act.wait_ge(psum_ready, kind + 1)
                f(phid[:, kind, :, 0:NCP], phid[:, kind, :, 0:NCP], ACT.Silu, bias=pebias[:, kind:kind + 1])\
                    .then_inc(phid_ready, 1)
            act.wait_ge(pkv_done, 1)
            act.wait_ge(kcp_zeroed, 1)
            for kv in range(NKV):
                r = slice(64 * kv, 64 * kv + 64)
                f(kcp[r, kv, :], bank(6)[r, 0:NCP], ACT.Copy)
            f(vcp, bank(7)[0:NCP, 0:P], ACT.Copy).then_inc(pkv_ready, 1)

            def queries(g):
                if g >= 2:
                    act.wait_ge(ps_done, 4 * (g - 1))
                f(qs[:, g % 2, :], proj[:, Q0 + g, 0:TP], ACT.Copy, scale=HD ** -0.5).then_inc(qs_ready, 1)

            def exps(n, rows):
                nk, st = P * (n % 4 + 1), stp[:, n % 3, :]
                act.wait_ge(pmax_ready, n + 1)
                for r in rows:
                    f(s_sb[n % 3][:, r, 0:nk], s_sb[n % 3][:, r, 0:nk], ACT.Exp, bias=st[:, r:r + 1],
                      accum_out=st[:, 8 + r:9 + r])
                for kv in range(NKV if 3 in rows else 0):
                    last = f(scp[n % 3][:, kv, 0:NCP], scp[n % 3][:, kv, 0:NCP], ACT.Exp, bias=st[:, 4 + kv:5 + kv],
                             accum_out=st[:, 12 + kv:13 + kv])
                if 3 in rows:
                    last.then_inc(pexp_ready, 1)

            def turned(n, q):
                pt = bank(5 + (groups(n) + q) % 2)
                act.wait_ge(pt_done, groups(n) + q + 1)
                if q <= n % 4:
                    f(ptp[(groups(n) + q) % 3].rearrange("p r q -> p (r q)"), pt, ACT.Copy).then_inc(pt_ready, 1)
                else:
                    f(ptc.rearrange("p r q -> p (r q)"), pt[0:NCP, 0:2 * P], ACT.Copy).then_inc(pt_ready, 1)

            queries(0)
            queries(1)
            exps(0, range(4))
            for n in range(24):
                for q in range(n % 4 + 2):
                    turned(n, q)
                    if n < 23 and n % 4 == 0 and q == 1:
                        exps(n + 1, range(4))
                    elif n < 23 and q in (1, 2):
                        exps(n + 1, range(2 * q - 2, 2 * q))
                    if q == 1 and n % 4 == 2 and n // 4 + 2 < NG:
                        queries(n // 4 + 2)

        def dve_nsa_prompt(dve, own):
            tt, ts, stt = dve.tensor_tensor, dve.tensor_scalar, dve.scalar_tensor_tensor
            dve.memset(kcp, 0.0).then_inc(kcp_zeroed, 1)
            dve.wait_ge(in_prompt_t, 16)
            dve.wait_ge(vg_ready, 1)

            def biased(n):
                g, qt = n // 4, n % 4
                nk, st, s, sc = P * (qt + 1), stp[:, n % 3, :], s_sb[n % 3], scp[n % 3]
                dve.wait_ge(ps_done, n + 1)
                if n >= 3:
                    dve.wait_ge(pt_done, groups(n - 2))
                slope = lambda kv: PT["nslope"][:, 6 * kv + g:6 * kv + g + 1]
                for r in range(4):
                    stt(out=s[:, r, 0:nk], in0=PT["dist"][:, TP - nk:TP], scalar=slope(r % 2), in1=bank(r)[:, 0:nk],
                        op0=ALU.mult, op1=ALU.add)
                for kv in range(NKV):
                    last = stt(out=sc[:, kv, 0:NCP], in0=PT["cdist"][:, qt, :], scalar=slope(kv),
                               in1=bank(4)[:, NCP * kv:NCP * (kv + 1)], op0=ALU.mult, op1=ALU.add)
                last.then_inc(ps_read, 1)
                dve.wait_ge(ps_read, n + 1)
                dve.tensor_reduce(st[:, 0:4], s[:, :, 0:nk], AX.X, ALU.max, negate=True)
                dve.tensor_reduce(st[:, 4:6], sc[:, :, 0:NCP], AX.X, ALU.max, negate=True)\
                    .then_inc(pmax_ready, 1)

            def scaled(n):
                g, qt = n // 4, n % 4
                nk, st, s, sc = P * (qt + 1), stp[:, n % 3, :], s_sb[n % 3], scp[n % 3]
                dve.wait_ge(pexp_ready, n + 1)
                own(dve.reciprocal(st[:, 16:22], st[:, 8:14]))
                own(tt(st[:, 16:22], st[:, 16:22], gnat[:, qt, 6 * g:6 * g + 6], ALU.mult))
                own(ts(st[:, 20:22], st[:, 20:22], PT["cvis"][:, qt:qt + 1], None, ALU.mult))
                tt(s[:, :, 0:nk], s[:, :, 0:nk], bcast(st[:, 16:20], P, 4, nk), ALU.mult)
                tt(sc[:, :, 0:NCP], sc[:, :, 0:NCP], bcast(st[:, 20:22], P, 2, NCP), ALU.mult)\
                    .then_inc(pp_ready, 1)

            def output(n):
                dve.wait_ge(po_done, n + 1)
                dve.tensor_copy(mixT[:, n // 4, P * (n % 4):P * (n % 4 + 1)], bank(7)[:, 0:P]).then_inc(prompt_done, 1)

            biased(0)
            biased(1)
            scaled(0)
            for n in range(24):
                if n < 22:
                    biased(n + 2)
                if n < 23:
                    scaled(n + 1)
                output(n)

        def pe_nsa_sample(pe):
            mm = pe.matmul
            w1 = [view(ring[kind], 16, P) for kind in range(2)]

            def compress(s, quarters):
                if 0 in quarters:
                    pe.wait_ge(in_cmp[s % 2], 16 * NPAGE * (s // 2 + 1))
                    if s:
                        pe.wait_ge(vnew_ready, s)
                        pe.wait_ge(kvc_ready, s)
                    else:
                        pe.wait_ge(prompt_done, 24)
                for quarter in quarters:
                    kind, half = quarter // 2, quarter % 2
                    for lp in range(8):
                        last = mm(bank(6 + kind)[:, 2 * P * half:2 * P * (half + 1)], w1[kind][:, 8 * half + lp, :],
                                  page[s % 2][:, :, P * kind + 16 * lp:P * kind + 16 * lp + 16],
                                  start=lp == 0, stop=lp == 7)
                if 3 in quarters:
                    last.then_inc(w1_used, 1)

            def compressed(s):
                pe.wait_ge(hid_ready, s + 1)
                for kv in range(NKV):
                    mm(bank(6)[64 * kv:64 * kv + 64, 0:NCB], C["w2"][:, 0, :], chid[:, 0, kv, 0:NCB],
                       start=True, stop=True)
                for kv in range(NKV):
                    last = mm(bank(6)[0:NCB, P + 64 * kv:P + 64 * kv + 64], chid[:, 1, kv, 0:NCB], C["w2"][:, 1, :],
                              start=True, stop=True)
                last.then_inc(kvc_done, 1)

            def new_rows(s):
                pe.wait_ge(qb_ready, s + 1)
                pe.wait_ge(cab_ready, s + 1)
                for br in range(2):
                    pe.transpose(bank(7)[0:DT, P * br:P * (br + 1)], vst[:, br, :], ident)
                mm(bank(7)[0:ROWS, 256:292], ST["pick"][0:TS, s, :], gsamp, start=True, stop=True)\
                    .then_inc(vnew_done, 1)

            def scores(s):
                pe.wait_ge(kvc_ready, s + 1)
                pe.wait_ge(in_pages[s % 2], 16 * (NPAGE + 1) * (s // 2 + 1))
                if s:
                    pe.wait_ge(seq_done, s)
                pg, kn = page[s % 2], slice(TP + DT * s, TP + DT * (s + 1))
                for half in range(2):
                    for b in range(2):
                        j = 8 * half + 4 * b
                        mm(bank(b)[ROWS * half:ROWS * (half + 1), :], qb, pg[:, j:j + 4, 256:384], start=True, stop=True)
                mm(bank(4)[0:ROWS, :], qb, wcache[s % 2][:, 0:WIN], start=True, stop=True)
                mm(bank(5)[0:ROWS, 0:DT], qb, proj[:, SK, kn], start=True, stop=True)
                mm(bank(5)[0:ROWS, DT:2 * DT], qb, proj[:, WK, kn], start=True, stop=True)
                mm(bank(5)[0:ROWS, 16:16 + NCB], qb, kc[:, s % 2, 0:NCB], start=True, stop=True).then_inc(sc_done, 1)

            def importance(s):
                pe.wait_ge(cp_ready, s + 1)
                mm(bank(5)[:, 0:NCB], ST["same"][0:ROWS, :], low[:, S_CMP:S_CMP + NCB], start=True, stop=True)\
                    .then_inc(imp_done, 1)

            i64 = ident[0:ROWS, 0:ROWS]

            def turn_window(s):
                pe.wait_ge(slc_biased, s + 1)
                for j in range(4):
                    pe.transpose(bank(3)[:, ROWS * j:ROWS * (j + 1)], low[:, S_WIN + P * j:S_WIN + P * (j + 1)], i64)
                pe.transpose(bank(3)[0:DT, 4 * ROWS:5 * ROWS], low[:, S_WNEW:S_WNEW + DT], i64).then_inc(spt_done, 1)

            o = bank(0)[:, 0:ROWS]

            def window_values(s):
                pe.wait_ge(spt_ready, 4 * s + 1)
                for j in range(4):
                    mm(o, wcache[s % 2][:, WIN + P * j:WIN + P * (j + 1)], pts[:, 16 + j, :], start=j == 0, stop=False)
                mm(o, vnew[:, 1, :], ptn[:, 1, :], start=False, stop=False)

            def values(s):
                pe.wait_ge(sp_ready, s + 1)
                for b in range(2):
                    for j in range(4):
                        last = pe.transpose(bank(1 + b)[:, P * j:P * (j + 1)],
                                            ssc[:, P * (4 * b + j):P * (4 * b + j + 1)], ident)
                    last.then_inc(spt_done, 1)
                pe.transpose(bank(4)[0:NCB, 0:ROWS], low[:, S_CMP:S_CMP + NCB], i64)
                pe.transpose(bank(4)[0:DT, 64:128], low[:, S_NEW:S_NEW + DT], i64).then_inc(spt_done, 1)
                for j in range(8):
                    if j in (0, 4):
                        pe.wait_ge(spt_ready, 4 * s + j // 4 + 2)
                    for half in range(2):
                        mm(o, page[s % 2][:, 8 * half + j, 384:512], pts[:, 2 * j + half, :], start=False, stop=False)
                pe.wait_ge(spt_ready, 4 * s + 4)
                mm(o, vc[:, s % 2, :], ptcs, start=False, stop=False)
                mm(o, vnew[:, 0, :], ptn[:, 0, :], start=False, stop=True).then_inc(so_done, 1)

            compress(0, (0, 1, 2, 3))
            compressed(0)
            pe.wait_ge(in_sample_t, 16)
            for s in range(NS):
                more = s < NS - 1
                new_rows(s)
                scores(s)
                if more:
                    compress(s + 1, (0,))
                importance(s)
                if more:
                    compress(s + 1, (1,))
                turn_window(s)
                if more:
                    compress(s + 1, (2,))
                window_values(s)
                if more:
                    compress(s + 1, (3,))
                values(s)
                if more:
                    compressed(s + 1)

        def act_nsa_sample(act, own):
            f = act.activation

            def halves(s):
                act.wait_ge(w1_used, s + 2)
                for kind in range(2):
                    if s:
                        act.wait_ge(hsum_ready, 2 * s)
                    for half in range(2):
                        last = f(cab[:, kind, half, :].rearrange("p (k g c) -> p k g c", k=2, g=NPAGE),
                                 bank(6 + kind)[:, 2 * P * half:2 * P * (half + 1)]
                                 .rearrange("p (g k c) -> p k g c", k=2, g=NPAGE), ACT.Copy)
                last.then_inc(cab_ready, 1)

            def hidden(s):
                if s:
                    act.wait_ge(kvc_done, s)
                for kind in range(2):
                    act.wait_ge(hsum_ready, 2 * s + kind + 1)
                    last = f(chid[:, kind, :, 0:NCB],
                             cab[:, kind, 0, :].rearrange("p (k c) -> p k c", k=2)[:, :, 0:NCB], ACT.Silu,
                             bias=pebias[:, kind:kind + 1])
                last.then_inc(hid_ready, 1)
                act.wait_ge(kvc_done, s + 1)
                f(kc[:, s % 2, 0:NCB], bank(6)[:, 0:NCB], ACT.Copy)
                f(vc[:, s % 2, :], bank(6)[0:NCB, P:2 * P], ACT.Copy).then_inc(kvc_ready, 1)

            halves(0)
            hidden(0)
            for s in range(NS):
                act.wait_ge(vnew_done, s + 1)
                if s:
                    act.wait_ge(seq_done, s)
                f(vnew.rearrange("p b c -> p (b c)"), bank(7)[0:DT, 0:2 * P], ACT.Copy)
                f(grt, bank(7)[0:ROWS, 256:292], ACT.Copy).then_inc(vnew_ready, 1)
                act.wait_ge(cmax_ready, s + 1)
                cmp_ = low[:, S_CMP:S_CMP + NCB]
                f(cmp_, cmp_, ACT.Exp, bias=stl[:, 0:1], accum_out=stl[:, 1:2]).then_inc(cexp_ready, 1)
                w = low[:, S_WIN:S_WIN + WIN + DT]
                act.wait_ge(wmax_ready, s + 1)
                f(w, w, ACT.Exp, bias=stl[:, 4:5], accum_out=stl[:, 6:7]).then_inc(wexp_ready, 1)
                act.wait_ge(spt_done, 4 * s + 1)
                f(pts[:, 16:20, :].rearrange("p j r -> p (j r)"), bank(3)[:, 0:4 * ROWS], ACT.Copy)
                f(ptn[:, 1, :], bank(3)[0:DT, 4 * ROWS:5 * ROWS], ACT.Copy).then_inc(spt_ready, 1)
                act.wait_ge(smax_ready, s + 1)
                f(ssc[:, 0:PAST2 + DT], ssc[:, 0:PAST2 + DT], ACT.Exp, bias=sst[:, 3:4], accum_out=sst[:, 5:6])\
                    .then_inc(sexp_ready, 1)
                if s < NS - 1:
                    halves(s + 1)
                for b in range(2):
                    act.wait_ge(spt_done, 4 * s + b + 2)
                    f(pts[:, 8 * b:8 * b + 8, :].rearrange("p j r -> p (j r)"), bank(1 + b), ACT.Copy)\
                        .then_inc(spt_ready, 1)
                act.wait_ge(spt_done, 4 * s + 4)
                f(ptcs, bank(4)[0:NCB, 0:ROWS], ACT.Copy)
                f(ptn[:, 0, :], bank(4)[0:DT, 64:128], ACT.Copy).then_inc(spt_ready, 1)
                if s < NS - 1:
                    hidden(s + 1)

        def dve_nsa_sample(dve, own):
            tt, ts = dve.tensor_tensor, dve.tensor_scalar
            own(dve.memset(qb, 0.0))

            def queries(s):
                if s:
                    dve.wait_ge(sc_done, s)
                kn = slice(TP + DT * s, TP + DT * (s + 1))
                for kv in range(NKV):
                    r = slice(64 * kv, 64 * kv + 64)
                    ts(qb[r, 32 * kv:32 * kv + 24].rearrange("p (g t) -> p g t", g=NG), proj[r, Q0:Q0 + NG, kn],
                       HD ** -0.5, None, ALU.mult)
                dve.tensor_copy(vst[:, 0, :], proj[:, SV, kn])
                dve.tensor_copy(vst[:, 1, :], proj[:, WV, kn]).then_inc(qb_ready, 1)

            def half_sum(s):
                dve.wait_ge(cab_ready, s + 1)
                for kind in range(2):
                    h = [cab[:, kind, i, :].rearrange("p (k c) -> p k c", k=2) for i in range(2)]
                    tt(h[0][:, :, 0:NCB], h[0][:, :, 0:NCB], h[1][:, :, 1:NCB + 1], ALU.add).then_inc(hsum_ready, 1)

            queries(0)
            half_sum(0)
            for s in range(NS):
                if s == 0:
                    dve.wait_ge(in_sample_t, 16)
                cmp_ = low[:, S_CMP:S_CMP + NCB]
                dve.wait_ge(sc_done, s + 1)
                own(tt(cmp_, bank(5)[0:ROWS, 16:16 + NCB], ST["b_cmp"][0:ROWS, :], ALU.add))
                dve.tensor_reduce(stl[:, 0:1], cmp_, AX.X, ALU.max, negate=True).then_inc(cmax_ready, 1)
                win = low[:, S_WIN:S_WIN + WIN + DT]
                tt(low[:, S_NEW:S_NEW + DT], bank(5)[0:ROWS, 0:DT], ST["b_new"][0:ROWS, :], ALU.add)
                dve.tensor_copy(high[:, S_NEW:S_NEW + DT], ST["b_new"][ROWS:P, :])
                tt(low[:, S_WNEW:S_WNEW + DT], bank(5)[0:ROWS, DT:2 * DT], ST["b_new"][0:ROWS, :], ALU.add)
                own(tt(win[:, 0:WIN], bank(4)[0:ROWS, :], ST["b_win"][0:ROWS, :], ALU.add))
                dve.tensor_reduce(stl[:, 4:5], win, AX.X, ALU.max, negate=True).then_inc(wmax_ready, 1)
                dve.wait_ge(cexp_ready, s + 1)
                own(dve.reciprocal(stl[:, 2:3], stl[:, 1:2]))
                ts(cmp_, cmp_, stl[:, 2:3], None, ALU.mult).then_inc(cp_ready, 1)
                dve.wait_ge(vnew_ready, s + 1)
                own(tt(grt, grt, ST["head"][0:ROWS, :], ALU.mult))
                own(dve.tensor_reduce(gr, grt.rearrange("p (g b k) -> p b g k", g=NG, b=3), AX.XY, ALU.add))
                dve.wait_ge(wexp_ready, s + 1)
                own(dve.reciprocal(stl[:, 9:10], stl[:, 6:7]))
                own(tt(stl[:, 9:10], stl[:, 9:10], gr[:, 1:2], ALU.mult))
                ts(win, win, stl[:, 9:10], None, ALU.mult)
                tt(ssc[:, 0:PAST2], banks(0, 2), ST["b_slc"], ALU.add).then_inc(slc_biased, 1)
                if s < NS - 1:
                    queries(s + 1)
                dve.wait_ge(imp_done, s + 1)
                dve.memset(impc[:, NCB:P], 0.0)
                own(dve.tensor_copy(impc[:, 0:NCB], bank(5)[:, 0:NCB]))
                own(dve.tensor_reduce(imp, view(impc, NSLC, 4), AX.X, ALU.add))
                own(tt(imp[:, 1:NSLC], imp[:, 1:NSLC], view(impc, NSLC, 4)[:, 0:NSLC - 1, 3], ALU.add))
                dve.tensor_copy(imph[0:ROWS, :], imp[0:ROWS, 0:NSLC // 2])
                own(dve.tensor_copy(imph[ROWS:P, :], imp[ROWS:P, NSLC // 2:NSLC]))
                c, m = NSLC - 2, NSLC // 2
                gt, eq = view(rank[:, 0:m * c], m, c), view(rank[:, m * c:2 * m * c], m, c)
                each, other = bcast(imph, P, m, c), imp[:, 1:1 + c].unsqueeze(1).to_broadcast([P, m, c])
                tt(gt, other, each, ALU.is_gt)
                own(tt(eq, other, each, ALU.is_equal))
                own(tt(eq, eq, ST["lower"], ALU.mult))
                own(tt(gt, gt, eq, ALU.add))
                own(dve.tensor_reduce(sel, gt, AX.X, ALU.add))
                own(ts(sel, sel, float(TOPN - 3), None, ALU.is_ge))
                own(tt(sel, sel, ST["drop"], ALU.mult))
                past = view(ssc[:, 0:PAST2], m, 64)
                own(tt(past, past, bcast(sel, P, m, 64), ALU.add))
                own(dve.tensor_reduce(sst[:, 3:4], ssc[:, 0:PAST2 + DT], AX.X, ALU.max, negate=True))
                own(dve.tensor_copy(stl[:, 7:8], sst[ROWS:P, 3:4]))
                own(tt(stl[:, 3:4], stl[:, 3:4], stl[:, 7:8], ALU.min))
                dve.tensor_copy(sst[ROWS:P, 3:4], stl[:, 3:4]).then_inc(smax_ready, 1)
                ts(cmp_, cmp_, gr[:, 2:3], None, ALU.mult)
                dve.wait_ge(sexp_ready, s + 1)
                own(dve.tensor_copy(stl[:, 7:8], sst[ROWS:P, 5:6]))
                own(tt(stl[:, 7:8], stl[:, 7:8], stl[:, 5:6], ALU.add))
                own(dve.reciprocal(stl[:, 8:9], stl[:, 7:8]))
                own(tt(stl[:, 8:9], stl[:, 8:9], gr[:, 0:1], ALU.mult))
                own(dve.tensor_copy(sst[ROWS:P, 8:9], stl[:, 8:9]))
                ts(ssc[:, 0:PAST2 + DT], ssc[:, 0:PAST2 + DT], sst[:, 8:9], None, ALU.mult).then_inc(sp_ready, 1)
                if s < NS - 1:
                    half_sum(s + 1)
                dve.wait_ge(so_done, s + 1)
                for kv in range(NKV):
                    r = slice(64 * kv, 64 * kv + 64)
                    last = dve.tensor_copy(mixT[r, 0:NG, TP + DT * s:TP + DT * (s + 1)],
                                           bank(0)[r, 32 * kv:32 * kv + 24].rearrange("p (g t) -> p g t", g=NG))
                last.then_inc(seq_done, 1)

        CHUNKS = [(P, slice(P * i, P * (i + 1)), 3, 3) for i in range(4)] + [(TS, slice(TP, TT_), 1, 0)]
        HALVES = ((0, 3), (3, 6))
        BA_, BB, BC, BD = (3, 4), (5, 6), (0, 1), (2, 7)

        class Inverse:

            def __init__(self):
                self.pe = self.act = self.dve = 0

        def row_sums(pe, first, tiles):
            for c in range(tiles):
                pe.wait_ge(cn_sq, first + c + 1)
                for half in range(2):
                    r = tiles * half + c
                    last = pe.matmul(bank(7)[0:2 * tiles, 0:HALF], C["onecol"][:, 23 - r:23 - r + 2 * tiles],
                                     halves_of(sq[:, c % 2, :])[:, half, :],
                                     start=r == 0, stop=r == 2 * tiles - 1, skip_group_check=True)
                last.then_inc(cn_ss, 1)

        def spread_rows(pe, first, tiles, turn):
            pe.wait_ge(cn_rec, turn)
            for c in range(tiles):
                if c >= 2:
                    pe.wait_ge(cn_ready, first + c - 1)
                for half in range(2):
                    r = tiles * half + c
                    last = pe.matmul(both(c % 2)[:, half, :], SPREAD(r, 2 * tiles), rinv[0:2 * tiles, :],
                                     start=True, stop=True)
                last.then_inc(cn_bc, 1)

        SPREAD = lambda r, rows: ident[0:rows, r:r + 1].to_broadcast([rows, P])

        def pe_gdn(pe):
            mm = pe.matmul
            n = [Inverse(), Inverse()]
            pe.wait_ge(mix_mem, 10)
            for j in range(4):
                pe.transpose(bank(6)[:, 16 * j:16 * j + 12], gproj[0:12, BA, P * j:P * (j + 1)], ident[0:12, 0:12])
            pe.transpose(bank(6)[0:TS, 64:76], gproj[0:12, BA, TP:TT_], ident[0:12, 0:12]).then_inc(ba_done, 1)
            spread_rows(pe, 0, 12, 1)
            pe.wait_ge(ban_ready, 1)
            pe.wait_ge(cn_ready, 12)
            for ci, (R, cols, squares, merges) in enumerate(CHUNKS):
                U, ALL = (GC["cum"], ones) if R == P else (GC["cum_s"], GC["all_s"])
                if ci:
                    pe.wait_ge(oc_ready, 2 * ci)
                    pe.wait_ge(sup_done, 2 * ci)
                pe.wait_ge(ug_ready, ci + 1)
                mm(bank(0)[0:R, 0:GH], U[0:R, 0:R], gat[0:R, ci, :], start=True, stop=True)
                mm(bank(0)[0:R, 8:8 + GH], ALL[0:R, 0:R], gat[0:R, ci, :], start=True, stop=True)
                for x, (h0, h1) in enumerate(HALVES):
                    last = mm(bank(1 + x)[:, 0:R * (h1 - h0)], ones[0:R, :], ug[0:R, h0:h1, 0:R], start=True, stop=True)
                last.then_inc(gc_done, 1)

                def product(x, pair, lhs, rhs, width, rows=P):
                    h0, h1 = HALVES[x]
                    for h in range(h0, h1):
                        last = mm(bank(pair[x])[0:rows, width * (h - h0):width * (h - h0 + 1)], lhs(h), rhs(h),
                                  start=True, stop=True)
                    return last

                kT = lambda h: gproj[:, GK + h, cols]
                qT = lambda h: gproj[:, GQ + h, cols]
                for x in range(2):
                    product(x, BA_, kT, kT, R, R)
                    last = product(x, BB, qT, kT, R, R)
                last.then_inc(kq_done, 1)
                pe.wait_ge(dexp_ready, ci + 1)
                for x, (h0, h1) in enumerate(HALVES):
                    for h in range(h0, h1):
                        y = slice(P * (h - h0), P * (h - h0 + 1))
                        pe.transpose(bank(BC[x])[0:R, y], kT(h), ident)
                        last = pe.transpose(bank(BD[x])[0:R, y], gproj[:, GV + h, cols], ident)
                last.then_inc(kv_done, 1)
                pe.wait_ge(bm_ready, ci + 1)
                for x, (h0, h1) in enumerate(HALVES):
                    for h in range(h0, h1):
                        y = slice(R * (h - h0), R * (h - h0 + 1))
                        pe.transpose(bank(BA_[x])[0:R, y], bm[0:R, h, 0:R], ident[0:R, 0:R])
                        last = pe.transpose(bank(BB[x])[0:R, y], qd[0:R, h, 0:R], ident[0:R, 0:R])
                    last.then_inc(tr_done, 1)
                sub = lambda t: (lambda h: t[0:R, h, 0:R])
                for x in range(2):
                    n[x].dve += 1
                for k in range(squares):
                    for x in range(2):
                        pe.wait_ge(inv_dve[x], n[x].dve)
                        product(x, BA_, sub(pwt), sub(pw), R, R).then_inc(inv_pe[x], 1)
                        if k < squares - 1:
                            product(x, BB, sub(pw), sub(pwt), R, R).then_inc(inv_pe[x], 1)
                    for x in range(2):
                        n[x].act += 1
                        n[x].dve += 1
                        if not k:
                            pe.wait_ge(tr_ready, 2 * ci + x + 1)
                        pe.wait_ge(inv_act[x], n[x].act)
                        product(x, BC, sub(pw), sub(tt_), R, R).then_inc(inv_pe[x], 1)
                for x in range(2 if merges else 0):
                    pe.wait_ge(inv_dve[x], n[x].dve)
                    h0, h1 = HALVES[x]
                    for h in range(h0, h1):
                        last = pe.transpose(bank(BB[x])[:, P * (h - h0):P * (h - h0 + 1)], tt_[:, h, :], ident)
                    last.then_inc(inv_pe[x], 1)
                    n[x].act += 1
                for k in range(merges):
                    for x in range(2):
                        if k:
                            pe.wait_ge(inv_dve[x], n[x].dve)
                        product(x, BA_, sub(pw), sub(tt_), R, R).then_inc(inv_pe[x], 1)
                    for x in range(2):
                        n[x].act += 1
                        pe.wait_ge(inv_act[x], n[x].act)
                        if k:
                            n[x].dve += 1
                            pe.wait_ge(inv_dve[x], n[x].dve)
                        last = product(x, BC, sub(tn), sub(zz), R, R)
                        if k < merges - 1:
                            last = product(x, BB, sub(zz), sub(tn), R, R)
                        last.then_inc(inv_pe[x], 1)
                        n[x].dve += 1
                for x in range(2):
                    pe.wait_ge(inv_dve[x], n[x].dve)
                    pe.wait_ge(vb_ready, 2 * ci + x + 1)
                    product(x, BD, lambda h: kbg[0:R, h, :], sub(tt_), R).then_inc(wt_done, 1)
                if R == P:
                    for x, (h0, h1) in enumerate(HALVES):
                        pe.wait_ge(nwt_ready, 2 * ci + x + 1)
                        for h in range(h0, h1):
                            o = bank(BA_[x])[:, P * (h - h0):P * (h - h0 + 1)]
                            mm(o, tt_[:, h, :], vb[:, h, :], start=True, stop=False)
                            last = mm(o, nwt[:, h, :], st_p[:, h, :], start=False, stop=True)
                        last.then_inc(vn_done, 1)
                    for x, (h0, h1) in enumerate(HALVES):
                        pe.wait_ge(vn_ready, 2 * ci + x + 1)
                        for h in range(h0, h1):
                            o = bank(BB[x])[:, P * (h - h0):P * (h - h0 + 1)]
                            mm(o, st_p[:, h, :], qg[:, h, :], start=True, stop=False)
                            last = mm(o, vnw[:, h, :], qt_[:, h, :], start=False, stop=True)
                        last.then_inc(oc_done, 1)
                        product(x, BC, lambda h: kdec[:, h, :], lambda h: vnw[:, h, :], P).then_inc(sup_mm, 1)
                    continue
                pe.wait_ge(wm_ready, 1)
                pe.wait_ge(nwt_ready, 2 * ci + 2)

                def from_state(h):
                    s0 = sg[h % 3]
                    pe.wait_ge(in_state[h % 3], 16 * (h // 3 + 1))
                    v = bank(3 + h % 2)[0:R, 0:P]
                    mm(v, tt_[0:R, h, 0:R], vb[0:R, h, :], start=True, stop=False)
                    for s in range(NS):
                        last = mm(v, wm[:, h, TS * s:TS * (s + 1)], s0[:, s, :], start=False, stop=s == NS - 1)
                    last.then_inc(vns_done, 1)
                    o = bank(5)[:, TS * h:TS * (h + 1)]
                    for s in range(NS):
                        last = mm(o[:, DT * s:DT * (s + 1)], s0[:, s, :], qg[:, h, DT * s:DT * (s + 1)], start=True,
                                  stop=True)
                    last.then_inc(qs_done, 1)

                def from_new_values(h):
                    pe.wait_ge(vns_ready, h + 1)
                    last = mm(bank(2)[:, TS * h:TS * (h + 1)], vnw[0:R, h, :], qt_[0:R, h, 0:R], start=True, stop=True)
                    if h == GH - 1:
                        last.then_inc(oc_done, 1)
                    pe.wait_ge(vx_ready, h + 1)
                    if h:
                        pe.wait_ge(snew_ready, h)
                    for b in range(2):
                        last = mm(bank(6 + b), kdec[0:R, h, :], vx[:, 4 * b:4 * b + 4, :], start=True, stop=True)
                    last.then_inc(snew_mm, 1)

                from_state(0)
                for h in range(GH):
                    if h + 1 < GH:
                        from_state(h + 1)
                    from_new_values(h)
            pe.wait_ge(oc_ready, 9)
            pe.wait_ge(snew_ready, GH)
            row_sums(pe, 12, 6)
            spread_rows(pe, 12, 6, 2)
            pe.wait_ge(cn_ready, 18)

        def column_squares(act, first, tiles, src_):
            for c in range(tiles):
                if c >= 2:
                    act.wait_ge(cn_ss, first + c - 1)
                act.activation(sq[:, c % 2, :], src_(c), ACT.Square).then_inc(cn_sq, 1)

        def row_roots(act, first, tiles, scale):
            act.wait_ge(cn_ss, first + tiles)
            act.activation(rinv[0:2 * tiles, :], bank(7)[0:2 * tiles, 0:HALF], ACT.Sqrt,
                           bias=C["eps"][0:2 * tiles, :], scale=scale).then_inc(cn_std, 1)

        def act_gdn(act, own):
            f = act.activation
            n = [Inverse(), Inverse()]
            act.wait_ge(gate_pre, 1)
            f(beta, ban[:, :, 0:GH], ACT.Sigmoid)
            own(f(nea, C["a_log"], ACT.Exp))
            own(f(spl, spl, ACT.Exp, scale=-1.0))
            f(spl, spl, ACT.Ln, bias=C["one"]).then_inc(gat_ready, 1)
            for ci, (R, cols, squares, merges) in enumerate(CHUNKS):
                act.wait_ge(gc_ready, ci + 1)
                f(dec[0:R, :, 0:R], dec[0:R, :, 0:R], ACT.Exp, scale=-1.0)
                f(kde[0:R, :], kde[0:R, :], ACT.Exp)
                f(egc[0:R, :], gcn[0:R, 0, 0:GH], ACT.Exp)
                for x, (h0, h1) in enumerate(HALVES):
                    last = f(egr[:, h0:h1, 0:R], view(bank(1 + x)[:, 0:R * (h1 - h0)], h1 - h0, R), ACT.Exp)
                last.then_inc(dexp_ready, 1)
                act.wait_ge(kv_done, ci + 1)
                act.wait_ge(bex_ready, ci + 1)
                act.wait_ge(dexp_ready, ci + 1)
                for x, (h0, h1) in enumerate(HALVES):
                    for h in range(h0, h1):
                        y = bank(BC[x])[0:R, P * (h - h0):P * (h - h0 + 1)]
                        f(kbg[0:R, h, :], y, ACT.Copy, scale=bex[0:R, h:h + 1])
                        last = f(kdec[0:R, h, :], y, ACT.Copy, scale=kde[0:R, h:h + 1])
                    last.then_inc(tr_ready, 1)

                def out(x, dst, pair, width, rows=P, scale=1.0):
                    h0, h1 = HALVES[x]
                    return f(dst[0:rows, h0:h1, 0:width], view(bank(pair[x])[0:rows, 0:width * (h1 - h0)], h1 - h0, width),
                             ACT.Copy, scale=scale)

                for k in range(squares):
                    for x in range(2):
                        n[x].pe += 1 if k == squares - 1 else 2
                        act.wait_ge(inv_pe[x], n[x].pe)
                        out(x, pw, BA_, R, R).then_inc(inv_act[x], 1)
                        n[x].pe += 1
                for x in range(2 if merges else 0):
                    n[x].pe += 1
                    act.wait_ge(inv_pe[x], n[x].pe)
                    out(x, tn, BB, R, R).then_inc(inv_act[x], 1)
                for k in range(merges):
                    for x in range(2):
                        n[x].pe += 1
                        act.wait_ge(inv_pe[x], n[x].pe)
                        out(x, zz, BA_, R, R).then_inc(inv_act[x], 1)
                        n[x].pe += 1
                for x in range(2):
                    act.wait_ge(wt_done, 2 * ci + x + 1)
                    out(x, nwt, BD, R, scale=-1.0).then_inc(nwt_ready, 1)
                if R == P:
                    for x in range(2):
                        act.wait_ge(vn_done, 2 * ci + x + 1)
                        out(x, vnw, BA_, P).then_inc(vn_ready, 1)
                    for x in range(2):
                        act.wait_ge(oc_done, 2 * ci + x + 1)
                        out(x, mixT[:, :, cols], BB, P).then_inc(oc_ready, 1)
                    continue
                for h in range(GH):
                    act.wait_ge(vns_done, h + 1)
                    f(vnw[0:R, h, :], bank(3 + h % 2)[0:R, 0:P], ACT.Copy).then_inc(vns_ready, 1)
                act.wait_ge(qs_done, GH)
                f(mixT[:, 0:GH, cols], view(bank(5)[:, 0:GH * TS], GH, TS), ACT.Copy).then_inc(qs_read, 1)
            act.wait_ge(oc_ready, 9)
            column_squares(act, 12, 6, lambda c: mixT[:, c, :])
            row_roots(act, 12, 6, 1.0 / P)

        def dve_convolution(dve, own):
            tt, ts, stt = dve.tensor_tensor, dve.tensor_scalar, dve.scalar_tensor_tensor
            w = C["conv_w"]
            done = evac_base["gdn_in"]
            for c in range(18):
                x, acc = gproj[:, c, 0:TP], cacc[:, c % 2, :]
                dve.wait_ge(act_out, done + c + 1)
                if c >= 2:
                    dve.wait_ge(conv_done, c - 1)
                dve.tensor_copy(cout_p[:, c, :], gproj[:, c, TP - 3:TP])
                own(ts(acc, x, w[:, c, 3:4], None, ALU.mult))
                for i in range(1, 4):
                    last = stt(out=acc[:, i:TP], in0=x[:, 0:TP - i], scalar=w[:, c, 3 - i:4 - i], in1=acc[:, i:TP],
                               op0=ALU.mult, op1=ALU.add)
                    if i < 3:
                        own(last)
                last.then_inc(conv_acc, 1)
            dve.wait_ge(in_conv, 16)
            new = gproj[:, 0:18, TP:TT_].rearrange("p c (s t) -> p c s t", s=NS)
            dve.tensor_copy(cout_s, new[:, :, :, 1:DT]).then_inc(couts_ready, 1)
            wi = lambda i, n: bcast(w[:, :, i], P, 18, NS, n)
            tt(sacc, new, wi(3, DT), ALU.mult)
            for d in range(1, 4):
                tt(stmp[:, :, :, d:DT], new[:, :, :, 0:DT - d], wi(3 - d, DT - d), ALU.mult)
                own(tt(stmp[:, :, :, 0:d], cbuf[:, :, :, 3 - d:3], wi(3 - d, d), ALU.mult))
                last = tt(sacc, sacc, stmp, ALU.add)
                if d < 3:
                    own(last)
            last.then_inc(conv_acc, 1)

        def row_reciprocals(dve, rows, turn):
            dve.wait_ge(cn_std, turn)
            dve.reciprocal(rinv[0:rows, :], rinv[0:rows, :]).then_inc(cn_rec, 1)

        def dve_gdn(dve, own):
            tt, ts, stt = dve.tensor_tensor, dve.tensor_scalar, dve.scalar_tensor_tensor
            n = [Inverse(), Inverse()]
            own(dve.memset(ban, 0.0))
            dve.wait_ge(ba_done, 1)
            dve.tensor_copy(ban[:, 0:4, :], view(bank(6)[:, 0:64], 4, 16)[:, :, 0:12])
            own(dve.tensor_copy(ban[0:TS, 4, :], bank(6)[0:TS, 64:76]))
            a_ = ban[:, :, GH:2 * GH]
            own(tt(a_, a_, C["dt_bias"].unsqueeze(1).to_broadcast([P, 5, GH]), ALU.add))
            own(ts(gat, a_, 0.0, None, ALU.max))
            stt(out=spl, in0=a_, scalar=-1.0, in1=a_, op0=ALU.mult, op1=ALU.max).then_inc(gate_pre, 1)
            dve.wait_ge(gate_pre, 1)
            dve.tensor_copy(sst1, C["one"]).then_inc(ban_ready, 1)

            for c in range(12):
                dve.wait_ge(cn_bc, c + 1)
                x = halves_of(gproj[:, c, :])
                stt(out=x, in0=x, scalar=P ** -0.5 if c < GK else 1.0, in1=both(c % 2), op0=ALU.mult,
                    op1=ALU.mult).then_inc(cn_ready, 1)
            dve.wait_ge(gat_ready, 1)
            own(tt(gat, gat, spl, ALU.add))
            own(stt(out=gat, in0=gat, scalar=-1.0, in1=nea.unsqueeze(1).to_broadcast([P, 5, GH]), op0=ALU.mult,
                    op1=ALU.mult))
            dve.wait_ge(cn_ready, 12)
            dve.wait_ge(in_gdn_t, 16)
            dve.wait_ge(conv_stored, 32)
            own(dve.memset(st_p, 0.0))
            own(dve.memset(wm, 0.0))
            for ci, (R, cols, squares, merges) in enumerate(CHUNKS):
                U, MASK, STRICT = (GC["cum"], GC["mask"], GC["strict"]) if R == P else \
                    (GC["cum_s"], GC["mask_s"], GC["strict_s"])
                heads = lambda t, k=GH: t[0:R, 0:R].unsqueeze(1).to_broadcast([R, k, R])
                bt, sub = beta[0:R, ci, :], (lambda t: t[0:R, :, 0:R])
                half = lambda t, x: t[0:R, HALVES[x][0]:HALVES[x][1], 0:R]
                from_bank = lambda pair, x, width=R: view(bank(pair[x])[0:R, 0:3 * width], 3, width)
                tt(sub(ug), heads(U), bcast(gat[0:R, ci, :], R, GH, R), ALU.mult).then_inc(ug_ready, 1)
                dve.wait_ge(gc_done, ci + 1)
                own(dve.tensor_copy(gcn[0:R, :, 0:GH], view(bank(0)[0:R, 0:16], 2, 8)[:, :, 0:GH]))
                tt(kde[0:R, :], gcn[0:R, 1, 0:GH], gcn[0:R, 0, 0:GH], ALU.subtract)
                for x, (h0, h1) in enumerate(HALVES):
                    for h in range(h0, h1):
                        last = stt(out=dec[0:R, h, 0:R], in0=bank(1 + x)[0:R, R * (h - h0):R * (h - h0 + 1)],
                                   scalar=gcn[0:R, 0, h:h + 1], in1=MASK[0:R, 0:R], op0=ALU.subtract, op1=ALU.subtract)
                last.then_inc(gc_ready, 1)
                dve.wait_ge(dexp_ready, ci + 1)
                tt(bex[0:R, :], bt, egc[0:R, :], ALU.mult).then_inc(bex_ready, 1)
                dve.wait_ge(kq_done, ci + 1)
                for x, (h0, h1) in enumerate(HALVES):
                    for h in range(h0, h1):
                        last = stt(out=bm[0:R, h, 0:R], in0=bank(BA_[x])[0:R, R * (h - h0):R * (h - h0 + 1)],
                                   scalar=bt[:, h:h + 1], in1=dec[0:R, h, 0:R], op0=ALU.mult, op1=ALU.mult)
                    tt(half(qd, x), from_bank(BB, x), half(dec, x), ALU.mult)
                own(last)
                tt(sub(bm), sub(bm), heads(STRICT), ALU.mult).then_inc(bm_ready, 1)
                tt(qg[:, :, 0:R], gproj[:, GQ:GQ + GH, cols], egr[:, :, 0:R], ALU.mult)
                dve.wait_ge(kv_done, ci + 1)
                for x, (h0, h1) in enumerate(HALVES):
                    for h in range(h0, h1):
                        last = ts(vb[0:R, h, :], bank(BD[x])[0:R, P * (h - h0):P * (h - h0 + 1)], bt[:, h:h + 1],
                                  None, ALU.mult)
                    last.then_inc(vb_ready, 1)
                dve.wait_ge(bm_ready, ci + 1)
                for x in range(2):
                    dve.wait_ge(tr_done, 2 * ci + x + 1)
                    own(tt(half(pwt, x), from_bank(BA_, x), heads(GC["diag"], 3), ALU.mult))
                    tt(half(pw, x), half(bm, x), heads(GC["diag"], 3), ALU.mult)
                    dve.tensor_copy(half(qt_, x), from_bank(BB, x))
                    tt(half(tt_, x), half(pwt, x), heads(ident, 3), ALU.add).then_inc(inv_dve[x], 1)
                    n[x].dve += 1

                def add(t, pair, x):
                    return tt(half(t, x), half(t, x), from_bank(pair, x), ALU.add)

                for k in range(squares):
                    if k < squares - 1:
                        for x in range(2):
                            n[x].pe += 2
                            dve.wait_ge(inv_pe[x], n[x].pe)
                            dve.tensor_copy(half(pwt, x), from_bank(BB, x))
                    for x in range(2):
                        n[x].pe += 1 if k < squares - 1 else 2
                        dve.wait_ge(inv_pe[x], n[x].pe)
                        dve.wait_ge(inv_dve[x], n[x].dve)
                        if k == squares - 1 and merges:
                            tt(half(pw, x), half(bm, x), heads(GC["off"][:, 0, :], 3), ALU.mult)
                        add(tt_, BC, x).then_inc(inv_dve[x], 1)
                        n[x].dve += 1
                for k in range(merges):
                    for x in range(2):
                        n[x].pe += 2 if k else 3
                        dve.wait_ge(inv_pe[x], n[x].pe)
                        dve.wait_ge(inv_dve[x], n[x].dve)
                        if k < merges - 1:
                            tt(half(pw, x), half(bm, x), heads(GC["off"][:, k + 1, :], 3), ALU.mult)
                        add(tt_, BC, x).then_inc(inv_dve[x], 1)
                        n[x].dve += 1
                        if k < merges - 1:
                            add(tn, BB, x).then_inc(inv_dve[x], 1)
                            n[x].dve += 1
                if R == P:
                    for x, (h0, h1) in enumerate(HALVES):
                        dve.wait_ge(sup_mm, 2 * ci + x + 1)
                        for h in range(h0, h1):
                            last = stt(out=st_p[:, h, :], in0=st_p[:, h, :], scalar=egr[:, h, P - 1:P],
                                       in1=bank(BC[x])[:, P * (h - h0):P * (h - h0 + 1)], op0=ALU.mult, op1=ALU.add)
                        last.then_inc(sup_done, 1)
                    continue
                dve.wait_ge(nwt_ready, 2 * ci + 2)
                dve.tensor_copy(wm.rearrange("p h (s c) -> p h s c", s=NS)[:, :, :, 0:DT],
                                nwt[:, :, 0:TS].rearrange("p h (s t) -> p h s t", s=NS)).then_inc(wm_ready, 1)
                for h in range(GH):
                    dve.wait_ge(vns_ready, h + 1)
                    tt(vx, vnw[0:R, h, :].unsqueeze(1).to_broadcast([R, NS, P]), bcast(GC["seq"][0:R, :], R, NS, P),
                       ALU.mult).then_inc(vx_ready, 1)
                    dve.wait_ge(snew_mm, h + 1)
                    egl = egr[:, h, 0:TS].rearrange("p (s t) -> p s t", t=DT)[:, :, DT - 1]
                    own(tt(sg[h % 3], sg[h % 3], bcast(egl, P, NS, P), ALU.mult))
                    tt(sg[h % 3], sg[h % 3], view(banks(6, 2), NS, P), ALU.add).then_inc(snew_ready, 1)
                dve.wait_ge(qs_read, 1)
                dve.wait_ge(oc_done, 9)
                tt(mixT[:, 0:GH, cols], mixT[:, 0:GH, cols], view(bank(2)[:, 0:GH * TS], GH, TS), ALU.add)\
                    .then_inc(oc_ready, 1)
            row_reciprocals(dve, 12, 2)
            dve.wait_ge(conv_done, 20)
            for c in range(6):
                dve.wait_ge(cn_bc, 12 + c + 1)
                x = halves_of(mixT[:, c, :])
                own(stt(out=x, in0=x, scalar=C["g_o"], in1=both(c % 2), op0=ALU.mult, op1=ALU.mult))
                tt(mixT[:, c, :], mixT[:, c, :], gproj[:, GZ + c, :], ALU.mult).then_inc(cn_ready, 1)

        @block.tensor
        def _(pe):
            mm = pe.matmul

            def square_sums(n, k, at=None):
                at = k if at is None else at
                pe.wait_ge(sq_ready, at + n * KT + 1)
                for half in range(2):
                    last = mm(both(3)[:, half, :], ones, halves_of(sq[:, k % 2, :])[:, half, :],
                              start=k == 0, stop=k == KT - 1)
                last.then_inc(sq_used, 1)

            def gemm(name, ktiles, rhs, inputs=None, norm=None):
                wb, tiles, eb = wbase[name], TILES[name], evac_base[name]
                evac = act_out if name in ("nsa_in", "up0", "gdn_in", "up1") else dve_out
                per = 8 if ktiles == KT else 2

                def tile(i, j, t):
                    if not isinstance(t, int) or t >= 2:
                        pe.wait_ge(evac, eb + t - 1)
                    elif name[:4] == "down":
                        pe.wait_ge(act_out, evac_base[f"up{name[4]}"] + 31 + t)
                    for k in range(ktiles):
                        hp = j // 2 if ktiles == KT else 2 * j + k // 16
                        slot = (wb + hp) % 4
                        if (ktiles == KT and j % 2 == 0 and k == 0) or (ktiles != KT and k % 16 == 0):
                            pe.wait_ge(in_panel[slot], 16 * (panel_uses(slot, wb + hp) + i))
                        if ktiles == KT:
                            lhs = view(ring[slot], KT, 256)[:, k, P * (j % 2):P * (j % 2 + 1)]
                        else:
                            lhs = view(ring[slot], 16, P)[:, k % 16, :]
                        if inputs and j == 0:
                            pe.wait_ge(inputs[0], inputs[1] + k + 1)
                        for half in range(2):
                            last = mm(both(j % 2)[:, half, :], lhs, halves_of(rhs[:, k, :])[:, half, :],
                                      start=k == 0, stop=k == ktiles - 1)
                    last.then_inc(pe_out, 1)

                first = 1 if norm else 0
                trips = tiles // per if tiles >= 2 * per else 0
                for t in range(per * first if trips else 0):
                    tile(0, t, t)
                    if t:
                        square_sums(norm, t - 1)
                if trips:
                    with pe.Fori(first, trips) as i:
                        for j in range(per):
                            tile(i, j, i * per + j)
                            if norm:
                                square_sums(norm, (j - 1) % 2 + 2, i * per + j - 1)
                for t in range(trips * per, tiles):
                    tile(t // per, t % per, t)
                    if norm and t:
                        square_sums(norm, t - 1)
                if norm:
                    square_sums(norm, KT - 1)

            def memory_sums():
                pe.wait_ge(in_common, 16)
                pe.wait_ge(mem_sq, KT)
                for k in range(KT):
                    last = mm(bank(0)[:, 0:MEM], ones, sqm[:, k, :], start=k == 0, stop=k == KT - 1)
                last.then_inc(mem_ss, 1)

            def memory_kv():
                for l in range(2):
                    pe.wait_ge(memn_ready, KT * (l + 1))
                    pe.wait_ge(in_panel[2 * l], 16)
                    wk, wv = view(ring[2 * l], KT, MEM), view(ring[2 * l + 1], KT, MEM)
                    for hp in range(2):
                        for k in range(KT):
                            last = mm(bank(1 + 2 * l)[:, MEM * hp:MEM * (hp + 1)], wk[:, k, P * hp:P * (hp + 1)],
                                      memn[:, l, k, :], start=k == 0, stop=k == KT - 1)
                    last.then_inc(pe_out, 1)
                    pe.wait_ge(in_panel[2 * l + 1], 16)
                    for m in range(2):
                        for k in range(KT):
                            last = mm(bank(2 + 2 * l)[:, MEM * m:MEM * (m + 1)], memn[:, l, k, P * m:P * (m + 1)],
                                      wv[:, k, :], start=k == 0, stop=k == KT - 1)
                    last.then_inc(pe_out, 1)

            def memory_attention(l):
                pr = (proj, gproj)[l]
                xq = (XQ0, XQ1)[l]
                kmem, vmem = view(mkv[l][:, 0:512], 2, MEM), view(mkv[l][:, 512:1024], 2, MEM)
                b = mb[l]
                pe.wait_ge(act_out, (NSA_T, NSA_T + 32 + GDN_T)[l])
                if l:
                    pe.wait_ge(in_mkv1, 16)
                else:
                    pe.wait_ge(memkv_ready, 2)

                def scores(qt):
                    if qt >= 2:
                        pe.wait_ge(xs_ready, 5 * l + qt - 1)
                    for hh in range(2):
                        for hp in range(2):
                            last = mm(bank(2 * (qt % 2) + hh)[:, MEM * hp:MEM * (hp + 1)],
                                      pr[64 * hh:64 * hh + 64, xq + hp, P * qt:P * (qt + 1)],
                                      kmem[64 * hh:64 * hh + 64, hp, :], start=True, stop=True)
                    last.then_inc(xm_ready, 1)

                def sample_scores():
                    pe.wait_ge(in_mcache, 16 * (l + 1))
                    pe.wait_ge(qm_ready, l + 1)
                    pe.wait_ge(xs_ready, 5 * l + 3)
                    for s in range(NS):
                        for hp in range(2):
                            last = mm(bank(0)[:, 0:MEM], b["qm"][:, MEM * s + P * hp:MEM * s + P * (hp + 1)],
                                      mcache[l][:, s, MEM * hp:MEM * (hp + 1)],
                                      start=s == hp == 0, stop=s == NS - 1 and hp == 1)
                    last.then_inc(xm_ready, 1)

                def values(n):
                    pe.wait_ge(xp_ready, 5 * l + n + 1)
                    if n:
                        pe.wait_ge(xpt_ready, 5 * l + n)
                    sm = b["sm"][n % 2]
                    for m in range(2):
                        for r in range(4 if n < 4 else 1):
                            last = pe.transpose(bank(4 + m)[:, P * r:P * (r + 1)], sm[:, r, P * m:P * (m + 1)], ident)
                    last.then_inc(xt_done, 1)
                    pe.wait_ge(xpt_ready, 5 * l + n + 1)
                    if n:
                        pe.wait_ge(mix_mem, 5 * l + n)
                    pt = b["pt"][n % 2]
                    if n < 4:
                        for hh in range(2):
                            for hp in range(2):
                                for m in range(2):
                                    last = mm(bank(6)[64 * hh:64 * hh + 64, P * hp:P * (hp + 1)],
                                              vmem[:, m, P * hp + 64 * hh:P * hp + 64 * hh + 64],
                                              pt[:, m, 2 * hh + hp, :], start=m == 0, stop=m == 1)
                    else:
                        for s in range(NS):
                            for hp in range(2):
                                for m in range(2):
                                    last = mm(bank(6)[:, 64 * hp + 8 * s:64 * hp + 8 * s + 8],
                                              mcache[l][:, s, 512 + MEM * m + P * hp:512 + MEM * m + P * (hp + 1)],
                                              pt[:, m, 0, 16 * s + 8 * hp:16 * s + 8 * hp + 8],
                                              start=m == 0, stop=m == 1)
                    last.then_inc(xo_done, 1)

                scores(0)
                scores(1)
                if l:
                    row_sums(pe, 0, 12)
                else:
                    compress_prompt(pe)
                for n in range(5):
                    if n < 2:
                        scores(n + 2)
                    elif n == 2:
                        sample_scores()
                    values(n)

            memory_sums()
            for k in range(KT):
                square_sums(0, k)
            memory_kv()
            pe.wait_ge(memkv_ready, 3)
            gemm("nsa_in", KT, hT, inputs=(h_ready, 0))
            memory_attention(0)
            pe_nsa_prompt(pe)
            pe_nsa_sample(pe)
            pe.wait_ge(seq_done, NS)
            gemm("out0", KT, mixT, norm=1)
            gemm("up0", KT, hT, inputs=(h_ready, KT))
            gemm("down0", FFT, u, inputs=(u_ready, 0), norm=2)
            gemm("gdn_in", KT, hT, inputs=(h_ready, 2 * KT))
            memory_attention(1)
            pe_gdn(pe)
            gemm("out1", KT, mixT, norm=3)
            gemm("up1", KT, hT, inputs=(h_ready, 3 * KT))
            gemm("down1", FFT, u, inputs=(u_ready, FFT), norm=4)

        @block.scalar
        def _(act):
            own = Chain(act, chain_act)
            f = act.activation

            def norm(n):
                if n == 0:
                    act.wait_ge(in_x, 16)
                for k in range(KT):
                    if n:
                        act.wait_ge(dve_out, 8 * (n - 1) + k + 1)
                    if n or k >= 2:
                        act.wait_ge(sq_used, n * KT + k - 1)
                    f(sq[:, k % 2, :], xT[:, k, :], ACT.Square).then_inc(sq_ready, 1)
                act.wait_ge(sq_used, (n + 1) * KT)
                if n:
                    act.wait_ge(h_ready, n * KT)
                f(halves_of(rstd), both(3), ACT.Sqrt, bias=C["eps"], scale=1.0 / D).then_inc(std_ready, 1)

            def convolved(t):
                if 2 <= t < 20:
                    act.wait_ge(conv_acc, t - 1)
                    f(gproj[:, t - 2, 0:TP], cacc[:, t % 2, :], ACT.Silu).then_inc(conv_done, 1)
                if t == 22:
                    act.wait_ge(conv_acc, 19)
                    f(gproj[:, 0:18, TP:TT_], sacc.rearrange("p c s t -> p c (s t)"), ACT.Silu).then_inc(conv_done, 1)
                if t == GZ + GH:
                    act.wait_ge(act_out, evac_base["gdn_in"] + GZ + GH)
                    f(gproj[:, GZ:GZ + GH, :], gproj[:, GZ:GZ + GH, :], ACT.Silu).then_inc(conv_done, 1)
                if t == GDN_T - 1:
                    act.wait_ge(conv_done, 19)

            def copy_out(name, dst, after=lambda t: None):
                for t in range(TILES[name]):
                    act.wait_ge(pe_out, obase[name] + t + 1)
                    f(halves_of(dst[:, t, :]), both(t % 2), ACT.Copy).then_inc(act_out, 1)
                    after(t)

            def up_out(l):
                with act.Fori(0, 16) as i:
                    for j in range(2):
                        dst = u[:, bass.ds(2 * i + j, 1), :].rearrange("p a n -> p (a n)")
                        act.wait_ge(pe_out, obase[f"up{l}"] + 1 + j + 2 * i)
                        act.nop(nofuse=True)
                        f(halves_of(dst), both(j), ACT.Relu).then_inc(act_out, 1)
                        act.wait_ge(act_out, evac_base[f"up{l}"] + 1 + j + 2 * i)
                        act.nop(nofuse=True)
                        f(dst, dst, ACT.Square).then_inc(u_ready, 1)

            def memory_norm():
                act.wait_ge(in_mem, 16)
                for k in range(KT):
                    f(sqm[:, k, :], memT[:, k, :], ACT.Square).then_inc(mem_sq, 1)
                act.wait_ge(mem_ss, 1)
                f(rstdm, bank(0)[:, 0:MEM], ACT.Sqrt, bias=C["eps"], scale=1.0 / D).then_inc(mem_std, 1)

            def memory_kv():
                for l in range(2):
                    for half in range(2):
                        act.wait_ge(pe_out, 2 * l + half + 1)
                        f((mkv0, mkv1_tmp)[l][:, 512 * half:512 * (half + 1)], bank(1 + 2 * l + half), ACT.Copy)\
                            .then_inc(memkv_ready, 1)

            def memory_attention(l):
                b = mb[l]

                def exps(n):
                    heads = 4 if n < 4 else 1
                    act.wait_ge(xmax_ready, 5 * l + n + 1)
                    if n >= 2:
                        act.wait_ge(xt_done, 5 * l + n - 1)
                    for r in range(heads):
                        last = f(b["sm"][n % 2][:, r, :], bank(2 * (n % 2) + r // 2)[:, MEM * (r % 2):MEM * (r % 2 + 1)]
                                 if n < 4 else bank(0)[:, 0:MEM], ACT.Exp, scale=HD ** -0.5,
                                 bias=b["stat"][:, n % 2, r:r + 1], accum_out=b["stat"][:, n % 2, 4 + r:5 + r])
                    last.then_inc(xs_ready, 1)

                def turned(n):
                    if l and n == 0:
                        row_roots(act, 0, 12, 1.0)
                    elif n == 0:
                        act.wait_ge(w1_used, 1)
                        f(pab.rearrange("p k h c -> p (k h c)"), bank(7)[:, 0:4 * CX], ACT.Copy).then_inc(pab_ready, 1)
                    heads = 4 if n < 4 else 1
                    act.wait_ge(xt_done, 5 * l + n + 1)
                    if n >= 2:
                        act.wait_ge(xo_done, 5 * l + n - 1)
                    for m in range(2):
                        last = f(b["pt"][n % 2][:, m, 0:heads, :].rearrange("p r q -> p (r q)"),
                                 bank(4 + m)[:, 0:P * heads], ACT.Copy)
                    last.then_inc(xpt_ready, 1)

                exps(0)
                for n in range(5):
                    if n < 4:
                        exps(n + 1)
                    turned(n)

            memory_norm()
            norm(0)
            memory_kv()
            copy_out("nsa_in", proj)
            memory_attention(0)
            act_nsa_prompt(act, own)
            act_nsa_sample(act, own)
            norm(1)
            up_out(0)
            norm(2)
            copy_out("gdn_in", gproj, convolved)
            column_squares(act, 0, 12, lambda c: gproj[:, c, :])
            memory_attention(1)
            act_gdn(act, own)
            norm(3)
            act.wait_ge(stored, 32)
            for b in range(3):
                act.wait_ge(state_stored[b], 16 * (GH // 3))
            up_out(1)
            norm(4)

        @block.vector
        def _(dve):
            own = Chain(dve, chain_dve)
            tt, ts, stt = dve.tensor_tensor, dve.tensor_scalar, dve.scalar_tensor_tensor

            def norm(n, gain):
                dve.wait_ge(std_ready, n + 1)
                own(dve.reciprocal(rstd, rstd))
                for k in range(KT):
                    stt(out=hT[:, k, :], in0=xT[:, k, :], scalar=gain[:, k:k + 1], in1=rstd, op0=ALU.mult,
                        op1=ALU.mult).then_inc(h_ready, 1)

            def residual(name):
                for t in range(8):
                    dve.wait_ge(pe_out, obase[name] + t + 1)
                    x = halves_of(xT[:, t, :])
                    tt(x, x, both(t % 2), ALU.add).then_inc(dve_out, 1)

            def memory_kv():
                dve.wait_ge(mem_std, 1)
                own(dve.reciprocal(rstdm, rstdm))
                for l in range(2):
                    for k in range(KT):
                        stt(out=memn[:, l, k, :], in0=memT[:, k, :], scalar=C["g_mem"][:, l, k:k + 1], in1=rstdm,
                            op0=ALU.mult, op1=ALU.mult).then_inc(memn_ready, 1)

            def memory_attention(l):
                b = mb[l]
                pr, xq = (proj, gproj)[l], (XQ0, XQ1)[l]
                own(dve.memset(b["qm"], 0.0))
                dve.wait_ge(act_out, (NSA_T, NSA_T + 32 + GDN_T)[l])
                for hp in range(2):
                    for hh in range(2):
                        r = slice(64 * hh, 64 * hh + 64)
                        dst = b["qm"][r, :].rearrange("p (s c) -> p s c", s=NS)
                        at = P * hp + 8 * hp + 4 * hh
                        last = dve.tensor_copy(dst[:, :, at:at + DT],
                                               pr[r, xq + hp, TP:TT_].rearrange("p (s t) -> p s t", s=NS))
                last.then_inc(qm_ready, 1)
                unit = lambda n: ((4 if n < 4 else 1), b["stat"][:, n % 2, :])

                def maxima(n):
                    heads, st = unit(n)
                    dve.wait_ge(xm_ready, 5 * l + n + 1)
                    own(dve.tensor_reduce(st[:, 0:heads], banks(2 * (n % 2), 2).rearrange("p (r c) -> p r c", r=4)
                                          if n < 4 else bank(0)[:, 0:MEM], AX.X, ALU.max))
                    ts(st[:, 0:heads], st[:, 0:heads], -HD ** -0.5, None, ALU.mult).then_inc(xmax_ready, 1)

                def scaled(n):
                    heads, st = unit(n)
                    dve.wait_ge(xs_ready, 5 * l + n + 1)
                    own(dve.reciprocal(st[:, 8:8 + heads], st[:, 4:4 + heads]))
                    sm = b["sm"][n % 2][:, 0:heads, :]
                    tt(sm, sm, bcast(st[:, 8:8 + heads], P, heads, MEM), ALU.mult).then_inc(xp_ready, 1)

                def output(n):
                    dve.wait_ge(xo_done, 5 * l + n + 1)
                    if n < 4:
                        dve.tensor_copy(mixT[:, 6:8, P * n:P * (n + 1)], view(bank(6)[:, 0:2 * P], 2, P))\
                           .then_inc(mix_mem, 1)
                    else:
                        for hh in range(2):
                            r = slice(64 * hh, 64 * hh + 64)
                            o = bank(6)[r, 0:P].rearrange("p (h s c) -> p h s c", h=2, s=NS)
                            last = dve.tensor_copy(
                                mixT[r, 6:8, TP:TT_].rearrange("p h (s t) -> p h s t", s=NS),
                                o[:, :, :, 4 * hh:4 * hh + DT])
                        last.then_inc(mix_mem, 1)

                maxima(0)
                maxima(1)
                for n in range(5):
                    scaled(n)
                    if l and n == 0:
                        row_reciprocals(dve, 24, 1)
                    elif n == 0:
                        block_sums_of_prompt(dve, own)
                    if n < 3:
                        maxima(n + 2)
                    if n:
                        output(n - 1)
                output(4)

            memory_kv()
            norm(0, C["g_mix"][:, 0, :])
            chunks_of_prompt(dve)
            memory_attention(0)
            dve_nsa_prompt(dve, own)
            dve_nsa_sample(dve, own)
            residual("out0")
            norm(1, C["g_ffn"][:, 0, :])
            residual("down0")
            norm(2, C["g_mix"][:, 1, :])
            dve_convolution(dve, own)
            memory_attention(1)
            dve_gdn(dve, own)
            residual("out1")
            norm(3, C["g_ffn"][:, 1, :])
            residual("down1")
            norm(4, C["g_fin"])


def constants():
    f = np.float32
    ar = np.arange
    c = {}
    slopes = np.exp2(f(-8.0) * ar(1, 13, dtype=f) / f(12)).astype(f)
    c["ident"], c["ones"] = np.eye(P, dtype=f), np.ones((P, P), f)
    c["eps"], c["one"] = np.full((P, 1), EPS, f), np.ones((P, 1), f)
    c["onecol"] = np.zeros((P, 47), f)
    c["onecol"][:, 23] = 1
    d = ar(P)[:, None] + TP - P - ar(TP)[None]
    c["dist"] = np.where(d >= 0, d, -NEG).astype(f)
    pos = ar(P)[:, None, None] + P * ar(4)[None, :, None]
    d = pos - (16 * ar(NCP) + 31)[None, None]
    c["cdist"] = np.where(d >= 0, d, -NEG).astype(f)
    c["cvis"] = (pos[:, :, 0] >= 31).astype(f)
    c["nslope"] = np.tile(-slopes, (P, 1))
    row = ar(ROWS)
    kv, g, t = row // 32, row % 32 // 4, row % 4
    real = g < NG
    sl = np.where(real, slopes[np.minimum(6 * kv + g, 11)], 0).astype(f)[:, None]

    def rows(a):
        return np.concatenate([a.astype(f), np.zeros((P - a.shape[0],) + a.shape[1:], f)])

    pos = (PAST + t)[:, None]
    c["b_slc"] = np.concatenate([-sl * (pos - h * PAST2 - ar(PAST2)[None]).astype(f) for h in range(2)])
    wp = PAST - WIN + ar(WIN)[None]
    c["b_win"] = rows(np.where(pos - wp < WIN, -sl * (pos - wp).astype(f), f(NEG)))
    c["b_cmp"] = rows(-sl * (pos - (16 * ar(NCB) + 31)[None]).astype(f))
    d = t[:, None] - ar(DT)[None]
    c["b_new"] = np.concatenate([np.where(d >= 0, -sl * d.astype(f), f(NEG)), np.full((ROWS, DT), NEG, f)])
    c["same"] = np.tile(rows((kv[:, None] == kv) & (t[:, None] == t) & real[:, None]), (1, 2))
    tok = ar(TS)[:, None, None]
    c["pick"] = rows(tok == DT * ar(NS)[None, :, None] + t[None, None])
    col = ar(36)
    c["head"] = rows(real[:, None] & (col[None] // 6 == g[:, None]) & (col[None] % 2 == kv[:, None]))
    own = ar(NSLC // 2)[None] + NSLC // 2 * (ar(P)[:, None] // ROWS)
    c["lower"] = (ar(1, NSLC - 1)[None, None] < own[:, :, None]).astype(f)
    c["drop"] = np.where((own == 0) | (own == NSLC - 1), 0, NEG).astype(f)
    i, j = ar(P)[:, None], ar(P)[None]
    c["cum"] = (i <= j).astype(f)
    si, sj = ar(TS)[:, None], ar(TS)[None]
    same = si // DT == sj // DT
    c["cum_s"], c["all_s"] = rows(same & (si <= sj)), rows(same)
    c["mask"], c["strict"] = np.where(j <= i, 0, NEG).astype(f), np.where(j < i, -1, 0).astype(f)
    c["mask_s"], c["strict_s"] = rows(np.where(same & (sj <= si), 0, NEG)), rows(np.where(same & (sj < si), -1, 0))
    c["diag"] = (i // 16 == j // 16).astype(f)
    c["off"] = np.stack([(i // (2 * m) == j // (2 * m)) & (i // m > j // m) for m in (16, 32, 64)], 1).astype(f)
    c["seq"] = rows(si // DT == ar(NS)[None])
    return c


def pack(tb, parts):
    out = [np.ascontiguousarray(np.asarray(parts[k], np.float32).reshape(P, -1)) for k in tb.at]
    assert [a.shape[1] for a in out] == [int(np.prod(s)) for _, s in tb.at.values()], [a.shape for a in out]
    return np.concatenate(out, 1)


def kernel(**inputs):
    import concourse.bacc as bacc
    from concourse.bass_utils import run_bass_kernel_spmd

    a = {k: np.asarray(v) for k, v in inputs.items()}
    c = constants()
    chan = lambda v: v.reshape(v.shape[:-1] + (KT, P)).transpose(v.ndim, *range(v.ndim))
    cols = lambda x: x.T.reshape(KT, P, -1).transpose(1, 0, 2)

    for name, key in (("g_mix", "norm_mix_g"), ("g_mem", "norm_mem_g"), ("g_ffn", "norm_ffn_g")):
        c[name] = chan(a[key])
    c["g_fin"] = chan(a["final_norm_g"])
    lpair = lambda w: w.reshape(16, 2 * HD, -1).transpose(1, 0, 2)
    c["pe"] = np.stack([lpair(a[k][0].reshape(32, HD, 1))[:, :, 0] for k in ("cmp_pe_k", "cmp_pe_v")], 1)
    c["w2"] = np.stack([a["cmp_w2_k"][0], a["cmp_w2_v"][0]], 1)
    c["conv_w"] = a["gdn_conv_w"][0].reshape(4, 18, P).transpose(2, 1, 0)
    c["g_o"] = a["gdn_norm_g"][0][:, None]
    c["a_log"], c["dt_bias"] = (np.broadcast_to(a[k][0], (P, GH)) for k in ("gdn_a_log", "gdn_dt_bias"))

    def wide(w):
        n = -(-w.shape[1] // 256)
        w = np.concatenate([w, np.zeros((D, 256 * n - w.shape[1]), w.dtype)], 1)
        return w.reshape(KT, P, n, 256).transpose(2, 1, 0, 3).reshape(n, P, 2048)

    def tall(w):
        return w.reshape(2, 16, P, KT, P).transpose(3, 0, 2, 1, 4).reshape(16, P, 2048)

    w = a["nsa_w_in"][0]
    heads = lambda x: x.reshape(-1, NKV, NG, HD).transpose(0, 2, 1, 3).reshape(x.shape[0], -1)
    gates = w[:, 1536:1572].reshape(D, NKV, NG, 3)[..., [1, 2, 0]].transpose(0, 2, 3, 1).reshape(D, 36)
    nsa_in = np.concatenate([heads(w[:, 0:768]), w[:, 768:1536], w[:, 1572:1828], gates], 1)
    w = a["gdn_w_in"][0]
    gdn_w = np.concatenate([w[:, 0:3072], w[:, 3084:3340], w[:, 3072:3084]], 1)
    wo = a["w_out"]
    out0 = np.concatenate([heads(wo[0][:768].T).T, wo[0][768:]], 0)
    w1 = np.stack([lpair(a[k][0]).reshape(P, 2048) for k in ("cmp_w1_k", "cmp_w1_v")])
    panels = np.concatenate([wide(a["w_mem_kv"][0]), wide(a["w_mem_kv"][1]), wide(nsa_in), w1, wide(out0),
                             wide(a["w_up"][0]), tall(a["w_down"][0]), wide(gdn_w), wide(wo[1]),
                             wide(a["w_up"][1]), tall(a["w_down"][1])])

    kv = a["cache_nsa_kv"][:, :, 0]
    ck = kv[:, :, 0:2].reshape(NPHYS, 8, 8, 2, 2, NKV, HD).transpose(0, 3, 6, 4, 2, 5, 1).reshape(NPHYS, P, 256)
    pages = np.concatenate([ck, kv[:, :, 2].reshape(NPHYS, PAGE, P).transpose(0, 2, 1), kv[:, :, 3].reshape(NPHYS, PAGE, P)], 2)
    wn = a["cache_nsa_win"][:, 0]
    win = np.concatenate([wn[:, :, 0].reshape(NS, WIN, P).transpose(0, 2, 1),
                          wn[:, :, 1].reshape(NS, 4, P, P).transpose(0, 2, 1, 3).reshape(NS, P, 512)], 2)
    mc = a["cache_mem_kv"].transpose(1, 0, 2, 3, 4, 5)
    mk = mc[:, :, :, 0].reshape(2, NS, MEM, 2, P).transpose(0, 1, 4, 3, 2).reshape(2, NS, P, 512)
    mv = mc[:, :, :, 1].reshape(2, NS, 2, P, MEM).transpose(0, 1, 3, 2, 4).reshape(2, NS, P, 512)

    arrays = dict(
        x=np.concatenate([cols(a["x_prompt"][0]), cols(a["x_sample"].reshape(TS, D))], 2),
        mem=cols(a["mem_prompt"][0]), w=panels, common=pack(COMMON, c), prompt=pack(PROMPT_T, c),
        sample=pack(SAMPLE_T, c), gdn=pack(GDN_TB, c), pages=pages, win=win, mcache=np.concatenate([mk, mv], 3),
        conv=a["state_gdn_conv"][:, 0].reshape(NS, 3, 18, P).transpose(3, 2, 0, 1),
        state=a["state_gdn_s"][:, 0].transpose(1, 2, 0, 3), table=a["page_table"].reshape(1, NS * NPAGE))
    outs = dict(y=(P, KT, TT_), kv=(P, 6, TT_), win_o=(NS, P, 1024), conv_p=(P, 18, 3), conv_s=(P, 18, NS, 3),
                state_p=(P, GH, P), state_s=(GH, P, NS, P), mem_o=(2, P, 1024))
    nc = bacc.Bacc("TRN2", target_bir_lowering=False, num_devices=1)
    ins, args = {}, []
    for name, v in arrays.items():
        v = np.ascontiguousarray(v)
        ins[f"in_{name}"] = v
        args.append(nc.dram_tensor(f"in_{name}", v.shape, mybir.dt.from_np(v.dtype), kind="ExternalInput").ap())
    for name, shape in outs.items():
        args.append(nc.dram_tensor(f"out_{name}", shape, F32, kind="ExternalOutput").ap())
    build(nc, *args)
    r = run_bass_kernel_spmd(nc, [ins], core_ids=[0]).results[0]
    o = {k: np.asarray(r[f"out_{k}"]) for k in outs}

    y = o["y"].transpose(2, 1, 0).reshape(TT_, D)
    kvr = o["kv"].transpose(2, 1, 0).reshape(TT_, 6, NKV, HD)
    wk = o["win_o"][:, :, 0:512].transpose(0, 2, 1)
    wv = o["win_o"][:, :, 512:].reshape(NS, P, 4, P).transpose(0, 2, 1, 3).reshape(NS, WIN, P)
    old = np.stack([wk, wv], 2).reshape(NS, WIN, 2, NKV, HD)
    new = kvr[TP:, 4:6].reshape(NS, DT, 2, NKV, HD)
    mo = o["mem_o"]
    mkp = mo[:, :, 0:512].reshape(2, P, 2, MEM).transpose(0, 3, 2, 1).reshape(2, MEM, XH, HD)
    mvp = mo[:, :, 512:].reshape(2, P, 2, MEM).transpose(0, 2, 1, 3).reshape(2, MEM, XH, HD)
    res = (y[:TP][None], y[TP:].reshape(NS, DT, D), kvr[:TP, 0:4][None, :, None], kvr[TP:, 0:4].reshape(NS, DT, 1, 4, NKV, HD),
           kvr[:TP, 4:6][None, None], np.concatenate([old[:, DT:], new], 1)[:, None],
           o["state_p"].transpose(1, 0, 2)[None, None], o["state_s"].transpose(2, 0, 1, 3)[:, None],
           o["conv_p"].transpose(2, 1, 0).reshape(1, 1, 3, 2304),
           o["conv_s"].transpose(2, 3, 1, 0).reshape(NS, 1, 3, 2304),
           np.stack([mkp, mvp], 2)[None])
    return tuple(np.ascontiguousarray(x) for x in res)
```

```python
from contextlib import ExitStack

import numpy as np

import concourse.bass as bass
from concourse import mybir

F32 = mybir.dt.float32
I32 = mybir.dt.int32
ALU = mybir.AluOpType
ACT = mybir.ActivationFunctionType
AX = mybir.AxisListType

P = 128
D = 1024
KT = D // P
TP, NS, DT = 512, 8, 4
TS = NS * DT
TT_ = TP + TS
HALF = TT_ // 2
MEM = 256
NKV, NG, HD = 2, 6, 64
NPAGE, PAGE = 16, 128
PAST = NPAGE * PAGE
NPHYS = (NS * NPAGE * 5 + 3) // 4
NCB = PAST // 16 - 1
NCP = TP // 16 - 1
NSLC = PAST // 64
TOPN = 16
WIN = 512
XH = 4
GH = 6
EPS = 1e-6
NEG = -1e30
FFT = 4 * D // P
NSA_T, GDN_T = 15, 27
ROWS = 64
PAST2 = PAST // 2

XQ0, CK, CV, SK, SV, WK, WV, Q0, GT = 0, 2, 3, 4, 5, 6, 7, 8, 14
XQ1, BA, GQ, GK, GV, GZ = 0, 2, 3, 9, 15, 21


class Table:

    def __init__(self, *parts):
        self.at, self.size = {}, 0
        for name, *shape in parts:
            n = int(np.prod(shape))
            self.at[name] = (self.size, tuple(shape))
            self.size += n


COMMON = Table(("ident", P), ("ones", P), ("g_mix", 2, KT), ("g_mem", 2, KT), ("g_ffn", 2, KT), ("g_fin", KT),
               ("pe", 2, 16), ("w2", 2, HD), ("conv_w", 18, 4), ("g_o", 1), ("a_log", GH), ("dt_bias", GH),
               ("eps", 1), ("one", 1))
PROMPT_T = Table(("dist", TP), ("cdist", 4, NCP), ("cvis", 4), ("nslope", 12))
SAMPLE_T = Table(("b_slc", PAST // 2), ("b_win", WIN), ("b_cmp", NCB), ("b_new", DT), ("same", P), ("pick", NS, ROWS),
                 ("head", 36), ("lower", NSLC // 2, NSLC - 2), ("drop", NSLC // 2))
GDN_TB = Table(("cum", P), ("cum_s", TS), ("all_s", TS), ("mask", P), ("mask_s", TS), ("diag", P), ("diag_t", P),
               ("off", 3, P), ("seq", NS))


def view(ap, *shape):
    if len(shape) < 2:
        return ap
    names = "abcd"[:len(shape)]
    return ap.rearrange(f"p ({' '.join(names)}) -> p {' '.join(names)}", **dict(zip(names[1:], shape[1:])))


class Arena:

    def __init__(self, t, lo, hi):
        self.t, self.lo, self.hi = t, lo, hi

    def take(self, *shape, rows=P):
        n = int(np.prod(shape))
        assert self.lo + n <= self.hi, (self.lo, n, self.hi)
        ap = self.t[0:rows, self.lo:self.lo + n]
        self.lo += n
        return view(ap, *shape)

    def table(self, tb):
        ap = self.take(tb.size)
        return ap, {k: view(ap[:, o:o + int(np.prod(s))], *s) for k, (o, s) in tb.at.items()}


class Chain:

    def __init__(self, eng, sem):
        self.eng, self.sem, self.n = eng, sem, 0

    def __call__(self, ins):
        ins.then_inc(self.sem, 1)
        self.n += 1
        self.eng.wait_ge(self.sem, self.n)


def bcast(ap, *shape):
    while len(ap.shape) < len(shape):
        ap = ap.unsqueeze(len(ap.shape))
    return ap.to_broadcast(list(shape))


def build(nc, x_in, mem_in, w_in, common_in, prompt_in, sample_in, gdn_in, pages_in, win_in, mcache_in, conv_in,
          state_in, table_in, y_out, kv_out, win_out, conv_out_p, conv_out_s, state_out_p, state_out_s, mem_out):
    with ExitStack() as ctx:
        sem = lambda name: ctx.enter_context(nc.semaphore(name))
        TOTAL = 53060
        sbuf = ctx.enter_context(nc.sbuf_tensor("sbuf", [P, TOTAL], F32))
        pages_sb = ctx.enter_context(nc.sbuf_tensor("page_table", [1, NS * NPAGE], I32))
        psum = ctx.enter_context(nc.psum_tensor("psum", [P, 8, 512], F32))
        bank = lambda b: psum[:, b, :]
        both = lambda j: psum[:, 2 * j:2 * j + 2, 0:HALF]
        halves_of = lambda ap: view(ap, 2, HALF)
        banks = lambda b, n: psum[:, b:b + n, :].rearrange("p a n -> p (a n)")

        top = Arena(sbuf, 0, TOTAL)
        _, C = top.table(COMMON)
        common_ap = sbuf[:, 0:COMMON.size]
        xT = top.take(KT, TT_)
        hT = top.take(KT, TT_)
        ring = [top.take(2048) for _ in range(4)]
        big0 = top.lo
        top.lo += 16384
        pj0 = top.lo
        top.lo += 8192
        work0 = top.lo
        big = lambda: Arena(sbuf, big0, big0 + 16384)
        pj = lambda: Arena(sbuf, pj0, pj0 + NSA_T * TT_)
        rest = lambda: Arena(sbuf, work0, TOTAL)
        mixT = hT

        a = rest()
        sq = a.take(2, TT_)
        rstd = a.take(TT_)
        norm_end = a.lo
        after_norm = lambda: Arena(sbuf, norm_end, TOTAL)

        persist = after_norm()
        gsamp = persist.take(36, rows=TS)
        pebias = persist.take(2)
        free0 = persist.lo
        free = lambda: Arena(sbuf, free0, TOTAL)

        a = free()
        mkv0 = a.take(1024)
        mkv0_end = a.lo
        memT = a.take(KT, MEM)
        a = big()
        sqm = a.take(KT, MEM)
        memn = a.take(2, KT, MEM)
        rstdm = a.take(MEM)
        mkv1_tmp = a.take(1024)

        proj = pj().take(NSA_T, TT_)
        page_kv, page_cmp = [[view(sbuf[:, lo:lo + 4096], NPAGE, 2 * P) for lo in (at, at + 8192)]
                             for at in (big0, big0 + 4096)]
        mcache = [view(sbuf[:, big0 + 8192:big0 + 16384], NS, 1024), None]

        def memory_buffers(a):
            return dict(sm=[a.take(4, MEM) for _ in range(2)], pt=[a.take(2, 4, P) for _ in range(2)],
                        stat=a.take(2, 16), qm=a.take(NS * (2 * P + 16)))

        a = Arena(sbuf, mkv0_end, TOTAL)
        mb = [memory_buffers(a), None]
        CX = NKV * TP // 16 + 2
        xtp = a.take(2, 8, CX)
        pab = a.take(2, 2, CX)
        phid = a.take(2, 2, 32)
        mkv = [mkv0, None]

        a = Arena(sbuf, big0 + 8192, big0 + 12288)
        s_sb = [a.take(4, TP) for _ in range(2)] + [None]
        vn = view(ring[3][:, 1024:2048], 2, 4, P)
        a = free()
        qs = [a.take(TP), ring[3][:, 0:TP], ring[3][:, TP:2 * TP]]
        prompt_ap, PT = a.table(PROMPT_T)
        s_sb[2] = a.take(4, TP)
        scp = [a.take(2, 32) for _ in range(3)]
        ptp = [a.take(4, P) for _ in range(3)]
        ptc = a.take(2, P, rows=NCP)
        stp = a.take(3, 24)
        gnat = a.take(4, 36)
        kcp = a.take(2, NCP)
        vcp = a.take(P, rows=NCP)

        sample_ap, ST = a.table(SAMPLE_T)
        prompt_end = a.lo - SAMPLE_T.size
        a = free()
        S_NEW, S_WIN, S_WNEW, S_CMP = PAST2, PAST2 + DT, PAST2 + DT + WIN, PAST2 + 2 * DT + WIN
        ssc = a.take(S_CMP + NCB + 1)
        low, high = ssc[0:ROWS, :], ssc[ROWS:P, :]
        pts = a.take(20, ROWS)
        ptcs = a.take(ROWS, rows=NCB)
        cab0 = ring[3][:, 0:1024].rearrange("p (k h c) -> p k h c", k=2, h=2)
        rank = ring[3]
        cab = a.take(2, 2, 2 * P)
        assert a.lo <= prompt_end
        a.lo = work0
        chid = a.take(2, 2, P)
        kc = a.take(2, P)
        vc = a.take(2, P, rows=NCB)
        vnew = a.take(2, P, rows=DT)
        ptn = a.take(2, ROWS, rows=DT)
        imp = a.take(NSLC)
        imph = a.take(NSLC // 2)
        sel = a.take(NSLC // 2)
        impc = rank[:, 1800:1800 + P]
        qb = a.take(ROWS)
        vst = a.take(2, DT)
        gr = a.take(3, rows=ROWS)
        grt = a.take(36, rows=ROWS)
        sst = a.take(16)
        stl = sst[0:ROWS, :]
        assert a.lo <= norm_end
        wcache = [ring[2][:, 1024 * s:1024 * (s + 1)] for s in range(2)]
        u = view(sbuf[:, pj0 + 8192 - FFT * TT_:pj0 + 8192], FFT, TT_)

        a = big()
        gproj = a.take(GDN_T, TT_)
        gdn_b = a
        mcache[1] = view(sbuf[:, pj0:pj0 + 8192], NS, 1024)
        a = free()
        gdn_ap, GC = a.table(GDN_TB)
        ban = a.take(5, 12)
        beta = a.take(5, GH)
        gat = a.take(5, GH)
        spl = a.take(5, GH)
        nea = a.take(GH)
        gcn, egc, bex, kde, egt, br, br2 = [a.take(5, GH) for _ in range(7)]
        kr, kr2 = br, br2
        small_end = a.lo
        mkv[1] = a.take(1024)
        mb[1] = memory_buffers(a)
        cbuf = a.take(18, NS, 3)
        cout_s = gdn_b.take(18, NS, 3)
        cout_p = gdn_b.take(18, 3)
        a = rest()
        sconv = [[a.take(12, NS, DT) for _ in range(2)]]
        a.lo = work0 + 2 * TT_
        sconv.append([a.take(6, NS, DT) for _ in range(2)])
        cacc = gdn_b.take(2, TP)
        osq = sq.rearrange("p a n -> p (a n)")
        rinv, qn = [view(rstd[:, 5 * GH * i:5 * GH * (i + 1)], 5, GH) for i in range(2)]
        a = Arena(sbuf, small_end, TOTAL)
        cw = lambda a: a.take(GH, P)
        ug, dec, egr, bm, qt_, kbg, kdec, vb, pw = [cw(a) for _ in range(9)]
        sg = [view(cacc.rearrange("p a n -> p (a n)"), NS, P), None, a.take(NS, P)]
        a = pj()
        a.hi = pj0 + 8192
        pwt, tt_, nwt, qg, st_p = [cw(a) for _ in range(5)]
        vnw = a.take(GH, P)
        wq = a.take(2, NS * (2 * TS + DT))
        vo = a.take(2, P, rows=2 * TS)
        vx = a.take(NS, P, rows=TS)
        sg[1] = a.take(NS, P)
        sg = [view(t.rearrange("p s v -> p (s v)"), 2, 4, P) for t in sg] + \
             [gproj[:, GK + 2 * i:GK + 2 * i + 2, 0:TP].rearrange("p c (s v) -> p c s v", s=4) for i in range(3)]
        qd, tn, zz = vnw, nwt, pwt

        in_common, in_x, in_mem, in_table = sem("in_common"), sem("in_x"), sem("in_mem"), sem("in_table")
        in_prompt_t, in_sample_t, in_gdn_t = sem("in_prompt_t"), sem("in_sample_t"), sem("in_gdn_t")
        in_panel = [sem(f"in_panel{s}") for s in range(4)]
        in_cmp = [sem(f"in_cmp{s}") for s in range(2)]
        in_pages = [sem(f"in_pages{s}") for s in range(2)]
        in_mcache, in_mkv1, in_conv = sem("in_mcache"), sem("in_mkv1"), sem("in_conv")
        in_state = [sem(f"in_state{h}") for h in range(GH)]
        stored, mem_stored = sem("stored"), sem("mem_stored")
        state_stored = sem("state_stored")
        chain_act, chain_dve = sem("chain_act"), sem("chain_dve")
        mem_sq, mem_ss, mem_std, memn_ready, memkv_ready = map(sem, ("mem_sq", "mem_ss", "mem_std", "memn_ready",
                                                                     "memkv_ready"))
        pe_out = sem("pe_out")
        act_out = sem("act_out")
        dve_out = sem("dve_out")
        u_ready = sem("u_ready")
        sq_ready, sq_used, std_ready, h_ready = map(sem, ("sq_ready", "sq_used", "std_ready",
                                                                   "h_ready"))
        xs_ready, xm_ready, xp_ready, xt_done, xpt_ready, xo_done, mix_mem = map(
            sem, ("xs_ready", "xm_ready", "xp_ready", "xt_done", "xpt_ready", "xo_done", "mix_mem"))
        qm_ready, xmax_ready = sem("qm_ready"), sem("xmax_ready")
        vg_done, vg_ready, w1_used, pab_ready, phid_ready, pkv_done, pkv_ready = map(
            sem, ("vg_done", "vg_ready", "w1_used", "pab_ready", "phid_ready", "pkv_done", "pkv_ready"))
        xtp_ready, psum_ready, kcp_zeroed = sem("xtp_ready"), sem("psum_ready"), sem("kcp_zeroed")
        qs_ready, ps_done, ps_read, pmax_ready, pexp_ready, pp_ready = map(
            sem, ("qs_ready", "ps_done", "ps_read", "pmax_ready", "pexp_ready", "pp_ready"))
        pt_done, pt_ready, po_done, prompt_done = map(sem, ("pt_done", "pt_ready", "po_done", "prompt_done"))
        first_done, first_read = sem("first_done"), sem("first_read")
        cab_ready, hsum_ready, hid_ready, kvc_done, kvc_ready = map(
            sem, ("cab_ready", "hsum_ready", "hid_ready", "kvc_done", "kvc_ready"))
        qb_ready, vnew_done, vnew_ready, sc_done, cmax_ready, cexp_ready, cp_ready, imp_done = map(
            sem, ("qb_ready", "vnew_done", "vnew_ready", "sc_done", "cmax_ready", "cexp_ready", "cp_ready",
                  "imp_done"))
        smax_ready, sexp_ready, sp_ready, spt_done, spt_ready, so_done, seq_done = map(
            sem, ("smax_ready", "sexp_ready", "sp_ready", "spt_done", "spt_ready", "so_done", "seq_done"))
        wmax_ready, wexp_ready, slc_biased = map(sem, ("wmax_ready", "wexp_ready", "slc_biased"))
        win_stored = [sem("win_stored0"), sem("win_stored1")]
        conv_acc, conv_done, couts_ready, conv_stored = map(sem, ("conv_acc", "conv_done", "couts_ready", "conv_stored"))
        ba_done, gate_pre, gat_ready = map(sem, ("ba_done", "gate_pre", "gat_ready"))
        ban_read, ks_read, kr_ready, cn_var = map(sem, ("ban_read", "ks_read", "kr_ready", "cn_var"))
        cn_sq, cn_ss, cn_std, cn_rec, cn_bc, cn_ready = map(sem, ("cn_sq", "cn_ss", "cn_std", "cn_rec", "cn_bc",
                                                                  "cn_ready"))
        kv_done, vb_ready, gates_ready = map(sem, ("kv_done", "vb_ready", "gates_ready"))
        gt_done, gexp_pre, gexp_ready, bexp_ready, qt_ready = map(
            sem, ("gt_done", "gexp_pre", "gexp_ready", "bexp_ready", "qt_ready"))
        ug_ready, gc_done, gc_ready, dexp_ready, kq_done, bm_ready, tr_done, tr_ready = map(
            sem, ("ug_ready", "gc_done", "gc_ready", "dexp_ready", "kq_done", "bm_ready", "tr_done",
                  "tr_ready"))
        inv_pe, inv_act, inv_dve = [[sem(f"inv_{e}{x}") for x in range(2)] for e in ("pe", "act", "dve")]
        wt_done, nwt_ready, vn_done, vn_ready, oc_done, oc_ready, sup_mm, sup_done = map(
            sem, ("wt_done", "nwt_ready", "vn_done", "vn_ready", "oc_done", "oc_ready", "sup_mm", "sup_done"))
        sdec_ready = sem("sdec_ready")
        wq_ready, vx_ready, snew_mm, snew_ready, vns_done, vns_ready = map(
            sem, ("wq_ready", "vx_ready", "snew_mm", "snew_ready", "vns_done", "vns_ready"))

        GEMMS = [("mem", 4), ("nsa_in", 8), ("w1", 2), ("window", 1), ("out0", 4), ("up0", 16), ("down0", 16),
                 ("gdn_in", 14), ("out1", 4), ("up1", 16), ("down1", 16)]
        TILES = dict(mem=4, nsa_in=NSA_T, out0=8, up0=32, down0=8, gdn_in=GDN_T, out1=8, up1=32, down1=8)
        wbase, obase, src, free_at = {}, {}, [], []
        w = o = n_src = 0
        for name, n in GEMMS:
            wbase[name], obase[name] = w, o
            for j in range(n):
                src.append(None if name == "window" else n_src)
                n_src += name != "window"
                if name in ("w1", "window"):
                    free_at.append(name)
                elif name == "mem":
                    free_at.append(o + j + 1)
                elif name.startswith("down"):
                    free_at.append(o + j // 2 + 1)
                else:
                    free_at.append(o + min(2 * j + 2, TILES[name]))
            w += n
            o += TILES.get(name, 0)
        n_panels = w
        evac_base = dict(nsa_in=0, up0=NSA_T, gdn_in=NSA_T + 32, up1=NSA_T + 32 + GDN_T,
                         out0=0, down0=8, out1=16, down1=24)

        def panel_uses(slot, i):
            return i // 4 + 1 - (1 if slot == 2 and i > wbase["window"] else 0)

        MEM_FIRST = (2, 2)
        GATES, CONV, LENGTHS = 4, 2, 18

        ident, ones = C["ident"], C["ones"]
        block = ctx.enter_context(nc.Block())

        @block.sync
        def _(sp):
            sp.dma_start(common_ap, common_in).then_inc(in_common, 16)
            sp.dma_start(memT, mem_in).then_inc(in_mem, 16)

            def panel(i):
                slot = i % 4
                if i >= 4:
                    f = free_at[i - 4]
                    if f == "w1":
                        sp.wait_ge(w1_used, NS)
                    elif f == "window":
                        sp.wait_ge(seq_done, NS)
                        for b in range(2):
                            sp.wait_ge(win_stored[b], 16 * (NS // 2))
                    else:
                        sp.wait_ge(pe_out, f)
                sp.dma_start(ring[slot], w_in[src[i]]).then_inc(in_panel[slot], 16)

            panel(0)
            sp.dma_start(xT, x_in).then_inc(in_x, 16)
            for i in range(1, 4):
                panel(i)
            sp.dma_start(pages_sb[:, :], table_in).then_inc(in_table, 16)

            def sequence(s):
                at = [sp.value_load(pages_sb[0:1, s * NPAGE + p:s * NPAGE + p + 1], min_val=0, max_val=NPHYS - 1)
                      for p in range(NPAGE)]

                def pages(to, cols, landed):
                    for p in range(NPAGE):
                        sp.dma_start(to[s % 2][:, p, :],
                                     pages_in[bass.ds(at[p], 1), :, cols].rearrange("a p n -> (a p) n"))\
                            .then_inc(landed[s % 2], 16)

                if s >= 3:
                    sp.wait_ge(w1_used, s - 1)
                pages(page_cmp, slice(0, 2 * P), in_cmp)
                if s == 1:
                    sp.wait_ge(prompt_done, 24)
                if s >= 2:
                    sp.wait_ge(seq_done, s - 1)
                pages(page_kv, slice(2 * P, 4 * P), in_pages)
                if s >= 2:
                    sp.wait_ge(win_stored[s % 2], 16 * (s // 2))
                if s:
                    window(s)

            def window(s):
                sp.dma_start(wcache[s % 2], win_in[s]).then_inc(in_pages[s % 2], 16)

            for i in range(4, 14):
                panel(i)
                if i == 8:
                    sp.wait_ge(memn_ready, 2 * KT)
                    sp.wait_ge(mem_stored, 32)
                    sp.dma_start(mcache[0], mcache_in[0].rearrange("s p n -> p s n")).then_inc(in_mcache, 16)
                if i == 10:
                    sp.wait_ge(in_table, 16)
                    sequence(0)
            sp.wait_ge(pe_out, 4 + NSA_T)
            window(0)
            sp.wait_ge(mix_mem, 5)
            sp.dma_start(prompt_ap, prompt_in).then_inc(in_prompt_t, 16)
            sp.wait_ge(w1_used, 1)
            sp.wait_ge(psum_ready, 2)
            sp.dma_start(sample_ap, sample_in).then_inc(in_sample_t, 16)
            for s in range(1, NS):
                sequence(s)
            for i in range(15, wbase["gdn_in"] + 14):
                if i == 15:
                    sp.wait_ge(smax_ready, NS)
                panel(i)
                if i == wbase["gdn_in"] + 3:
                    sp.wait_ge(pe_out, obase["gdn_in"])
                    sp.wait_ge(dve_out, 16)
                    sp.dma_start(mkv[1], mem_out[1]).then_inc(in_mkv1, 16)
                    sp.dma_start(gdn_ap, gdn_in).then_inc(in_gdn_t, 16)
                    sp.dma_start(cbuf, conv_in).then_inc(in_conv, 16)
                    sp.dma_start(mcache[1], mcache_in[1].rearrange("s p n -> p s n")).then_inc(in_mcache, 16)
            for i in range(wbase["out1"], wbase["out1"] + 4):
                panel(i)
            for h in range(GH):
                if h == 0:
                    sp.wait_ge(conv_done, 20)
                    sp.wait_ge(mix_mem, 10)
                    sp.wait_ge(conv_stored, 32)
                if h == 3:
                    sp.wait_ge(kq_done, 8)
                    sp.wait_ge(tr_ready, 8)
                sp.dma_start(sg[h], state_in[h].rearrange("p (a s) v -> p a s v", a=2)).then_inc(in_state[h], 16)
            for i in range(wbase["up1"], n_panels):
                panel(i)

        @block.gpsimd
        def _(pool):
            for l in range(2):
                pool.wait_ge(memkv_ready, 2 * l + 2)
                pool.dma_start(mem_out[l], (mkv0, mkv1_tmp)[l]).then_inc(mem_stored, 16)
            pool.wait_ge(act_out, WV + 1)
            pool.dma_start(kv_out, proj[:, CK:WV + 1, :]).then_inc(stored, 16)
            for s in range(NS):
                pool.wait_ge(in_pages[s % 2], 16 * (NPAGE + 1) * (s // 2 + 1))
                pool.dma_start(win_out[s], wcache[s % 2]).then_inc(win_stored[s % 2], 16)
            pool.wait_ge(conv_done, 20)
            pool.wait_ge(couts_ready, 1)
            pool.dma_start(conv_out_p, cout_p).then_inc(conv_stored, 16)
            pool.dma_start(conv_out_s, cout_s).then_inc(conv_stored, 16)
            pool.wait_ge(sup_done, 8)
            pool.dma_start(state_out_p, st_p).then_inc(stored, 16)
            for h in range(GH):
                pool.wait_ge(snew_ready, h + 1)
                pool.dma_start(state_out_s[h].rearrange("p (a s) v -> p a s v", a=2), sg[h]).then_inc(state_stored, 16)
            for k in range(KT):
                pool.wait_ge(h_ready, 4 * KT + k + 1)
                pool.dma_start(y_out[:, k, :], hT[:, k, :]).then_inc(stored, 16)
            pool.wait_ge(stored, 16 * (2 + KT))
            pool.wait_ge(mem_stored, 32)
            pool.wait_ge(conv_stored, 32)
            for b in range(2):
                pool.wait_ge(win_stored[b], 16 * (NS // 2))
            pool.wait_ge(state_stored, 16 * GH)

        ident, ones = C["ident"], C["ones"]


        PAIR = ((0, 3), (1, 3), (0, 2), (1, 2), (0, 1), (1, 1), (0, 0), (1, 0))
        unit = lambda n: (2 * (n // 8) + PAIR[n % 8][0], PAIR[n % 8][1])
        groups = lambda n: sum(unit(m)[1] + 2 for m in range(n))
        scored = lambda g: 8 * (g // 2) + 1 + max(m for m in range(8) if PAIR[m][0] == g % 2)

        def compress_prompt(pe):
            w1 = [view(ring[kind], 16, P) for kind in range(2)]
            pe.wait_ge(in_panel[0], 16 * panel_uses(0, wbase["w1"]))
            pe.wait_ge(in_panel[1], 16 * panel_uses(1, wbase["w1"] + 1))
            pe.wait_ge(xtp_ready, 1)
            for kind in range(2):
                for half in range(2):
                    at = CX * (2 * kind + half)
                    for lp in range(8):
                        last = pe.matmul(bank(7)[:, at:at + CX], w1[kind][:, 8 * half + lp, :], xtp[:, kind, lp, :],
                                         start=lp == 0, stop=lp == 7)
            last.then_inc(w1_used, 1)

        def compress_first(pe, kind):
            w1 = view(ring[kind], 16, P)
            pe.wait_ge(in_cmp[0], 16 * NPAGE)
            if kind:
                pe.wait_ge(first_read, 1)
            else:
                pe.wait_ge(pab_ready, 1)
            for half in range(2):
                for lp in range(8):
                    last = pe.matmul(bank(7)[:, 2 * P * half:2 * P * (half + 1)], w1[:, 8 * half + lp, :],
                                     page_cmp[0][:, :, P * kind + 16 * lp:P * kind + 16 * lp + 16],
                                     start=lp == 0, stop=lp == 7)
            last.then_inc(first_done, 1)

        def first_halves(act, kind):
            act.wait_ge(first_done, kind + 1)
            for half in range(2):
                last = act.activation(cab0[:, kind, half, :].rearrange("p (k g c) -> p k g c", k=2, g=NPAGE),
                                      bank(7)[:, 2 * P * half:2 * P * (half + 1)]
                                      .rearrange("p (g k c) -> p k g c", k=2, g=NPAGE), ACT.Copy)
            last.then_inc(first_read, 1)

        def compressed_first(pe):
            pe.wait_ge(hid_ready, 1)
            for kv in range(NKV):
                pe.matmul(bank(7)[64 * kv:64 * kv + 64, 0:NCB], C["w2"][:, 0, :], chid[:, 0, kv, 0:NCB],
                          start=True, stop=True)
            for kv in range(NKV):
                last = pe.matmul(bank(7)[0:NCB, P + 64 * kv:P + 64 * kv + 64], chid[:, 1, kv, 0:NCB], C["w2"][:, 1, :],
                                 start=True, stop=True)
            last.then_inc(kvc_done, 1)

        def chunks_of_prompt(dve):
            dve.wait_ge(act_out, CV + 1)
            for kind in range(2):
                for kv in range(NKV):
                    src_ = proj[64 * kv:64 * kv + 64, CK + kind, 0:TP].rearrange("p (c l two) -> p two l c", two=2, l=8)
                    for two in range(2):
                        dve.tensor_copy(xtp[64 * two:64 * two + 64, kind, :, 32 * kv:32 * kv + 32], src_[:, two, :, :])
                last = dve.tensor_copy(xtp[:, kind, :, 64:66],
                                       C["pe"][:, kind, :].rearrange("p (half l) -> p l half", half=2))
            last.then_inc(xtp_ready, 1)

        def block_sums_of_prompt(dve, own):
            dve.wait_ge(pab_ready, 1)
            own(dve.tensor_tensor(pebias, pab[:, :, 0, 64], pab[:, :, 1, 65], ALU.add))
            for kind in range(2):
                part = pab[:, kind, :, 0:64].rearrange("p h (k c) -> p h k c", k=2)
                dve.tensor_tensor(phid[:, kind, :, 0:NCP], part[:, 0, :, 0:NCP], part[:, 1, :, 1:NCP + 1], ALU.add)\
                    .then_inc(psum_ready, 1)

        def pe_nsa_prompt(pe):
            mm = pe.matmul
            pe.wait_ge(mix_mem, 5)
            pe.wait_ge(act_out, NSA_T)
            compress_prompt(pe)
            for j in range(4):
                pe.transpose(bank(0)[:, 48 * j:48 * j + 36], proj[0:36, GT, P * j:P * (j + 1)], ident[0:36, 0:36])
            pe.transpose(bank(0)[0:TS, 192:228], proj[0:36, GT, TP:TT_], ident[0:36, 0:36])
            for br, tile in enumerate((SV, WV)):
                for j in range(4):
                    last = pe.transpose(bank(1 + br)[:, P * j:P * (j + 1)], proj[:, tile, P * j:P * (j + 1)], ident)
            last.then_inc(vg_done, 1)
            compress_first(pe, 0)
            pe.wait_ge(phid_ready, 2)
            for kv in range(NKV):
                mm(bank(6)[64 * kv:64 * kv + 64, 0:NCP], C["w2"][:, 0, :], phid[:, 0, kv, 0:NCP], start=True, stop=True)
            for kv in range(NKV):
                last = mm(bank(5)[0:NCP, 64 * kv:64 * kv + 64], phid[:, 1, kv, 0:NCP], C["w2"][:, 1, :],
                          start=True, stop=True)
            last.then_inc(pkv_done, 1)
            compress_first(pe, 1)
            pe.wait_ge(pkv_ready, 1)
            pe.wait_ge(kcp_zeroed, 1)
            pe.wait_ge(vg_ready, 1)

            def scores(n):
                g, qt = unit(n)
                pe.wait_ge(qs_ready, g + 1)
                if n:
                    pe.wait_ge(ps_read, n)
                nk = P * (qt + 1)
                for br, tile in enumerate((SK, WK)):
                    for kv in range(NKV):
                        r = slice(64 * kv, 64 * kv + 64)
                        last = mm(bank(2 * br + kv)[:, 0:nk], qs[g % 3][r, P * qt:P * (qt + 1)], proj[r, tile, 0:nk],
                                  start=True, stop=True)
                    if br == 0:
                        last.then_inc(ps_done, 1)
                mm(bank(4)[:, 0:2 * NCP], qs[g % 3][:, P * qt:P * (qt + 1)], kcp, start=True, stop=True)\
                    .then_inc(ps_done, 1)

            def values(n):
                g, qt = unit(n)
                pe.wait_ge(pp_ready, n + 1)

                def turn(q):
                    pt = bank(5 + (groups(n) + q) % 2)
                    if groups(n) + q > 1:
                        pe.wait_ge(pt_ready, groups(n) + q - 1)
                    if q <= qt:
                        for r in range(4):
                            last = pe.transpose(pt[:, P * r:P * (r + 1)], s_sb[n % 3][:, r, P * q:P * (q + 1)], ident)
                    else:
                        for kv in range(NKV):
                            last = pe.transpose(pt[0:NCP, P * kv:P * (kv + 1)], scp[n % 3][:, kv, 0:NCP], ident)
                    last.then_inc(pt_done, 1)

                turn(0)
                if n:
                    pe.wait_ge(prompt_done, n)
                for q in range(qt + 2):
                    if q <= qt:
                        turn(q + 1)
                    if q == qt and n < 21:
                        scores(n + 3)
                    pe.wait_ge(pt_ready, groups(n) + q + 1)
                    for kv in range(NKV):
                        o = bank(7)[64 * kv:64 * kv + 64, 0:P]
                        if q <= qt:
                            for br in range(2):
                                mm(o, vn[:, br, q, 64 * kv:64 * kv + 64], ptp[(groups(n) + q) % 3][:, 2 * br + kv, :],
                                   start=q == br == 0, stop=False)
                        else:
                            last = mm(o, vcp[:, 64 * kv:64 * kv + 64], ptc[:, kv, :], start=False, stop=True)
                last.then_inc(po_done, 1)

            scores(0)
            compressed_first(pe)
            scores(1)
            scores(2)
            for n in range(24):
                values(n)

        def act_nsa_prompt(act, own):
            f = act.activation
            act.wait_ge(vg_done, 1)
            f(gnat, view(bank(0)[:, 0:192], 4, 48)[:, :, 0:36], ACT.Sigmoid)
            f(gsamp, bank(0)[0:TS, 192:228], ACT.Sigmoid)
            for br in range(2):
                last = f(vn[:, br, :, :].rearrange("p j c -> p (j c)"), bank(1 + br), ACT.Copy)
            last.then_inc(vg_ready, 1)
            for kind in range(2):
                act.wait_ge(psum_ready, kind + 1)
                f(phid[:, kind, :, 0:NCP], phid[:, kind, :, 0:NCP], ACT.Silu, bias=pebias[:, kind:kind + 1])\
                    .then_inc(phid_ready, 1)
            first_halves(act, 0)
            act.wait_ge(pkv_done, 1)
            act.wait_ge(kcp_zeroed, 1)
            for kv in range(NKV):
                r = slice(64 * kv, 64 * kv + 64)
                f(kcp[r, kv, :], bank(6)[r, 0:NCP], ACT.Copy)
            f(vcp, bank(5)[0:NCP, 0:P], ACT.Copy).then_inc(pkv_ready, 1)

            def queries(g):
                if g >= 3:
                    act.wait_ge(ps_done, 2 * scored(g - 3))
                f(qs[g % 3], proj[:, Q0 + g, 0:TP], ACT.Copy, scale=HD ** -0.5).then_inc(qs_ready, 1)

            def exps(n, rows):
                nk, st = P * (unit(n)[1] + 1), stp[:, n % 3, :]
                act.wait_ge(pmax_ready, n + 1)
                for r in rows:
                    f(s_sb[n % 3][:, r, 0:nk], s_sb[n % 3][:, r, 0:nk], ACT.Exp, bias=st[:, r:r + 1],
                      accum_out=st[:, 8 + r:9 + r])
                for kv in range(NKV if 3 in rows else 0):
                    last = f(scp[n % 3][:, kv, 0:NCP], scp[n % 3][:, kv, 0:NCP], ACT.Exp, bias=st[:, 4 + kv:5 + kv],
                             accum_out=st[:, 12 + kv:13 + kv])
                if 3 in rows:
                    last.then_inc(pexp_ready, 1)

            def turned(n, q):
                pt = bank(5 + (groups(n) + q) % 2)
                act.wait_ge(pt_done, groups(n) + q + 1)
                if q <= unit(n)[1]:
                    f(ptp[(groups(n) + q) % 3].rearrange("p r q -> p (r q)"), pt, ACT.Copy).then_inc(pt_ready, 1)
                else:
                    f(ptc.rearrange("p r q -> p (r q)"), pt[0:NCP, 0:2 * P], ACT.Copy).then_inc(pt_ready, 1)

            queries(0)
            first_halves(act, 1)
            hidden_units(act, 0, cab0)
            act.wait_ge(hid_ready, 1)
            for g in (1, 2):
                queries(g)
            exps(0, range(4))
            compressed_out(act, 0, bank(7))
            exps(1, range(4))
            for n in range(24):
                qt = unit(n)[1]
                for q in range(qt + 2):
                    turned(n, q)
                    if q == 1 and n in (4, 6, 12):
                        queries({4: 3, 6: 4, 12: 5}[n])
                if n < 22:
                    exps(n + 2, range(4))

        def dve_nsa_prompt(dve, own):
            tt, ts, stt = dve.tensor_tensor, dve.tensor_scalar, dve.scalar_tensor_tensor
            dve.wait_ge(in_prompt_t, 16)
            dve.wait_ge(vg_ready, 1)

            def biased(n):
                g, qt = unit(n)
                nk, st, s, sc = P * (qt + 1), stp[:, n % 3, :], s_sb[n % 3], scp[n % 3]
                dve.wait_ge(ps_done, 2 * n + 1)
                if n >= 3:
                    dve.wait_ge(pt_done, groups(n - 2))
                slope = lambda kv: PT["nslope"][:, 6 * kv + g:6 * kv + g + 1]
                for r in range(4):
                    if r == 2:
                        dve.wait_ge(ps_done, 2 * n + 2)
                    stt(out=s[:, r, 0:nk], in0=PT["dist"][:, TP - nk:TP], scalar=slope(r % 2), in1=bank(r)[:, 0:nk],
                        op0=ALU.mult, op1=ALU.add)
                for kv in range(NKV):
                    last = stt(out=sc[:, kv, 0:NCP], in0=PT["cdist"][:, qt, :], scalar=slope(kv),
                               in1=bank(4)[:, NCP * kv:NCP * (kv + 1)], op0=ALU.mult, op1=ALU.add)
                last.then_inc(ps_read, 1)
                dve.wait_ge(ps_read, n + 1)
                dve.tensor_reduce(st[:, 0:4], s[:, :, 0:nk], AX.X, ALU.max, negate=True)
                dve.tensor_reduce(st[:, 4:6], sc[:, :, 0:NCP], AX.X, ALU.max, negate=True)\
                    .then_inc(pmax_ready, 1)

            def scaled(n):
                g, qt = unit(n)
                nk, st, s, sc = P * (qt + 1), stp[:, n % 3, :], s_sb[n % 3], scp[n % 3]
                dve.wait_ge(pexp_ready, n + 1)
                own(dve.reciprocal(st[:, 16:22], st[:, 8:14]))
                own(tt(st[:, 16:22], st[:, 16:22], gnat[:, qt, 6 * g:6 * g + 6], ALU.mult))
                own(ts(st[:, 20:22], st[:, 20:22], PT["cvis"][:, qt:qt + 1], None, ALU.mult))
                tt(s[:, :, 0:nk], s[:, :, 0:nk], bcast(st[:, 16:20], P, 4, nk), ALU.mult)
                tt(sc[:, :, 0:NCP], sc[:, :, 0:NCP], bcast(st[:, 20:22], P, 2, NCP), ALU.mult)\
                    .then_inc(pp_ready, 1)

            def output(n):
                dve.wait_ge(po_done, n + 1)
                g, qt = unit(n)
                dve.tensor_copy(mixT[:, g, P * qt:P * (qt + 1)], bank(7)[:, 0:P]).then_inc(prompt_done, 1)

            biased(0)
            biased(1)
            scaled(0)
            biased(2)
            for n in range(24):
                if n < 23:
                    scaled(n + 1)
                output(n)
                if n < 21:
                    biased(n + 3)

        def pe_nsa_sample(pe):
            mm = pe.matmul
            w1 = [view(ring[kind], 16, P) for kind in range(2)]

            def compress(s, quarters):
                if 0 in quarters:
                    pe.wait_ge(in_cmp[s % 2], 16 * NPAGE * (s // 2 + 1))
                    pe.wait_ge(vnew_ready, s)
                    pe.wait_ge(kvc_ready, s)
                for quarter in quarters:
                    kind, half = quarter // 2, quarter % 2
                    for lp in range(8):
                        last = mm(bank(6 + kind)[:, 2 * P * half:2 * P * (half + 1)], w1[kind][:, 8 * half + lp, :],
                                  page_cmp[s % 2][:, :, P * kind + 16 * lp:P * kind + 16 * lp + 16],
                                  start=lp == 0, stop=lp == 7)
                if 3 in quarters:
                    last.then_inc(w1_used, 1)

            def compressed(s):
                pe.wait_ge(hid_ready, s + 1)
                for kv in range(NKV):
                    mm(bank(6)[64 * kv:64 * kv + 64, 0:NCB], C["w2"][:, 0, :], chid[:, 0, kv, 0:NCB],
                       start=True, stop=True)
                for kv in range(NKV):
                    last = mm(bank(6)[0:NCB, P + 64 * kv:P + 64 * kv + 64], chid[:, 1, kv, 0:NCB], C["w2"][:, 1, :],
                              start=True, stop=True)
                last.then_inc(kvc_done, 1)

            def new_rows(s):
                pe.wait_ge(qb_ready, s + 1)
                pe.wait_ge(cab_ready, s)
                for br in range(2):
                    pe.transpose(bank(7)[0:DT, P * br:P * (br + 1)], vst[:, br, :], ident)
                mm(bank(7)[0:ROWS, 256:292], ST["pick"][0:TS, s, :], gsamp, start=True, stop=True)\
                    .then_inc(vnew_done, 1)

            def scores(s):
                pe.wait_ge(kvc_ready, s + 1)
                pe.wait_ge(in_pages[s % 2], 16 * (NPAGE + 1) * (s // 2 + 1))
                if s:
                    pe.wait_ge(seq_done, s)
                pg, kn = page_kv[s % 2], slice(TP + DT * s, TP + DT * (s + 1))
                for half in range(2):
                    for b in range(2):
                        j = 8 * half + 4 * b
                        mm(bank(b)[ROWS * half:ROWS * (half + 1), :], qb, pg[:, j:j + 4, 0:P], start=True, stop=True)
                mm(bank(4)[0:ROWS, :], qb, wcache[s % 2][:, 0:WIN], start=True, stop=True)
                mm(bank(5)[0:ROWS, 0:DT], qb, proj[:, SK, kn], start=True, stop=True)
                mm(bank(5)[0:ROWS, DT:2 * DT], qb, proj[:, WK, kn], start=True, stop=True)
                mm(bank(5)[0:ROWS, 16:16 + NCB], qb, kc[:, s % 2, 0:NCB], start=True, stop=True).then_inc(sc_done, 1)

            def importance(s):
                pe.wait_ge(cp_ready, s + 1)
                mm(bank(5)[:, 0:NCB], ST["same"][0:ROWS, :], low[:, S_CMP:S_CMP + NCB], start=True, stop=True)\
                    .then_inc(imp_done, 1)

            i64 = ident[0:ROWS, 0:ROWS]

            def turn_window(s):
                pe.wait_ge(slc_biased, s + 1)
                for j in range(4):
                    pe.transpose(bank(3)[:, ROWS * j:ROWS * (j + 1)], low[:, S_WIN + P * j:S_WIN + P * (j + 1)], i64)
                pe.transpose(bank(3)[0:DT, 4 * ROWS:5 * ROWS], low[:, S_WNEW:S_WNEW + DT], i64).then_inc(spt_done, 1)

            o = bank(0)[:, 0:ROWS]

            def window_values(s):
                pe.wait_ge(spt_ready, 4 * s + 1)
                for j in range(4):
                    mm(o, wcache[s % 2][:, WIN + P * j:WIN + P * (j + 1)], pts[:, 16 + j, :], start=j == 0, stop=False)
                mm(o, vnew[:, 1, :], ptn[:, 1, :], start=False, stop=False)

            def values(s):
                pe.wait_ge(sp_ready, s + 1)
                for b in range(2):
                    for j in range(4):
                        last = pe.transpose(bank(1 + b)[:, P * j:P * (j + 1)],
                                            ssc[:, P * (4 * b + j):P * (4 * b + j + 1)], ident)
                    last.then_inc(spt_done, 1)
                pe.transpose(bank(4)[0:NCB, 0:ROWS], low[:, S_CMP:S_CMP + NCB], i64)
                pe.transpose(bank(4)[0:DT, 64:128], low[:, S_NEW:S_NEW + DT], i64).then_inc(spt_done, 1)
                for j in range(8):
                    if j in (0, 4):
                        pe.wait_ge(spt_ready, 4 * s + j // 4 + 2)
                    for half in range(2):
                        mm(o, page_kv[s % 2][:, 8 * half + j, P:2 * P], pts[:, 2 * j + half, :], start=False, stop=False)
                pe.wait_ge(spt_ready, 4 * s + 4)
                mm(o, vc[:, s % 2, :], ptcs, start=False, stop=False)
                mm(o, vnew[:, 0, :], ptn[:, 0, :], start=False, stop=True).then_inc(so_done, 1)

            pe.wait_ge(prompt_done, 24)
            pe.wait_ge(in_sample_t, 16)
            for s in range(NS):
                more = s < NS - 1
                new_rows(s)
                scores(s)
                if more:
                    compress(s + 1, (0,))
                importance(s)
                if more:
                    compress(s + 1, (1,))
                turn_window(s)
                if more:
                    compress(s + 1, (2,))
                window_values(s)
                if more:
                    compress(s + 1, (3,))
                values(s)
                if more:
                    compressed(s + 1)

        def hidden_units(act, s, sums):
            f = act.activation
            for kind in range(2):
                act.wait_ge(hsum_ready, 2 * s + kind + 1)
                last = f(chid[:, kind, :, 0:NCB], sums[:, kind, 0, :].rearrange("p (k c) -> p k c", k=2)[:, :, 0:NCB],
                         ACT.Silu, bias=pebias[:, kind:kind + 1])
            last.then_inc(hid_ready, 1)

        def compressed_out(act, s, kvc):
            f = act.activation
            act.wait_ge(kvc_done, s + 1)
            f(kc[:, s % 2, 0:NCB], kvc[:, 0:NCB], ACT.Copy)
            f(vc[:, s % 2, :], kvc[0:NCB, P:2 * P], ACT.Copy).then_inc(kvc_ready, 1)

        def add_halves(dve, sums):
            for kind in range(2):
                h = [sums[:, kind, i, :].rearrange("p (k c) -> p k c", k=2) for i in range(2)]
                dve.tensor_tensor(h[0][:, :, 0:NCB], h[0][:, :, 0:NCB], h[1][:, :, 1:NCB + 1], ALU.add)\
                    .then_inc(hsum_ready, 1)

        def act_nsa_sample(act, own):
            f = act.activation

            def halves(s):
                act.wait_ge(w1_used, s + 1)
                for kind in range(2):
                    act.wait_ge(hsum_ready, 2 * s)
                    for half in range(2):
                        last = f(cab[:, kind, half, :].rearrange("p (k g c) -> p k g c", k=2, g=NPAGE),
                                 bank(6 + kind)[:, 2 * P * half:2 * P * (half + 1)]
                                 .rearrange("p (g k c) -> p k g c", k=2, g=NPAGE), ACT.Copy)
                last.then_inc(cab_ready, 1)

            def hidden(s):
                act.wait_ge(kvc_done, s)
                hidden_units(act, s, cab)
                compressed_out(act, s, bank(6))

            for s in range(NS):
                act.wait_ge(vnew_done, s + 1)
                if s:
                    act.wait_ge(seq_done, s)
                f(vnew.rearrange("p b c -> p (b c)"), bank(7)[0:DT, 0:2 * P], ACT.Copy)
                f(grt, bank(7)[0:ROWS, 256:292], ACT.Copy).then_inc(vnew_ready, 1)
                act.wait_ge(cmax_ready, s + 1)
                cmp_ = low[:, S_CMP:S_CMP + NCB]
                f(cmp_, cmp_, ACT.Exp, bias=stl[:, 0:1], accum_out=stl[:, 1:2]).then_inc(cexp_ready, 1)
                w = low[:, S_WIN:S_WIN + WIN + DT]
                act.wait_ge(wmax_ready, s + 1)
                f(w, w, ACT.Exp, bias=stl[:, 4:5], accum_out=stl[:, 6:7]).then_inc(wexp_ready, 1)
                act.wait_ge(spt_done, 4 * s + 1)
                f(pts[:, 16:20, :].rearrange("p j r -> p (j r)"), bank(3)[:, 0:4 * ROWS], ACT.Copy)
                f(ptn[:, 1, :], bank(3)[0:DT, 4 * ROWS:5 * ROWS], ACT.Copy).then_inc(spt_ready, 1)
                act.wait_ge(smax_ready, s + 1)
                f(ssc[:, 0:PAST2 + DT], ssc[:, 0:PAST2 + DT], ACT.Exp, bias=sst[:, 3:4], accum_out=sst[:, 5:6])\
                    .then_inc(sexp_ready, 1)
                if s < NS - 1:
                    halves(s + 1)
                for b in range(2):
                    act.wait_ge(spt_done, 4 * s + b + 2)
                    f(pts[:, 8 * b:8 * b + 8, :].rearrange("p j r -> p (j r)"), bank(1 + b), ACT.Copy)\
                        .then_inc(spt_ready, 1)
                act.wait_ge(spt_done, 4 * s + 4)
                f(ptcs, bank(4)[0:NCB, 0:ROWS], ACT.Copy)
                f(ptn[:, 0, :], bank(4)[0:DT, 64:128], ACT.Copy).then_inc(spt_ready, 1)
                if s < NS - 1:
                    hidden(s + 1)

        def dve_nsa_sample(dve, own):
            tt, ts = dve.tensor_tensor, dve.tensor_scalar
            own(dve.memset(qb, 0.0))

            def queries(s):
                if s:
                    dve.wait_ge(sc_done, s)
                kn = slice(TP + DT * s, TP + DT * (s + 1))
                for kv in range(NKV):
                    r = slice(64 * kv, 64 * kv + 64)
                    ts(qb[r, 32 * kv:32 * kv + 24].rearrange("p (g t) -> p g t", g=NG), proj[r, Q0:Q0 + NG, kn],
                       HD ** -0.5, None, ALU.mult)
                dve.tensor_copy(vst[:, 0, :], proj[:, SV, kn])
                dve.tensor_copy(vst[:, 1, :], proj[:, WV, kn]).then_inc(qb_ready, 1)

            def half_sum(s):
                dve.wait_ge(cab_ready, s)
                add_halves(dve, cab)

            queries(0)
            for s in range(NS):
                if s == 0:
                    dve.wait_ge(in_sample_t, 16)
                cmp_ = low[:, S_CMP:S_CMP + NCB]
                dve.wait_ge(sc_done, s + 1)
                own(tt(cmp_, bank(5)[0:ROWS, 16:16 + NCB], ST["b_cmp"][0:ROWS, :], ALU.add))
                dve.tensor_reduce(stl[:, 0:1], cmp_, AX.X, ALU.max, negate=True).then_inc(cmax_ready, 1)
                win = low[:, S_WIN:S_WIN + WIN + DT]
                tt(low[:, S_NEW:S_NEW + DT], bank(5)[0:ROWS, 0:DT], ST["b_new"][0:ROWS, :], ALU.add)
                dve.tensor_copy(high[:, S_NEW:S_NEW + DT], ST["b_new"][ROWS:P, :])
                tt(low[:, S_WNEW:S_WNEW + DT], bank(5)[0:ROWS, DT:2 * DT], ST["b_new"][0:ROWS, :], ALU.add)
                own(tt(win[:, 0:WIN], bank(4)[0:ROWS, :], ST["b_win"][0:ROWS, :], ALU.add))
                dve.tensor_reduce(stl[:, 4:5], win, AX.X, ALU.max, negate=True).then_inc(wmax_ready, 1)
                dve.wait_ge(cexp_ready, s + 1)
                own(dve.reciprocal(stl[:, 2:3], stl[:, 1:2]))
                ts(cmp_, cmp_, stl[:, 2:3], None, ALU.mult).then_inc(cp_ready, 1)
                dve.wait_ge(vnew_ready, s + 1)
                own(tt(grt, grt, ST["head"][0:ROWS, :], ALU.mult))
                own(dve.tensor_reduce(gr, grt.rearrange("p (g b k) -> p b g k", g=NG, b=3), AX.XY, ALU.add))
                dve.wait_ge(wexp_ready, s + 1)
                own(dve.reciprocal(stl[:, 9:10], stl[:, 6:7]))
                own(tt(stl[:, 9:10], stl[:, 9:10], gr[:, 1:2], ALU.mult))
                ts(win, win, stl[:, 9:10], None, ALU.mult)
                tt(ssc[:, 0:PAST2], banks(0, 2), ST["b_slc"], ALU.add).then_inc(slc_biased, 1)
                if s < NS - 1:
                    queries(s + 1)
                dve.wait_ge(imp_done, s + 1)
                dve.memset(impc[:, NCB:P], 0.0)
                own(dve.tensor_copy(impc[:, 0:NCB], bank(5)[:, 0:NCB]))
                own(dve.tensor_reduce(imp, view(impc, NSLC, 4), AX.X, ALU.add))
                own(tt(imp[:, 1:NSLC], imp[:, 1:NSLC], view(impc, NSLC, 4)[:, 0:NSLC - 1, 3], ALU.add))
                dve.tensor_copy(imph[0:ROWS, :], imp[0:ROWS, 0:NSLC // 2])
                own(dve.tensor_copy(imph[ROWS:P, :], imp[ROWS:P, NSLC // 2:NSLC]))
                c, m = NSLC - 2, NSLC // 2
                gt, eq = view(rank[:, 0:m * c], m, c), view(rank[:, m * c:2 * m * c], m, c)
                each, other = bcast(imph, P, m, c), imp[:, 1:1 + c].unsqueeze(1).to_broadcast([P, m, c])
                tt(gt, other, each, ALU.is_gt)
                own(tt(eq, other, each, ALU.is_equal))
                own(tt(eq, eq, ST["lower"], ALU.mult))
                own(tt(gt, gt, eq, ALU.add))
                own(dve.tensor_reduce(sel, gt, AX.X, ALU.add))
                own(ts(sel, sel, float(TOPN - 3), None, ALU.is_ge))
                own(tt(sel, sel, ST["drop"], ALU.mult))
                past = view(ssc[:, 0:PAST2], m, 64)
                own(tt(past, past, bcast(sel, P, m, 64), ALU.add))
                own(dve.tensor_reduce(sst[:, 3:4], ssc[:, 0:PAST2 + DT], AX.X, ALU.max, negate=True))
                own(dve.tensor_copy(stl[:, 7:8], sst[ROWS:P, 3:4]))
                own(tt(stl[:, 3:4], stl[:, 3:4], stl[:, 7:8], ALU.min))
                dve.tensor_copy(sst[ROWS:P, 3:4], stl[:, 3:4]).then_inc(smax_ready, 1)
                ts(cmp_, cmp_, gr[:, 2:3], None, ALU.mult)
                dve.wait_ge(sexp_ready, s + 1)
                own(dve.tensor_copy(stl[:, 7:8], sst[ROWS:P, 5:6]))
                own(tt(stl[:, 7:8], stl[:, 7:8], stl[:, 5:6], ALU.add))
                own(dve.reciprocal(stl[:, 8:9], stl[:, 7:8]))
                own(tt(stl[:, 8:9], stl[:, 8:9], gr[:, 0:1], ALU.mult))
                own(dve.tensor_copy(sst[ROWS:P, 8:9], stl[:, 8:9]))
                ts(ssc[:, 0:PAST2 + DT], ssc[:, 0:PAST2 + DT], sst[:, 8:9], None, ALU.mult).then_inc(sp_ready, 1)
                if s < NS - 1:
                    half_sum(s + 1)
                dve.wait_ge(so_done, s + 1)
                for kv in range(NKV):
                    r = slice(64 * kv, 64 * kv + 64)
                    last = dve.tensor_copy(mixT[r, 0:NG, TP + DT * s:TP + DT * (s + 1)],
                                           bank(0)[r, 32 * kv:32 * kv + 24].rearrange("p (g t) -> p g t", g=NG))
                last.then_inc(seq_done, 1)

        CHUNKS = [(P, slice(P * i, P * (i + 1)), 3, 3) for i in range(4)] + [(TS, slice(TP, TT_), 1, 0)]
        HALVES = ((0, 3), (3, 6))
        BA_, BB, BC, BD = (3, 4), (5, 6), (0, 1), (2, 7)

        class Inverse:

            def __init__(self):
                self.pe = self.act = self.dve = 0

        def lengths(pe, c):
            if c == 0:
                pe.wait_ge(gexp_pre, 1)
            pe.wait_ge(cn_sq, c + 1)
            for ci, (R, cols, _, _) in enumerate(CHUNKS):
                at = 5 * GH * (c // GH) + GH * ci + c % GH
                last = pe.matmul(bank(7)[0:R, at:at + 1], sq[:, c % 2, cols], ones[:, 0:1], start=True, stop=True)
            last.then_inc(cn_ss, 1)

        def gate_inputs(pe):
            pe.wait_ge(act_out, evac_base["gdn_in"] + BA + 1)
            for j in range(4):
                pe.transpose(bank(7)[:, 304 + 16 * j:316 + 16 * j], gproj[0:12, BA, P * j:P * (j + 1)],
                             ident[0:12, 0:12])
            pe.transpose(bank(7)[0:TS, 368:380], gproj[0:12, BA, TP:TT_], ident[0:12, 0:12]).then_inc(ba_done, 1)

        def gate_sums(pe):
            pe.wait_ge(gates_ready, 1)
            pe.wait_ge(in_gdn_t, 16)
            mm = pe.matmul
            mm(bank(7)[:, 384:408], GC["cum"], gat[:, 0:4, :], start=True, stop=True)
            mm(bank(7)[:, 416:440], ones, gat[:, 0:4, :], start=True, stop=True)
            mm(bank(7)[0:TS, 408:414], GC["cum_s"][0:TS, :], gat[0:TS, 4, :], start=True, stop=True)
            mm(bank(7)[0:TS, 440:446], GC["all_s"][0:TS, :], gat[0:TS, 4, :], start=True, stop=True).then_inc(gt_done, 1)

        def gates_act(act, own):
            f = act.activation
            act.wait_ge(gate_pre, 1)
            own(f(nea, C["a_log"], ACT.Exp))
            own(f(spl, spl, ACT.Exp, scale=-1.0))
            f(spl, spl, ACT.Ln, bias=C["one"])
            f(beta, ban[:, :, 0:GH], ACT.Sigmoid).then_inc(gat_ready, 1)

        def decays_act(act):
            act.wait_ge(gexp_pre, 1)
            for t in (kde, egt):
                act.activation(t, t, ACT.Exp)
            act.activation(egc, gcn, ACT.Exp).then_inc(gexp_ready, 1)

        def from_bank7(dve, dst, at):
            dve.tensor_copy(dst[:, 0:4, :], view(bank(7)[:, at:at + 24], 4, GH))
            return dve.tensor_copy(dst[0:TS, 4, :], bank(7)[0:TS, at + 24:at + 30])

        def gates_dve(dve, own):
            dve.wait_ge(ba_done, 1)
            dve.tensor_copy(ban[:, 0:4, :], view(bank(7)[:, 304:368], 4, 16)[:, :, 0:12])
            own(dve.tensor_copy(ban[0:TS, 4, :], bank(7)[0:TS, 368:380]))
            a_ = ban[:, :, GH:2 * GH]
            dve.tensor_tensor(a_, a_, C["dt_bias"].unsqueeze(1).to_broadcast([P, 5, GH]), ALU.add).then_inc(ban_read, 1)
            dve.wait_ge(ban_read, 1)
            dve.tensor_scalar(gat, a_, 0.0, None, ALU.max)
            dve.scalar_tensor_tensor(out=spl, in0=a_, scalar=-1.0, in1=a_, op0=ALU.mult, op1=ALU.max)\
                .then_inc(gate_pre, 1)

        def lengths_dve(dve, own):
            dve.wait_ge(cn_ss, 2 * GH)
            dve.wait_ge(conv_done, 20)
            own(dve.memset(qn, 1.0))
            from_bank7(dve, qn, 0)
            own(from_bank7(dve, kr2, 5 * GH))
            own(dve.tensor_scalar(qn, qn, EPS, EPS * P, ALU.add, ALU.mult))
            own(dve.tensor_scalar(kr2, kr2, EPS, None, ALU.add))
            dve.reciprocal(kr2, kr2).then_inc(ks_read, 1)

        def gates_done_dve(dve, own):
            dve.wait_ge(gat_ready, 1)
            own(dve.tensor_tensor(gat, gat, spl, ALU.add))
            dve.scalar_tensor_tensor(out=gat, in0=gat, scalar=-1.0, in1=nea.unsqueeze(1).to_broadcast([P, 5, GH]),
                                     op0=ALU.mult, op1=ALU.mult).then_inc(gates_ready, 1)

        def gate_sums_dve(dve, own):
            dve.wait_ge(gt_done, 1)
            from_bank7(dve, gcn, 384)
            own(from_bank7(dve, egt, 416))
            dve.tensor_tensor(kde, egt, gcn, ALU.subtract).then_inc(gexp_pre, 1)

        def factors_dve(dve, own):
            tt = dve.tensor_tensor
            dve.wait_ge(kr_ready, 1)
            tt(br, beta, kr, ALU.mult)
            own(tt(br2, beta, kr2, ALU.mult))
            dve.wait_ge(gexp_ready, 1)
            tt(bex, br2, egc, ALU.mult).then_inc(bexp_ready, 1)

        def output_sums(pe, ci, to):
            pe.wait_ge(cn_sq, 2 * GH + ci + 1)
            R = CHUNKS[ci][0]
            for h in range(GH):
                last = pe.matmul(to[0:R, h:h + 1], osq[:, R * h:R * (h + 1)], ones[:, 0:1], start=True, stop=True)
            return last

        def spread_prompt(pe, c):
            pe.wait_ge(cn_rec, 1)
            if c >= 2:
                pe.wait_ge(cn_ready, c - 1)
            for ci, (R, cols, _, _) in enumerate(CHUNKS[0:4]):
                last = pe.matmul(bank(c % 2)[:, cols], rinv[:, ci, c:c + 1].to_broadcast([P, P]), ident,
                                 start=True, stop=True)
            last.then_inc(cn_bc, 1)

        def spread_samples(pe):
            pe.wait_ge(cn_rec, 2)
            for h in range(GH):
                last = pe.matmul(bank(2)[:, TS * (h + 1):TS * (h + 2)], rinv[0:TS, 4, h:h + 1].to_broadcast([TS, P]),
                                 ident[0:TS, 0:TS], start=True, stop=True)
            last.then_inc(cn_bc, 1)

        def pe_gdn(pe):
            mm = pe.matmul
            n = [Inverse(), Inverse()]
            pe.wait_ge(mix_mem, 10)
            pe.wait_ge(act_out, evac_base["gdn_in"] + GDN_T)
            pe.wait_ge(conv_done, 20)

            def product(x, pair, lhs, rhs, width, rows=P):
                h0, h1 = HALVES[x]
                for h in range(h0, h1):
                    last = mm(bank(pair[x])[0:rows, width * (h - h0):width * (h - h0 + 1)], lhs(h), rhs(h),
                              start=True, stop=True)
                return last

            def running_sums(ci):
                R = CHUNKS[ci][0]
                pe.wait_ge(ug_ready, ci + 1)
                pe.wait_ge(nwt_ready, 2 * ci)
                for x, (h0, h1) in enumerate(HALVES):
                    last = mm(bank(BD[x])[:, 0:R * (h1 - h0)], ones[0:R, :], ug[0:R, h0:h1, 0:R], start=True, stop=True)
                last.then_inc(gc_done, 1)

            running_sums(0)
            for ci, (R, cols, squares, merges) in enumerate(CHUNKS):
                kT = lambda h: gproj[:, GK + h, cols]
                qT = lambda h: gproj[:, GQ + h, cols]
                pe.wait_ge(vn_ready, 2 * ci)
                for x in range(2):
                    product(x, BA_, kT, kT, R, R)
                pe.wait_ge(oc_ready, 2 * ci)
                for x in range(2):
                    last = product(x, BB, qT, kT, R, R)
                    if x and ci:
                        last = output_sums(pe, ci - 1, bank(BB[1])[:, 3 * P:])
                    last.then_inc(kq_done, 1)
                pe.wait_ge(sup_done, 2 * ci)
                pe.wait_ge(dexp_ready, ci + 1)
                for x, (h0, h1) in enumerate(HALVES):
                    for h in range(h0, h1):
                        y = slice(P * (h - h0), P * (h - h0 + 1))
                        pe.transpose(bank(BC[x])[0:R, y], kT(h), ident)
                        last = pe.transpose(bank(BD[x])[0:R, y], gproj[:, GV + h, cols], ident)
                    last.then_inc(kv_done, 1)
                for x, (h0, h1) in enumerate(HALVES):
                    pe.wait_ge(bm_ready, 2 * ci + x + 1)
                    for h in range(h0, h1):
                        y = slice(R * (h - h0), R * (h - h0 + 1))
                        pe.transpose(bank(BA_[x])[0:R, y], bm[0:R, h, 0:R], ident[0:R, 0:R])
                        last = pe.transpose(bank(BB[x])[0:R, y], qd[0:R, h, 0:R], ident[0:R, 0:R])
                    last.then_inc(tr_done, 1)
                sub = lambda t: (lambda h: t[0:R, h, 0:R])
                for x in range(2):
                    n[x].dve += 1
                for k in range(squares):
                    for x in range(2):
                        pe.wait_ge(inv_dve[x], n[x].dve)
                        product(x, BA_, sub(pwt), sub(pw), R, R).then_inc(inv_pe[x], 1)
                        if not k:
                            pe.wait_ge(qt_ready, 2 * ci + x + 1)
                        if k < squares - 1:
                            product(x, BB, sub(pw), sub(pwt), R, R).then_inc(inv_pe[x], 1)
                    for x in range(2):
                        n[x].act += 1
                        n[x].dve += 1
                        if not k:
                            pe.wait_ge(tr_ready, 2 * ci + x + 1)
                        pe.wait_ge(inv_act[x], n[x].act)
                        product(x, BC, sub(pw), sub(tt_), R, R).then_inc(inv_pe[x], 1)
                for x in range(2 if merges else 0):
                    pe.wait_ge(inv_dve[x], n[x].dve)
                    h0, h1 = HALVES[x]
                    for h in range(h0, h1):
                        last = pe.transpose(bank(BB[x])[:, P * (h - h0):P * (h - h0 + 1)], tt_[:, h, :], ident)
                    last.then_inc(inv_pe[x], 1)
                    n[x].act += 1
                for k in range(merges):
                    for x in range(2):
                        if k:
                            pe.wait_ge(inv_dve[x], n[x].dve)
                        product(x, BA_, sub(pw), sub(tt_), R, R).then_inc(inv_pe[x], 1)
                    for x in range(2):
                        n[x].act += 1
                        pe.wait_ge(inv_act[x], n[x].act)
                        if k:
                            n[x].dve += 1
                            pe.wait_ge(inv_dve[x], n[x].dve)
                        last = product(x, BC, sub(tn), sub(zz), R, R)
                        if k < merges - 1:
                            last = product(x, BB, sub(zz), sub(tn), R, R)
                        last.then_inc(inv_pe[x], 1)
                        n[x].dve += 1
                for x in range(2):
                    pe.wait_ge(inv_dve[x], n[x].dve)
                    pe.wait_ge(vb_ready, 2 * ci + x + 1)
                    product(x, BD, lambda h: kbg[0:R, h, :], sub(tt_), R).then_inc(wt_done, 1)
                if R == P:
                    for x, (h0, h1) in enumerate(HALVES):
                        pe.wait_ge(nwt_ready, 2 * ci + x + 1)
                        for h in range(h0, h1):
                            o = bank(BA_[x])[:, P * (h - h0):P * (h - h0 + 1)]
                            mm(o, tt_[:, h, :], vb[:, h, :], start=True, stop=False)
                            last = mm(o, nwt[:, h, :], st_p[:, h, :], start=False, stop=True)
                        last.then_inc(vn_done, 1)
                    running_sums(ci + 1)
                    for x, (h0, h1) in enumerate(HALVES):
                        pe.wait_ge(vn_ready, 2 * ci + x + 1)
                        for h in range(h0, h1):
                            o = bank(BB[x])[:, P * (h - h0):P * (h - h0 + 1)]
                            mm(o, st_p[:, h, :], qg[:, h, :], start=True, stop=False)
                            last = mm(o, vnw[:, h, :], qt_[:, h, :], start=False, stop=True)
                        last.then_inc(oc_done, 1)
                        product(x, BC, lambda h: kdec[:, h, :], lambda h: vnw[:, h, :], P).then_inc(sup_mm, 1)
                    continue

                def from_state(h):
                    pe.wait_ge(in_state[h], 16)
                    pe.wait_ge(wq_ready, h + 1)
                    v = bank(3 + h % 2)[0:2 * TS, 0:P]
                    for s in range(NS):
                        mm(v, wq[:, h % 2, 2 * TS * s:2 * TS * (s + 1)], sg[h][:, s // 4, s % 4, :],
                           start=s == 0, stop=False,
                           skip_group_check=True)
                    mm(v[0:TS, :], tt_[0:R, h, 0:R], vb[0:R, h, :], start=False, stop=True, skip_group_check=True)\
                        .then_inc(vns_done, 1)

                def from_new_values(h):
                    pe.wait_ge(vns_ready, h + 1)
                    last = mm(bank(5)[:, TS * h:TS * (h + 1)], vo[:, h % 2, :], qt_[0:2 * TS, h, 0:TS],
                              start=True, stop=True)
                    if h == GH - 1:
                        last.then_inc(oc_done, 1)
                        output_sums(pe, 4, bank(2)).then_inc(cn_ss, 1)
                    pe.wait_ge(vx_ready, h + 1)
                    if h:
                        pe.wait_ge(snew_ready, h)
                    for b in range(2):
                        last = mm(bank(6 + b), kdec[0:R, h, :], vx[:, 4 * b:4 * b + 4, :], start=True, stop=True)
                    last.then_inc(snew_mm, 1)

                from_state(0)
                for h in range(GH):
                    if h + 1 < GH:
                        from_state(h + 1)
                    spread_prompt(pe, h)
                    from_new_values(h)
            spread_samples(pe)
            pe.wait_ge(snew_ready, GH)
            pe.wait_ge(cn_ready, GH + 1)

        def column_squares(act, first, tiles, src_):
            for c in tiles:
                if c >= 2:
                    act.wait_ge(cn_ss, first + c - 1)
                act.activation(sq[:, c % 2, :], src_(c), ACT.Square).then_inc(cn_sq, 1)

        def act_gdn(act, own):
            f = act.activation
            n = [Inverse(), Inverse()]

            def decays(ci):
                R = CHUNKS[ci][0]
                act.wait_ge(gc_ready, ci + 1)
                f(dec[0:R, :, 0:R], dec[0:R, :, 0:R], ACT.Exp, scale=-1.0)
                for x, (h0, h1) in enumerate(HALVES):
                    last = f(egr[:, h0:h1, 0:R], view(bank(BD[x])[:, 0:R * (h1 - h0)], h1 - h0, R), ACT.Exp)
                last.then_inc(dexp_ready, 1)

            def output_squares(ci):
                R, cols = CHUNKS[ci][0:2]
                act.wait_ge(oc_ready, min(2 * ci + 2, 9))
                act.wait_ge(kq_done, 2 * ci + 2)
                f(view(osq[:, 0:GH * R], GH, R), mixT[:, 0:GH, cols], ACT.Square).then_inc(cn_sq, 1)

            decays(0)
            act.wait_ge(bexp_ready, 1)
            for ci, (R, cols, squares, merges) in enumerate(CHUNKS):
                for x, (h0, h1) in enumerate(HALVES):
                    act.wait_ge(kv_done, 2 * ci + x + 1)
                    for h in range(h0, h1):
                        y = bank(BC[x])[0:R, P * (h - h0):P * (h - h0 + 1)]
                        f(kbg[0:R, h, :], y, ACT.Copy, scale=bex[0:R, ci, h:h + 1])
                        last = f(kdec[0:R, h, :], y, ACT.Copy, scale=kde[0:R, ci, h:h + 1])
                    last.then_inc(tr_ready, 1)

                if R == TS:
                    act.wait_ge(cn_var, 1)
                    f(rinv[:, 0:4, :], rinv[:, 0:4, :], ACT.Sqrt).then_inc(cn_std, 1)

                def out(x, dst, pair, width, rows=P, scale=1.0):
                    h0, h1 = HALVES[x]
                    return f(dst[0:rows, h0:h1, 0:width], view(bank(pair[x])[0:rows, 0:width * (h1 - h0)], h1 - h0, width),
                             ACT.Copy, scale=scale)

                for k in range(squares):
                    for x in range(2):
                        n[x].pe += 1 if k == squares - 1 else 2
                        act.wait_ge(inv_pe[x], n[x].pe)
                        out(x, pw, BA_, R, R).then_inc(inv_act[x], 1)
                        n[x].pe += 1
                for x in range(2 if merges else 0):
                    n[x].pe += 1
                    act.wait_ge(inv_pe[x], n[x].pe)
                    out(x, tn, BB, R, R).then_inc(inv_act[x], 1)
                for k in range(merges):
                    for x in range(2):
                        n[x].pe += 1
                        act.wait_ge(inv_pe[x], n[x].pe)
                        out(x, zz, BA_, R, R).then_inc(inv_act[x], 1)
                        n[x].pe += 1
                for x in range(2):
                    act.wait_ge(wt_done, 2 * ci + x + 1)
                    out(x, nwt, BD, R, scale=-1.0).then_inc(nwt_ready, 1)
                if R == P:
                    for x in range(2):
                        act.wait_ge(vn_done, 2 * ci + x + 1)
                        out(x, vnw, BA_, P).then_inc(vn_ready, 1)
                    for x in range(2):
                        act.wait_ge(oc_done, 2 * ci + x + 1)
                        out(x, mixT[:, :, cols], BB, P).then_inc(oc_ready, 1)
                        if not x:
                            decays(ci + 1)
                    output_squares(ci)
                    continue
                for h in range(GH):
                    act.wait_ge(vns_done, h + 1)
                    if h >= 2:
                        act.wait_ge(snew_mm, h - 1)
                    f(vo[:, h % 2, :], bank(3 + h % 2)[0:2 * TS, 0:P], ACT.Copy).then_inc(vns_ready, 1)
                    for s in range(NS):
                        x = sg[h][:, s // 4, s % 4, :]
                        last = f(x, x, ACT.Copy, scale=egr[:, h, DT * (s + 1) - 1:DT * (s + 1)])
                    last.then_inc(sdec_ready, 1)
                act.wait_ge(oc_done, 9)
                f(mixT[:, 0:GH, cols], view(bank(5)[:, 0:GH * TS], GH, TS), ACT.Copy).then_inc(oc_ready, 1)
            output_squares(4)
            act.wait_ge(cn_var, 2)
            f(rinv[0:TS, 4, :], rinv[0:TS, 4, :], ACT.Sqrt).then_inc(cn_std, 1)

        def conv_count(c):
            return c + 1 if c < 12 else c + 2

        def conv_tile(dve, own, c):
            w, x, acc = C["conv_w"], gproj[:, GQ + c, 0:TP], cacc[:, c % 2, :]
            dve.wait_ge(act_out, evac_base["gdn_in"] + GQ + c + 1)
            if c >= 2:
                dve.wait_ge(conv_done, conv_count(c - 2))
            dve.tensor_copy(cout_p[:, c, :], gproj[:, GQ + c, TP - 3:TP])
            own(dve.tensor_scalar(acc, x, w[:, c, 3:4], None, ALU.mult))
            for i in range(1, 4):
                last = dve.scalar_tensor_tensor(out=acc[:, i:TP], in0=x[:, 0:TP - i], scalar=w[:, c, 3 - i:4 - i],
                                                in1=acc[:, i:TP], op0=ALU.mult, op1=ALU.add)
                if i < 3:
                    own(last)
            last.then_inc(conv_acc, 1)

        def conv_samples(dve, own, part):
            tt = dve.tensor_tensor
            c0, c1 = ((0, 12), (12, 18))[part]
            sacc, stmp = sconv[part]
            if not part:
                dve.wait_ge(in_conv, 16)
            new = gproj[:, GQ + c0:GQ + c1, TP:TT_].rearrange("p c (s t) -> p c s t", s=NS)
            last = dve.tensor_copy(cout_s[:, c0:c1], new[:, :, :, 1:DT])
            if part:
                last.then_inc(couts_ready, 1)
            wi = lambda i, n: bcast(C["conv_w"][:, c0:c1, i], P, c1 - c0, NS, n)
            tt(sacc, new, wi(3, DT), ALU.mult)
            for d in range(1, 4):
                tt(stmp[:, :, :, d:DT], new[:, :, :, 0:DT - d], wi(3 - d, DT - d), ALU.mult)
                own(tt(stmp[:, :, :, 0:d], cbuf[:, c0:c1, :, 3 - d:3], wi(3 - d, d), ALU.mult))
                last = tt(sacc, sacc, stmp, ALU.add)
                if d < 3:
                    own(last)
            last.then_inc(conv_acc, 1)

        def dve_gdn(dve, own):
            tt, ts, stt = dve.tensor_tensor, dve.tensor_scalar, dve.scalar_tensor_tensor
            n = [Inverse(), Inverse()]
            dve.wait_ge(act_out, evac_base["gdn_in"] + GDN_T)
            dve.wait_ge(conv_stored, 32)
            dve.wait_ge(mix_mem, 10)

            def decay_rows(ci):
                R, U = CHUNKS[ci][0], GC["cum" if ci < 4 else "cum_s"]
                tt(ug[0:R, :, 0:R], U[0:R, 0:R].unsqueeze(1).to_broadcast([R, GH, R]),
                   bcast(gat[0:R, ci, :], R, GH, R), ALU.mult).then_inc(ug_ready, 1)

            decay_rows(0)
            dve.memset(st_p, 0.0)
            dve.memset(wq, 0.0)

            def exponents(ci):
                R, MASK = CHUNKS[ci][0], GC["mask" if ci < 4 else "mask_s"]
                dve.wait_ge(gc_done, ci + 1)
                for x, (h0, h1) in enumerate(HALVES):
                    for h in range(h0, h1):
                        last = stt(out=dec[0:R, h, 0:R], in0=bank(BD[x])[0:R, R * (h - h0):R * (h - h0 + 1)],
                                   scalar=gcn[0:R, ci, h:h + 1], in1=MASK[0:R, 0:R], op0=ALU.subtract,
                                   op1=ALU.subtract)
                last.then_inc(gc_ready, 1)

            exponents(0)
            for ci, (R, cols, squares, merges) in enumerate(CHUNKS):
                heads = lambda t, k=3: t[0:R, 0:R].unsqueeze(1).to_broadcast([R, k, R])
                half = lambda t, x: t[0:R, HALVES[x][0]:HALVES[x][1], 0:R]
                from_bank = lambda pair, x, width=R: view(bank(pair[x])[0:R, 0:3 * width], 3, width)
                dve.wait_ge(dexp_ready, ci + 1)
                dve.wait_ge(kq_done, 2 * ci + 2)
                for x, (h0, h1) in enumerate(HALVES):
                    for h in range(h0, h1):
                        stt(out=bm[0:R, h, 0:R], in0=bank(BA_[x])[0:R, R * (h - h0):R * (h - h0 + 1)],
                            scalar=br2[0:R, ci, h:h + 1], in1=dec[0:R, h, 0:R], op0=ALU.mult, op1=ALU.mult)
                    if x and ci:
                        last = stt(out=rinv[:, ci - 1, :], in0=bank(BB[1])[:, 3 * P:3 * P + GH], scalar=1.0 / P,
                                   in1=qn[:, ci - 1, :], op0=ALU.mult, op1=ALU.add)
                        if ci == 4:
                            last.then_inc(cn_var, 1)
                    tt(half(qd, x), from_bank(BB, x), half(dec, x), ALU.mult).then_inc(bm_ready, 1)
                for x in range(2):
                    dve.wait_ge(bm_ready, 2 * ci + x + 1)
                    tt(half(pw, x), half(bm, x), heads(GC["diag"]), ALU.mult)
                for x in range(2):
                    dve.wait_ge(tr_done, 2 * ci + x + 1)
                    own(tt(half(pwt, x), from_bank(BA_, x), heads(GC["diag_t"]), ALU.mult))
                    tt(half(tt_, x), half(pwt, x), heads(ident), ALU.add).then_inc(inv_dve[x], 1)
                    n[x].dve += 1
                    dve.tensor_copy(half(qt_, x), from_bank(BB, x)).then_inc(qt_ready, 1)

                def beta_values(x):
                    dve.wait_ge(kv_done, 2 * ci + x + 1)
                    h0, h1 = HALVES[x]
                    for h in range(h0, h1):
                        last = ts(vb[0:R, h, :], bank(BD[x])[0:R, P * (h - h0):P * (h - h0 + 1)], br[0:R, ci, h:h + 1],
                                  None, ALU.mult)
                    last.then_inc(vb_ready, 1)

                def decayed_queries():
                    return tt(qg[:, :, 0:R], gproj[:, GQ:GQ + GH, cols], egr[:, :, 0:R], ALU.mult)

                def add(t, pair, x):
                    return tt(half(t, x), half(t, x), from_bank(pair, x), ALU.add)

                for k in range(squares):
                    if k < squares - 1:
                        for x in range(2):
                            n[x].pe += 2
                            dve.wait_ge(inv_pe[x], n[x].pe)
                            dve.tensor_copy(half(pwt, x), from_bank(BB, x))
                    for x in range(2):
                        n[x].pe += 1 if k < squares - 1 else 2
                        dve.wait_ge(inv_pe[x], n[x].pe)
                        dve.wait_ge(inv_dve[x], n[x].dve)
                        if k == squares - 1 and merges:
                            tt(half(pw, x), half(bm, x), heads(GC["off"][:, 0, :], 3), ALU.mult)
                        add(tt_, BC, x).then_inc(inv_dve[x], 1)
                        n[x].dve += 1
                    if k < squares - 1:
                        beta_values(k)
                if not merges:
                    beta_values(0)
                    beta_values(1)
                    own(decayed_queries())
                else:
                    decayed_queries()
                for k in range(merges):
                    if k == 1:
                        decay_rows(ci + 1)
                    for x in range(2):
                        n[x].pe += 2 if k else 3
                        dve.wait_ge(inv_pe[x], n[x].pe)
                        dve.wait_ge(inv_dve[x], n[x].dve)
                        if k < merges - 1:
                            tt(half(pw, x), half(bm, x), heads(GC["off"][:, k + 1, :], 3), ALU.mult)
                        add(tt_, BC, x).then_inc(inv_dve[x], 1)
                        n[x].dve += 1
                        if k < merges - 1:
                            add(tn, BB, x).then_inc(inv_dve[x], 1)
                            n[x].dve += 1
                if R == P:
                    exponents(ci + 1)
                    for x, (h0, h1) in enumerate(HALVES):
                        dve.wait_ge(sup_mm, 2 * ci + x + 1)
                        for h in range(h0, h1):
                            last = stt(out=st_p[:, h, :], in0=st_p[:, h, :], scalar=egt[:, ci, h:h + 1],
                                       in1=bank(BC[x])[:, P * (h - h0):P * (h - h0 + 1)], op0=ALU.mult, op1=ALU.add)
                        last.then_inc(sup_done, 1)
                    continue
                dve.wait_ge(cn_std, 1)
                dve.reciprocal(rinv[:, 0:4, :], rinv[:, 0:4, :]).then_inc(cn_rec, 1)
                dve.tensor_copy(qt_[TS:2 * TS, :, 0:TS], ident[TS:2 * TS, TS:2 * TS].unsqueeze(1)
                                .to_broadcast([TS, GH, TS]))
                dve.wait_ge(nwt_ready, 2 * ci + 2)

                def state_rows(h):
                    if h >= 2:
                        dve.wait_ge(vns_done, h - 1)
                    frames = wq[:, h % 2, :].rearrange("p (s c) -> p s c", s=NS)
                    for at, t in ((0, nwt), (TS, qg)):
                        last = dve.tensor_copy(frames[:, :, at:at + DT], t[:, h, 0:TS].rearrange("p (s t) -> p s t", s=NS))
                    last.then_inc(wq_ready, 1)

                state_rows(0)
                state_rows(1)
                for h in range(GH):
                    dve.wait_ge(vns_ready, h + 1)
                    tt(vx, vo[0:TS, h % 2, :].unsqueeze(1).to_broadcast([R, NS, P]), bcast(GC["seq"][0:R, :], R, NS, P),
                       ALU.mult).then_inc(vx_ready, 1)
                    if h + 2 < GH:
                        state_rows(h + 2)
                    x = mixT[:, h, 0:TP]
                    own(stt(out=x, in0=x, scalar=C["g_o"], in1=gproj[:, GZ + h, 0:TP], op0=ALU.mult, op1=ALU.mult))
                    dve.wait_ge(cn_bc, h + 1)
                    tt(x, x, bank(h % 2), ALU.mult).then_inc(cn_ready, 1)
                    if h == GH - 1:
                        x = mixT[:, 0:GH, TP:TT_]
                        dve.wait_ge(cn_ss, 2 * GH + 1)
                        stt(out=rinv[0:TS, 4, :], in0=bank(2)[0:TS, 0:GH], scalar=1.0 / P, in1=qn[0:TS, 4, :],
                            op0=ALU.mult, op1=ALU.add).then_inc(cn_var, 1)
                        stt(out=x, in0=x, scalar=C["g_o"], in1=gproj[:, GZ:GZ + GH, TP:TT_], op0=ALU.mult, op1=ALU.mult)
                    dve.wait_ge(sdec_ready, h + 1)
                    dve.wait_ge(snew_mm, h + 1)
                    tt(sg[h], sg[h], view(banks(6, 2), 2, 4, P), ALU.add).then_inc(snew_ready, 1)
            dve.wait_ge(cn_std, 2)
            dve.reciprocal(rinv[0:TS, 4, :], rinv[0:TS, 4, :]).then_inc(cn_rec, 1)
            dve.wait_ge(cn_bc, GH + 1)
            tt(x, x, view(bank(2)[:, TS:TS * (GH + 1)], GH, TS), ALU.mult).then_inc(cn_ready, 1)

        @block.tensor
        def _(pe):
            mm = pe.matmul

            def square_sums(n, k, at=None):
                at = k if at is None else at
                pe.wait_ge(sq_ready, at + n * KT + 1)
                for half in range(2):
                    last = mm(both(3)[:, half, :], ones, halves_of(sq[:, k % 2, :])[:, half, :],
                              start=k == 0, stop=k == KT - 1)
                last.then_inc(sq_used, 1)

            def gemm(name, ktiles, rhs, inputs=None, norm=None, after=None):
                wb, tiles, eb = wbase[name], TILES[name], evac_base[name]
                evac = act_out if name in ("nsa_in", "up0", "gdn_in", "up1") else dve_out
                per = 8 if ktiles == KT else 2

                def tile(i, j, t):
                    if not isinstance(t, int) or t >= 2:
                        pe.wait_ge(evac, eb + t - 1)
                    elif name[:4] == "down":
                        pe.wait_ge(act_out, evac_base[f"up{name[4]}"] + 31 + t)
                    for k in range(ktiles):
                        hp = j // 2 if ktiles == KT else 2 * j + k // 16
                        slot = (wb + hp) % 4
                        if (ktiles == KT and j % 2 == 0 and k == 0) or (ktiles != KT and k % 16 == 0):
                            pe.wait_ge(in_panel[slot], 16 * (panel_uses(slot, wb + hp) + i))
                        if ktiles == KT:
                            lhs = view(ring[slot], KT, 256)[:, k, P * (j % 2):P * (j % 2 + 1)]
                        else:
                            lhs = view(ring[slot], 16, P)[:, k % 16, :]
                        if inputs and j == 0:
                            pe.wait_ge(inputs[0], inputs[1] + k + 1)
                        for half in range(2):
                            last = mm(both(j % 2)[:, half, :], lhs, halves_of(rhs(k))[:, half, :],
                                      start=k == 0, stop=k == ktiles - 1)
                    last.then_inc(pe_out, 1)

                first = 1 if norm else 0
                trips = tiles // per if tiles >= 2 * per and not after else 0
                for t in range(per * first if trips else 0):
                    tile(0, t, t)
                    if t:
                        square_sums(norm, t - 1)
                if trips:
                    with pe.Fori(first, trips) as i:
                        for j in range(per):
                            tile(i, j, i * per + j)
                            if norm:
                                square_sums(norm, (j - 1) % 2 + 2, i * per + j - 1)
                for t in range(trips * per, tiles):
                    tile(t // per, t % per, t)
                    if after:
                        after(t)
                    if norm and t:
                        square_sums(norm, t - 1)
                if norm:
                    square_sums(norm, KT - 1)

            def memory_sums():
                pe.wait_ge(in_common, 16)
                pe.wait_ge(mem_sq, KT)
                for k in range(KT):
                    last = mm(bank(0)[:, 0:MEM], ones, sqm[:, k, :], start=k == 0, stop=k == KT - 1)
                last.then_inc(mem_ss, 1)

            def memory_kv():
                for l in range(2):
                    pe.wait_ge(memn_ready, KT * (l + 1))
                    pe.wait_ge(in_panel[2 * l], 16)
                    wk, wv = view(ring[2 * l], KT, MEM), view(ring[2 * l + 1], KT, MEM)
                    for hp in range(2):
                        for k in range(KT):
                            last = mm(bank(1 + 2 * l)[:, MEM * hp:MEM * (hp + 1)], wk[:, k, P * hp:P * (hp + 1)],
                                      memn[:, l, k, :], start=k == 0, stop=k == KT - 1)
                    last.then_inc(pe_out, 1)
                    pe.wait_ge(in_panel[2 * l + 1], 16)
                    for m in range(2):
                        for k in range(KT):
                            last = mm(bank(2 + 2 * l)[:, MEM * m:MEM * (m + 1)], memn[:, l, k, P * m:P * (m + 1)],
                                      wv[:, k, :], start=k == 0, stop=k == KT - 1)
                    last.then_inc(pe_out, 1)

            def memory_attention(l):
                pr, xq = (proj, gproj)[l], (XQ0, XQ1)[l]
                kmem, vmem = view(mkv[l][:, 0:512], 2, MEM), view(mkv[l][:, 512:1024], 2, MEM)
                b = mb[l]

                def scores(qt):
                    if qt == 0:
                        pe.wait_ge(act_out, evac_base[("nsa_in", "gdn_in")[l]] + xq + 2)
                        if l:
                            pe.wait_ge(in_mkv1, 16)
                        else:
                            pe.wait_ge(memkv_ready, 4)
                    else:
                        pe.wait_ge(xpt_ready, 5 * l + qt)
                    for hh in range(2):
                        for hp in range(2):
                            last = mm(bank(4 + hh)[:, MEM * hp:MEM * (hp + 1)],
                                      pr[64 * hh:64 * hh + 64, xq + hp, P * qt:P * (qt + 1)],
                                      kmem[64 * hh:64 * hh + 64, hp, :], start=True, stop=True)
                    last.then_inc(xm_ready, 1)

                def sample_scores():
                    pe.wait_ge(in_mcache, 16 * (l + 1))
                    pe.wait_ge(qm_ready, l + 1)
                    pe.wait_ge(xpt_ready, 5 * l + 4)
                    for s in range(NS):
                        for hp in range(2):
                            last = mm(bank(4)[:, 0:MEM], b["qm"][:, MEM * s + P * hp:MEM * s + P * (hp + 1)],
                                      mcache[l][:, s, MEM * hp:MEM * (hp + 1)],
                                      start=s == hp == 0, stop=s == NS - 1 and hp == 1)
                    last.then_inc(xm_ready, 1)

                def transposes(n):
                    pe.wait_ge(xp_ready, 5 * l + n + 1)
                    sm = b["sm"][n % 2]
                    for m in range(2):
                        for r in range(4 if n < 4 else 1):
                            last = pe.transpose(bank(4 + m)[:, P * r:P * (r + 1)], sm[:, r, P * m:P * (m + 1)], ident)
                    last.then_inc(xt_done, 1)

                def values(n):
                    pe.wait_ge(xpt_ready, 5 * l + n + 1)
                    if n:
                        pe.wait_ge(mix_mem, 5 * l + n)
                    pt = b["pt"][n % 2]
                    if n < 4:
                        for hh in range(2):
                            for hp in range(2):
                                for m in range(2):
                                    last = mm(bank(6)[64 * hh:64 * hh + 64, P * hp:P * (hp + 1)],
                                              vmem[:, m, P * hp + 64 * hh:P * hp + 64 * hh + 64],
                                              pt[:, m, 2 * hh + hp, :], start=m == 0, stop=m == 1)
                    else:
                        for s in range(NS):
                            for hp in range(2):
                                for m in range(2):
                                    last = mm(bank(6)[:, 64 * hp + 8 * s:64 * hp + 8 * s + 8],
                                              mcache[l][:, s, 512 + MEM * m + P * hp:512 + MEM * m + P * (hp + 1)],
                                              pt[:, m, 0, 16 * s + 8 * hp:16 * s + 8 * hp + 8],
                                              start=m == 0, stop=m == 1)
                    last.then_inc(xo_done, 1)

                def after(t):
                    n, odd = divmod(t - MEM_FIRST[l], 2)
                    if odd and 0 <= n < 5:
                        transposes(n)
                    elif not odd and 0 <= n <= 5:
                        if n < 4:
                            scores(n)
                        elif n == 4:
                            sample_scores()
                        if n:
                            values(n - 1)
                return after

            def gdn_steps():
                memory = memory_attention(1)

                def after(t):
                    memory(t)
                    if t == GATES:
                        gate_inputs(pe)
                    if t == GATES + 4:
                        gate_sums(pe)
                    if LENGTHS < t <= LENGTHS + GH:
                        for c in range(2):
                            lengths(pe, 2 * (t - LENGTHS - 1) + c)
                return after

            memory_sums()
            for k in range(KT):
                square_sums(0, k)
            memory_kv()
            pe.wait_ge(memkv_ready, 3)
            gemm("nsa_in", KT, lambda k: hT[:, k, :], inputs=(h_ready, 0), after=memory_attention(0))
            pe_nsa_prompt(pe)
            pe_nsa_sample(pe)
            pe.wait_ge(seq_done, NS)
            gemm("out0", KT, lambda k: mixT[:, k, :] if k < 6 else proj[:, XQ0 + k - 6, :], norm=1)
            gemm("up0", KT, lambda k: hT[:, k, :], inputs=(h_ready, KT))
            gemm("down0", FFT, lambda k: u[:, k, :], inputs=(u_ready, 0), norm=2)
            gemm("gdn_in", KT, lambda k: hT[:, k, :], inputs=(h_ready, 2 * KT), after=gdn_steps())
            pe_gdn(pe)
            gemm("out1", KT, lambda k: mixT[:, k, :] if k < 6 else gproj[:, XQ1 + k - 6, :], norm=3)
            gemm("up1", KT, lambda k: hT[:, k, :], inputs=(h_ready, 3 * KT))
            gemm("down1", FFT, lambda k: u[:, k, :], inputs=(u_ready, FFT), norm=4)

        @block.scalar
        def _(act):
            own = Chain(act, chain_act)
            f = act.activation

            def norm(n):
                if n == 0:
                    act.wait_ge(in_x, 16)
                for k in range(KT):
                    if n:
                        act.wait_ge(dve_out, 8 * (n - 1) + k + 1)
                    if n or k >= 2:
                        act.wait_ge(sq_used, n * KT + k - 1)
                    f(sq[:, k % 2, :], xT[:, k, :], ACT.Square).then_inc(sq_ready, 1)
                act.wait_ge(sq_used, (n + 1) * KT)
                if n:
                    act.wait_ge(h_ready, n * KT)
                f(halves_of(rstd), both(3), ACT.Sqrt, bias=C["eps"], scale=1.0 / D).then_inc(std_ready, 1)

            def convolved(t):
                c = t - GQ - CONV
                if c == 12:
                    act.wait_ge(conv_acc, 13)
                    f(gproj[:, GQ:GQ + 12, TP:TT_], sconv[0][0].rearrange("p c s t -> p c (s t)"), ACT.Silu)\
                        .then_inc(conv_done, 1)
                if 0 <= c < 18:
                    act.wait_ge(conv_acc, conv_count(c))
                    f(gproj[:, GQ + c, 0:TP], cacc[:, c % 2, :], ACT.Silu).then_inc(conv_done, 1)
                if c == 18:
                    act.wait_ge(conv_acc, 20)
                    f(gproj[:, GV:GV + 6, TP:TT_], sconv[1][0].rearrange("p c s t -> p c (s t)"), ACT.Silu)\
                        .then_inc(conv_done, 1)

            def copy_out(name, dst, after):
                for t in range(TILES[name]):
                    act.wait_ge(pe_out, obase[name] + t + 1)
                    gate = name == "gdn_in" and t >= GZ
                    f(halves_of(dst[:, t, :]), both(t % 2), ACT.Silu if gate else ACT.Copy).then_inc(act_out, 1)
                    after(t)

            def up_out(l):
                with act.Fori(0, 16) as i:
                    for j in range(2):
                        dst = u[:, bass.ds(2 * i + j, 1), :].rearrange("p a n -> p (a n)")
                        act.wait_ge(pe_out, obase[f"up{l}"] + 1 + j + 2 * i)
                        act.nop(nofuse=True)
                        f(halves_of(dst), both(j), ACT.Relu).then_inc(act_out, 1)
                        act.wait_ge(act_out, evac_base[f"up{l}"] + 1 + j + 2 * i)
                        act.nop(nofuse=True)
                        f(dst, dst, ACT.Square).then_inc(u_ready, 1)

            def memory_norm():
                act.wait_ge(in_mem, 16)
                for k in range(KT):
                    f(sqm[:, k, :], memT[:, k, :], ACT.Square).then_inc(mem_sq, 1)
                act.wait_ge(mem_ss, 1)
                f(rstdm, bank(0)[:, 0:MEM], ACT.Sqrt, bias=C["eps"], scale=1.0 / D).then_inc(mem_std, 1)

            def memory_kv():
                for l in range(2):
                    for half in range(2):
                        act.wait_ge(pe_out, 2 * l + half + 1)
                        f((mkv0, mkv1_tmp)[l][:, 512 * half:512 * (half + 1)], bank(1 + 2 * l + half), ACT.Copy)\
                            .then_inc(memkv_ready, 1)

            def memory_attention(l):
                b = mb[l]

                def exps(n):
                    heads = 4 if n < 4 else 1
                    act.wait_ge(xmax_ready, 5 * l + n + 1)
                    if n >= 2:
                        act.wait_ge(xt_done, 5 * l + n - 1)
                    for r in range(heads):
                        last = f(b["sm"][n % 2][:, r, :], bank(4 + r // 2)[:, MEM * (r % 2):MEM * (r % 2 + 1)], ACT.Exp, scale=HD ** -0.5,
                                 bias=b["stat"][:, n % 2, r:r + 1], accum_out=b["stat"][:, n % 2, 4 + r:5 + r])
                    last.then_inc(xs_ready, 1)

                def turned(n):
                    heads = 4 if n < 4 else 1
                    act.wait_ge(xt_done, 5 * l + n + 1)
                    if n >= 2:
                        act.wait_ge(xo_done, 5 * l + n - 1)
                    for m in range(2):
                        last = f(b["pt"][n % 2][:, m, 0:heads, :].rearrange("p r q -> p (r q)"),
                                 bank(4 + m)[:, 0:P * heads], ACT.Copy)
                    last.then_inc(xpt_ready, 1)

                def after(t):
                    n, odd = divmod(t - MEM_FIRST[l], 2)
                    if 0 <= n < 5:
                        (turned if odd else exps)(n)
                return after

            def gdn_steps():
                memory = memory_attention(1)

                def after(t):
                    convolved(t)
                    memory(t)
                    if t == GATES + 1:
                        gates_act(act, own)
                    if t == GATES + 5:
                        decays_act(act)
                    if LENGTHS <= t < LENGTHS + GH:
                        c = 2 * (t - LENGTHS)
                        act.wait_ge(conv_done, 13)
                        column_squares(act, 0, range(c, c + 2), lambda c: gproj[:, GQ + c, :])
                return after

            def compressions():
                act.wait_ge(w1_used, 1)
                f(pab.rearrange("p k h c -> p (k h c)"), bank(7)[:, 0:4 * CX], ACT.Copy).then_inc(pab_ready, 1)

            memory_norm()
            norm(0)
            memory_kv()
            copy_out("nsa_in", proj, memory_attention(0))
            compressions()
            act_nsa_prompt(act, own)
            act_nsa_sample(act, own)
            norm(1)
            up_out(0)
            norm(2)
            copy_out("gdn_in", gproj, gdn_steps())
            act.wait_ge(ks_read, 1)
            f(kr, kr2, ACT.Sqrt).then_inc(kr_ready, 1)
            act_gdn(act, own)
            norm(3)
            act.wait_ge(stored, 32)
            act.wait_ge(state_stored, 16 * GH)
            up_out(1)
            norm(4)

        @block.vector
        def _(dve):
            own = Chain(dve, chain_dve)
            tt, ts, stt = dve.tensor_tensor, dve.tensor_scalar, dve.scalar_tensor_tensor

            def norm(n, gain):
                dve.wait_ge(std_ready, n + 1)
                own(dve.reciprocal(rstd, rstd))
                for k in range(KT):
                    stt(out=hT[:, k, :], in0=xT[:, k, :], scalar=gain[:, k:k + 1], in1=rstd, op0=ALU.mult,
                        op1=ALU.mult).then_inc(h_ready, 1)

            def residual(name):
                for t in range(8):
                    dve.wait_ge(pe_out, obase[name] + t + 1)
                    x = halves_of(xT[:, t, :])
                    tt(x, x, both(t % 2), ALU.add).then_inc(dve_out, 1)

            def memory_kv():
                dve.wait_ge(mem_std, 1)
                own(dve.reciprocal(rstdm, rstdm))
                for l in range(2):
                    for k in range(KT):
                        stt(out=memn[:, l, k, :], in0=memT[:, k, :], scalar=C["g_mem"][:, l, k:k + 1], in1=rstdm,
                            op0=ALU.mult, op1=ALU.mult).then_inc(memn_ready, 1)

            def memory_attention(l):
                b = mb[l]
                pr, xq = (proj, gproj)[l], (XQ0, XQ1)[l]
                own(dve.memset(b["qm"], 0.0))
                dve.wait_ge(act_out, evac_base[("nsa_in", "gdn_in")[l]] + xq + 2)
                for hp in range(2):
                    for hh in range(2):
                        r = slice(64 * hh, 64 * hh + 64)
                        dst = b["qm"][r, :].rearrange("p (s c) -> p s c", s=NS)
                        at = P * hp + 8 * hp + 4 * hh
                        last = dve.tensor_copy(dst[:, :, at:at + DT],
                                               pr[r, xq + hp, TP:TT_].rearrange("p (s t) -> p s t", s=NS))
                last.then_inc(qm_ready, 1)
                unit = lambda n: ((4 if n < 4 else 1), b["stat"][:, n % 2, :])

                def maxima(n):
                    heads, st = unit(n)
                    dve.wait_ge(xm_ready, 5 * l + n + 1)
                    own(dve.tensor_reduce(st[:, 0:heads], banks(4, 2).rearrange("p (r c) -> p r c", r=4)
                                          if n < 4 else bank(4)[:, 0:MEM], AX.X, ALU.max))
                    ts(st[:, 0:heads], st[:, 0:heads], -HD ** -0.5, None, ALU.mult).then_inc(xmax_ready, 1)

                def scaled(n):
                    heads, st = unit(n)
                    dve.wait_ge(xs_ready, 5 * l + n + 1)
                    own(dve.reciprocal(st[:, 8:8 + heads], st[:, 4:4 + heads]))
                    sm = b["sm"][n % 2][:, 0:heads, :]
                    tt(sm, sm, bcast(st[:, 8:8 + heads], P, heads, MEM), ALU.mult).then_inc(xp_ready, 1)

                def output(n):
                    dve.wait_ge(xo_done, 5 * l + n + 1)
                    if n < 4:
                        dve.tensor_copy(pr[:, xq:xq + 2, P * n:P * (n + 1)], view(bank(6)[:, 0:2 * P], 2, P))\
                           .then_inc(mix_mem, 1)
                    else:
                        for hh in range(2):
                            r = slice(64 * hh, 64 * hh + 64)
                            o = bank(6)[r, 0:P].rearrange("p (h s c) -> p h s c", h=2, s=NS)
                            last = dve.tensor_copy(
                                pr[r, xq:xq + 2, TP:TT_].rearrange("p h (s t) -> p h s t", s=NS),
                                o[:, :, :, 4 * hh:4 * hh + DT])
                        last.then_inc(mix_mem, 1)

                def after(t):
                    n, odd = divmod(t - MEM_FIRST[l], 2)
                    if not odd and 0 <= n <= 5:
                        if n < 5:
                            maxima(n)
                        if n:
                            output(n - 1)
                        if n < 5:
                            scaled(n)
                return after

            def gdn_steps():
                for t in (ban, gcn, egt, kr2):
                    dve.memset(t, 0.0)
                memory = memory_attention(1)
                for t in range(GDN_T):
                    memory(t)
                    if t == GATES:
                        gates_dve(dve, own)
                    if t == GATES + 2:
                        gates_done_dve(dve, own)
                    if t == GATES + 4:
                        gate_sums_dve(dve, own)
                    c = t - GQ
                    if 0 <= c < 18:
                        conv_tile(dve, own, c)
                    if c == 11:
                        conv_samples(dve, own, 0)
                    if c == 17:
                        conv_samples(dve, own, 1)
                lengths_dve(dve, own)
                factors_dve(dve, own)

            memory_kv()
            norm(0, C["g_mix"][:, 0, :])
            memory = memory_attention(0)
            for t in range(NSA_T):
                if t == CV + 2:
                    chunks_of_prompt(dve)
                memory(t)
            block_sums_of_prompt(dve, own)
            dve.memset(kcp, 0.0).then_inc(kcp_zeroed, 1)
            dve.wait_ge(first_read, 2)
            add_halves(dve, cab0)
            dve_nsa_prompt(dve, own)
            dve_nsa_sample(dve, own)
            residual("out0")
            norm(1, C["g_ffn"][:, 0, :])
            residual("down0")
            norm(2, C["g_mix"][:, 1, :])
            gdn_steps()
            dve_gdn(dve, own)
            residual("out1")
            norm(3, C["g_ffn"][:, 1, :])
            residual("down1")
            norm(4, C["g_fin"])


def constants():
    f = np.float32
    ar = np.arange
    c = {}
    slopes = np.exp2(f(-8.0) * ar(1, 13, dtype=f) / f(12)).astype(f)
    c["ident"], c["ones"] = np.eye(P, dtype=f), np.ones((P, P), f)
    c["eps"], c["one"] = np.full((P, 1), EPS, f), np.ones((P, 1), f)
    d = ar(P)[:, None] + TP - P - ar(TP)[None]
    c["dist"] = np.where(d >= 0, d, -NEG).astype(f)
    pos = ar(P)[:, None, None] + P * ar(4)[None, :, None]
    d = pos - (16 * ar(NCP) + 31)[None, None]
    c["cdist"] = np.where(d >= 0, d, -NEG).astype(f)
    c["cvis"] = (pos[:, :, 0] >= 31).astype(f)
    c["nslope"] = np.tile(-slopes, (P, 1))
    row = ar(ROWS)
    kv, g, t = row // 32, row % 32 // 4, row % 4
    real = g < NG
    sl = np.where(real, slopes[np.minimum(6 * kv + g, 11)], 0).astype(f)[:, None]

    def rows(a):
        return np.concatenate([a.astype(f), np.zeros((P - a.shape[0],) + a.shape[1:], f)])

    pos = (PAST + t)[:, None]
    c["b_slc"] = np.concatenate([-sl * (pos - h * PAST2 - ar(PAST2)[None]).astype(f) for h in range(2)])
    wp = PAST - WIN + ar(WIN)[None]
    c["b_win"] = rows(np.where(pos - wp < WIN, -sl * (pos - wp).astype(f), f(NEG)))
    c["b_cmp"] = rows(-sl * (pos - (16 * ar(NCB) + 31)[None]).astype(f))
    d = t[:, None] - ar(DT)[None]
    c["b_new"] = np.concatenate([np.where(d >= 0, -sl * d.astype(f), f(NEG)), np.full((ROWS, DT), NEG, f)])
    c["same"] = np.tile(rows((kv[:, None] == kv) & (t[:, None] == t) & real[:, None]), (1, 2))
    tok = ar(TS)[:, None, None]
    c["pick"] = rows(tok == DT * ar(NS)[None, :, None] + t[None, None])
    col = ar(36)
    c["head"] = rows(real[:, None] & (col[None] // 6 == g[:, None]) & (col[None] % 2 == kv[:, None]))
    own = ar(NSLC // 2)[None] + NSLC // 2 * (ar(P)[:, None] // ROWS)
    c["lower"] = (ar(1, NSLC - 1)[None, None] < own[:, :, None]).astype(f)
    c["drop"] = np.where((own == 0) | (own == NSLC - 1), 0, NEG).astype(f)
    i, j = ar(P)[:, None], ar(P)[None]
    c["cum"] = (i <= j).astype(f)
    si, sj = ar(TS)[:, None], ar(TS)[None]
    same = si // DT == sj // DT
    c["cum_s"], c["all_s"] = rows(same & (si <= sj)), rows(same)
    c["mask"] = np.where(j <= i, 0, NEG).astype(f)
    c["mask_s"] = rows(np.where(same & (sj <= si), 0, NEG))
    c["diag"] = -((i // 16 == j // 16) & (j < i)).astype(f)
    c["diag_t"] = c["diag"].T
    c["off"] = -np.stack([(i // (2 * m) == j // (2 * m)) & (i // m > j // m) for m in (16, 32, 64)], 1).astype(f)
    c["seq"] = rows(si // DT == ar(NS)[None])
    return c


def pack(tb, parts):
    out = [np.ascontiguousarray(np.asarray(parts[k], np.float32).reshape(P, -1)) for k in tb.at]
    assert [a.shape[1] for a in out] == [int(np.prod(s)) for _, s in tb.at.values()], [a.shape for a in out]
    return np.concatenate(out, 1)


def kernel(**inputs):
    import concourse.bacc as bacc
    from concourse.bass_utils import run_bass_kernel_spmd

    a = {k: np.asarray(v) for k, v in inputs.items()}
    c = constants()
    chan = lambda v: v.reshape(v.shape[:-1] + (KT, P)).transpose(v.ndim, *range(v.ndim))
    cols = lambda x: x.T.reshape(KT, P, -1).transpose(1, 0, 2)

    for name, key in (("g_mix", "norm_mix_g"), ("g_mem", "norm_mem_g"), ("g_ffn", "norm_ffn_g")):
        c[name] = chan(a[key])
    c["g_fin"] = chan(a["final_norm_g"])
    lpair = lambda w: w.reshape(16, 2 * HD, -1).transpose(1, 0, 2)
    c["pe"] = np.stack([lpair(a[k][0].reshape(32, HD, 1))[:, :, 0] for k in ("cmp_pe_k", "cmp_pe_v")], 1)
    c["w2"] = np.stack([a["cmp_w2_k"][0], a["cmp_w2_v"][0]], 1)
    c["conv_w"] = a["gdn_conv_w"][0].reshape(4, 18, P).transpose(2, 1, 0)
    c["g_o"] = a["gdn_norm_g"][0][:, None]
    c["a_log"], c["dt_bias"] = (np.broadcast_to(a[k][0], (P, GH)) for k in ("gdn_a_log", "gdn_dt_bias"))

    def wide(w):
        n = -(-w.shape[1] // 256)
        w = np.concatenate([w, np.zeros((D, 256 * n - w.shape[1]), w.dtype)], 1)
        return w.reshape(KT, P, n, 256).transpose(2, 1, 0, 3).reshape(n, P, 2048)

    def tall(w):
        return w.reshape(2, 16, P, KT, P).transpose(3, 0, 2, 1, 4).reshape(16, P, 2048)

    w = a["nsa_w_in"][0]
    heads = lambda x: x.reshape(-1, NKV, NG, HD).transpose(0, 2, 1, 3).reshape(x.shape[0], -1)
    gates = w[:, 1536:1572].reshape(D, NKV, NG, 3)[..., [1, 2, 0]].transpose(0, 2, 3, 1).reshape(D, 36)
    nsa_in = np.concatenate([w[:, 1572:1828], w[:, 768:1536], heads(w[:, 0:768]), gates], 1)
    w = a["gdn_w_in"][0]
    gdn_w = np.concatenate([w[:, 3084:3340], w[:, 3072:3084], np.zeros((D, P - 2 * GH), w.dtype), w[:, 0:3072]], 1)
    wo = a["w_out"]
    out0 = np.concatenate([heads(wo[0][:768].T).T, wo[0][768:]], 0)
    w1 = np.stack([lpair(a[k][0]).reshape(P, 2048) for k in ("cmp_w1_k", "cmp_w1_v")])
    panels = np.concatenate([wide(a["w_mem_kv"][0]), wide(a["w_mem_kv"][1]), wide(nsa_in), w1, wide(out0),
                             wide(a["w_up"][0]), tall(a["w_down"][0]), wide(gdn_w), wide(wo[1]),
                             wide(a["w_up"][1]), tall(a["w_down"][1])])

    kv = a["cache_nsa_kv"][:, :, 0]
    ck = kv[:, :, 0:2].reshape(NPHYS, 8, 8, 2, 2, NKV, HD).transpose(0, 3, 6, 4, 2, 5, 1).reshape(NPHYS, P, 256)
    pages = np.concatenate([ck, kv[:, :, 2].reshape(NPHYS, PAGE, P).transpose(0, 2, 1), kv[:, :, 3].reshape(NPHYS, PAGE, P)], 2)
    wn = a["cache_nsa_win"][:, 0]
    win = np.concatenate([wn[:, :, 0].reshape(NS, WIN, P).transpose(0, 2, 1),
                          wn[:, :, 1].reshape(NS, 4, P, P).transpose(0, 2, 1, 3).reshape(NS, P, 512)], 2)
    mc = a["cache_mem_kv"].transpose(1, 0, 2, 3, 4, 5)
    mk = mc[:, :, :, 0].reshape(2, NS, MEM, 2, P).transpose(0, 1, 4, 3, 2).reshape(2, NS, P, 512)
    mv = mc[:, :, :, 1].reshape(2, NS, 2, P, MEM).transpose(0, 1, 3, 2, 4).reshape(2, NS, P, 512)

    arrays = dict(
        x=np.concatenate([cols(a["x_prompt"][0]), cols(a["x_sample"].reshape(TS, D))], 2),
        mem=cols(a["mem_prompt"][0]), w=panels, common=pack(COMMON, c), prompt=pack(PROMPT_T, c),
        sample=pack(SAMPLE_T, c), gdn=pack(GDN_TB, c), pages=pages, win=win, mcache=np.concatenate([mk, mv], 3),
        conv=a["state_gdn_conv"][:, 0].reshape(NS, 3, 18, P).transpose(3, 2, 0, 1),
        state=a["state_gdn_s"][:, 0].transpose(1, 2, 0, 3), table=a["page_table"].reshape(1, NS * NPAGE))
    outs = dict(y=(P, KT, TT_), kv=(P, 6, TT_), win_o=(NS, P, 1024), conv_p=(P, 18, 3), conv_s=(P, 18, NS, 3),
                state_p=(P, GH, P), state_s=(GH, P, NS, P), mem_o=(2, P, 1024))
    nc = bacc.Bacc("TRN2", target_bir_lowering=False, num_devices=1)
    ins, args = {}, []
    for name, v in arrays.items():
        v = np.ascontiguousarray(v)
        ins[f"in_{name}"] = v
        args.append(nc.dram_tensor(f"in_{name}", v.shape, mybir.dt.from_np(v.dtype), kind="ExternalInput").ap())
    for name, shape in outs.items():
        args.append(nc.dram_tensor(f"out_{name}", shape, F32, kind="ExternalOutput").ap())
    build(nc, *args)
    r = run_bass_kernel_spmd(nc, [ins], core_ids=[0]).results[0]
    o = {k: np.asarray(r[f"out_{k}"]) for k in outs}

    y = o["y"].transpose(2, 1, 0).reshape(TT_, D)
    kvr = o["kv"].transpose(2, 1, 0).reshape(TT_, 6, NKV, HD)
    wk = o["win_o"][:, :, 0:512].transpose(0, 2, 1)
    wv = o["win_o"][:, :, 512:].reshape(NS, P, 4, P).transpose(0, 2, 1, 3).reshape(NS, WIN, P)
    old = np.stack([wk, wv], 2).reshape(NS, WIN, 2, NKV, HD)
    new = kvr[TP:, 4:6].reshape(NS, DT, 2, NKV, HD)
    mo = o["mem_o"]
    mkp = mo[:, :, 0:512].reshape(2, P, 2, MEM).transpose(0, 3, 2, 1).reshape(2, MEM, XH, HD)
    mvp = mo[:, :, 512:].reshape(2, P, 2, MEM).transpose(0, 2, 1, 3).reshape(2, MEM, XH, HD)
    res = (y[:TP][None], y[TP:].reshape(NS, DT, D), kvr[:TP, 0:4][None, :, None], kvr[TP:, 0:4].reshape(NS, DT, 1, 4, NKV, HD),
           kvr[:TP, 4:6][None, None], np.concatenate([old[:, DT:], new], 1)[:, None],
           o["state_p"].transpose(1, 0, 2)[None, None], o["state_s"].transpose(2, 0, 1, 3)[:, None],
           o["conv_p"].transpose(2, 1, 0).reshape(1, 1, 3, 2304),
           o["conv_s"].transpose(2, 3, 1, 0).reshape(NS, 1, 3, 2304),
           np.stack([mkp, mvp], 2)[None])
    return tuple(np.ascontiguousarray(x) for x in res)
```
